# Optimizing a Trainium2 kernel written in Bass

```python
import math
import jax, jax.numpy as jnp
from jax import lax
import numpy as np

D_MODEL = 1024
BATCH = 1
SEQ = 512
DEPTH = 1

D_MIX = D_MODEL
D_ATTN = D_MIX // 2
D_LRU = D_MIX - D_ATTN
HEAD_DIM = 64
V_DIM = 2 * HEAD_DIM
N_ATTN_HEADS = D_ATTN // V_DIM
N_LRU_BLOCKS = 8
LRU_BLOCK = D_LRU // N_LRU_BLOCKS
CONV_WIDTH = 4
CONV_PAD = (CONV_WIDTH // 2, CONV_WIDTH - 1 - CONV_WIDTH // 2)
LRU_C = 8.0
MIX_IN = 3 * D_ATTN + 2 * D_LRU
D_FF = ((8 * D_MODEL // 3 + 127) // 128) * 128
ROPE_THETA = 10000.0
Q_BLOCK = 128
EPS = 1e-6
N_SUB = 3


def rms_norm(x, g):
    xf = x.astype(jnp.float32)
    y = xf * lax.rsqrt(jnp.mean(xf * xf, axis=-1, keepdims=True) + EPS)
    return (y * g.astype(jnp.float32)).astype(x.dtype)

def rope_tables(positions):
    inv = ROPE_THETA ** (-jnp.arange(0, HEAD_DIM, 2, dtype=jnp.float32) / HEAD_DIM)
    ang = positions.astype(jnp.float32)[..., None] * inv
    return jnp.cos(ang), jnp.sin(ang)

def apply_rope(t, cos, sin):
    cos = cos[:, :, None, None, :]
    sin = sin[:, :, None, None, :]
    t1, t2 = jnp.split(t.astype(jnp.float32), 2, axis=-1)
    out = jnp.concatenate([t1 * cos - t2 * sin, t2 * cos + t1 * sin], axis=-1)
    return out.astype(t.dtype)

def diff_attention(q, k, v, lam, subln_g, lambda_init, cos, sin):
    B, S = q.shape[0], q.shape[1]
    q = apply_rope(q, cos, sin) * (HEAD_DIM ** -0.5)
    k = apply_rope(k, cos, sin)
    nb = S // Q_BLOCK
    qb = q.reshape(B, nb, Q_BLOCK, N_ATTN_HEADS, 2, HEAD_DIM).transpose(1, 0, 2, 3, 4, 5)

    def block(qblk):
        s = jnp.einsum('bqhmd,bkhmd->bhmqk', qblk, k, preferred_element_type=jnp.float32)
        p = jax.nn.softmax(s, axis=-1)
        w = p[:, :, 0] - lam * p[:, :, 1]
        return jnp.einsum('bhqk,bkhe->bqhe', w.astype(v.dtype), v)

    o = lax.map(block, qb)
    o = o.transpose(1, 0, 2, 3, 4).reshape(B, S, N_ATTN_HEADS, V_DIM)
    o = rms_norm(o, subln_g) * (1.0 - lambda_init)
    return o.reshape(B, S, D_ATTN)

def _lin_combine(e1, e2):
    a1, b1 = e1
    a2, b2 = e2
    return (a1 * a2, a2 * b1 + b2)

def rg_lru(xc, w_gate, b_gate, lam, reverse):
    B, S = xc.shape[0], xc.shape[1]
    xb = xc.reshape(B, S, N_LRU_BLOCKS, LRU_BLOCK)
    g = jnp.einsum('bsni,gnij->gbsnj', xb, w_gate).reshape(2, B, S, D_LRU)
    g = jax.nn.sigmoid(g.astype(jnp.float32) + b_gate.astype(jnp.float32)[:, None, None, :])
    r, i = g[0], g[1]
    log_a = -LRU_C * r * jax.nn.softplus(-lam.astype(jnp.float32))
    a = jnp.exp(log_a)
    mult = jnp.sqrt(-jnp.expm1(2.0 * log_a))
    b = mult * i * xc.astype(jnp.float32)
    _, h = lax.associative_scan(_lin_combine, (a, b), axis=1, reverse=reverse)
    return h

def recurrent_group(xr, yr, conv_w, conv_b, w_gate, b_gate, lam):
    xc = lax.conv_general_dilated(
        xr, conv_w[:, None, :].astype(xr.dtype), window_strides=(1,), padding=[CONV_PAD],
        dimension_numbers=('NWC', 'WIO', 'NWC'), feature_group_count=D_LRU) + conv_b
    h = rg_lru(xc, w_gate[0], b_gate[0], lam[0], False) + rg_lru(xc, w_gate[1], b_gate[1], lam[1], True)
    return (h * jax.nn.gelu(yr.astype(jnp.float32))).astype(xr.dtype)

def swiglu(h, w_in, w_out):
    gu = h @ w_in
    g, u = jnp.split(gu, 2, axis=-1)
    return (jax.nn.silu(g) * u) @ w_out

def first_inputs(seed: int = 0) -> dict:
    key = jax.random.key(seed)
    ks = jax.random.split(key, 20)
    f32 = jnp.float32
    nrm = lambda k, shape, s: jax.random.normal(k, shape, f32) * s
    u = jax.random.uniform(ks[18], (DEPTH, 2, D_LRU), f32, 0.9, 0.999)
    s = u ** (1.0 / LRU_C)
    lru_lambda = jnp.log(s) - jnp.log1p(-s)
    return {
        "x": nrm(ks[0], (BATCH, SEQ, D_MODEL), 1.0),
        "c": nrm(ks[1], (BATCH, D_MODEL), 1.0),
        "positions": jnp.broadcast_to(jnp.arange(SEQ, dtype=jnp.int32), (BATCH, SEQ)),
        "w_ada": nrm(ks[2], (DEPTH, D_MODEL, N_SUB * 3 * D_MODEL), 0.5 * D_MODEL ** -0.5),
        "b_ada": nrm(ks[3], (DEPTH, N_SUB * 3 * D_MODEL), 0.02),
        "norm_g": 1.0 + nrm(ks[4], (DEPTH, 2 * N_SUB, D_MODEL), 0.05),
        "ffn1_w_in": nrm(ks[5], (DEPTH, D_MODEL, 2 * D_FF), D_MODEL ** -0.5),
        "ffn1_w_out": nrm(ks[6], (DEPTH, D_FF, D_MODEL), D_FF ** -0.5),
        "ffn2_w_in": nrm(ks[7], (DEPTH, D_MODEL, 2 * D_FF), D_MODEL ** -0.5),
        "ffn2_w_out": nrm(ks[8], (DEPTH, D_FF, D_MODEL), D_FF ** -0.5),
        "w_mix_in": nrm(ks[9], (DEPTH, D_MODEL, MIX_IN), D_MODEL ** -0.5),
        "w_mix_out": nrm(ks[10], (DEPTH, D_MIX, D_MODEL), D_MIX ** -0.5),
        "lambda_q": nrm(ks[11], (DEPTH, 2, HEAD_DIM), 0.1),
        "lambda_k": nrm(ks[12], (DEPTH, 2, HEAD_DIM), 0.1),
        "subln_g": 1.0 + nrm(ks[13], (DEPTH, V_DIM), 0.05),
        "conv_w": nrm(ks[14], (DEPTH, CONV_WIDTH, D_LRU), CONV_WIDTH ** -0.5),
        "conv_b": nrm(ks[15], (DEPTH, D_LRU), 0.02),
        "lru_w_gate": nrm(ks[16], (DEPTH, 2, 2, N_LRU_BLOCKS, LRU_BLOCK, LRU_BLOCK), LRU_BLOCK ** -0.5),
        "lru_b_gate": nrm(ks[17], (DEPTH, 2, 2, D_LRU), 0.1),
        "lru_lambda": lru_lambda,
    }

def first_block(x, c, positions, w_ada, b_ada, norm_g, ffn1_w_in, ffn1_w_out, ffn2_w_in, ffn2_w_out,
              w_mix_in, w_mix_out, lambda_q, lambda_k, subln_g, conv_w, conv_b,
              lru_w_gate, lru_b_gate, lru_lambda):
    B, S, D = x.shape
    cos, sin = rope_tables(positions)
    cond = jax.nn.silu(c)
    split_pts = [D_ATTN, 2 * D_ATTN, 3 * D_ATTN, 3 * D_ATTN + D_LRU]

    for l in range(DEPTH):
        ada = (cond @ w_ada[l] + b_ada[l]).reshape(B, N_SUB, 3, D)

        def sublayer(h_res, j, fn, res_w):
            shift = ada[:, j, 0][:, None, :]
            scale = ada[:, j, 1][:, None, :]
            gate = ada[:, j, 2][:, None, :]
            h = rms_norm(h_res, norm_g[l, 2 * j]) * (1.0 + scale) + shift
            y = rms_norm(fn(h), norm_g[l, 2 * j + 1])
            return h_res + res_w * gate * y

        lambda_init = 0.8 - 0.6 * math.exp(-0.3 * l)
        lam = (jnp.exp(jnp.sum(lambda_q[l, 0].astype(jnp.float32) * lambda_k[l, 0].astype(jnp.float32)))
               - jnp.exp(jnp.sum(lambda_q[l, 1].astype(jnp.float32) * lambda_k[l, 1].astype(jnp.float32)))
               + lambda_init)

        def mixer(h):
            z = h @ w_mix_in[l]
            q, k, v, xr, yr = jnp.split(z, split_pts, axis=-1)
            q = q.reshape(B, S, N_ATTN_HEADS, 2, HEAD_DIM)
            k = k.reshape(B, S, N_ATTN_HEADS, 2, HEAD_DIM)
            v = v.reshape(B, S, N_ATTN_HEADS, V_DIM)
            attn = diff_attention(q, k, v, lam, subln_g[l], lambda_init, cos, sin)
            rec = recurrent_group(xr, yr, conv_w[l], conv_b[l], lru_w_gate[l], lru_b_gate[l], lru_lambda[l])
            return jnp.concatenate([attn, rec], axis=-1) @ w_mix_out[l]

        x = sublayer(x, 0, lambda h: swiglu(h, ffn1_w_in[l], ffn1_w_out[l]), 0.5)
        x = sublayer(x, 1, mixer, 1.0)
        x = sublayer(x, 2, lambda h: swiglu(h, ffn2_w_in[l], ffn2_w_out[l]), 0.5)
    return x


_first_inputs = first_inputs


def first_inputs(seed=0):
    import zlib

    import numpy as np

    out = dict(_first_inputs(seed))
    spreads = {}
    factors = {'lambda_q': 8.0, 'lambda_k': 8.0, 'subln_g': 8.0, 'conv_b': 3.305, 'lru_b_gate': 7.089}
    for name, (base, spread) in spreads.items():
        noise = np.random.default_rng([zlib.crc32(name.encode()), seed]).standard_normal(out[name].shape)
        drawn = base * np.exp(spread * noise) if base else spread * noise
        out[name] = __import__('jax').numpy.asarray(drawn.astype(out[name].dtype))
    for name, factor in factors.items():
        out[name] = (out[name] * factor).astype(out[name].dtype)
    return out


_narrow_inputs = first_inputs


def first_inputs(seed=0):
    out = dict(_narrow_inputs(seed))
    wider = {'subln_g': 4.64, 'conv_b': 3.44, 'lru_w_gate': 3.04, 'lru_b_gate': 3.48}
    for name, times in wider.items():
        mean = out[name].mean()
        out[name] = (mean + times * (out[name] - mean)).astype(out[name].dtype)
    return out


DEPTH_2 = 2

GRID_W = 64
CTX_LEN = 256
N_Q_HEADS = 8
N_KV_HEADS = 2
Q_PER_KV = N_Q_HEADS // N_KV_HEADS
ATTN_WIDTH = N_Q_HEADS * HEAD_DIM
KV_WIDTH = N_KV_HEADS * HEAD_DIM
POOL_WINDOWS = (2, 4, 8, 16)
POOL_GROUP = 128
POOL_WIDTH = POOL_GROUP * len(POOL_WINDOWS)
SG_GROUPS = 4
SG_GROUP_WIDTH = 128
SG_CHUNK = 128
SG_WIDTH = SG_GROUPS * SG_GROUP_WIDTH
CONV_WIDTH_2 = 512
CONV_K = 3
EVEN_IN = ATTN_WIDTH + 2 * KV_WIDTH + POOL_WIDTH
ODD_IN = 2 * SG_WIDTH + 3 * CONV_WIDTH_2
MIX_WIDTH = ATTN_WIDTH + POOL_WIDTH
N_GROUPS = 4
EXPERTS_PER_GROUP = 4
N_EXPERTS = N_GROUPS * EXPERTS_PER_GROUP
TOP_K = 2
D_EXPERT = 256


def rms_norm_2(x, gain):
    x32 = x.astype(jnp.float32)
    y = x32 * lax.rsqrt(jnp.mean(x32 * x32, axis=-1, keepdims=True) + EPS)
    return (y * gain.astype(jnp.float32)).astype(x.dtype)

def modulate(x, gain, shift, scale):
    return rms_norm_2(x, gain) * (1 + scale) + shift

def adaln(cond, mod_w, mod_b):
    m = jax.nn.silu(cond) @ mod_w + mod_b
    return jnp.split(m, 6, axis=-1)

def axial_angles(n_rows):
    row = jnp.repeat(jnp.arange(n_rows, dtype=jnp.float32), GRID_W)
    col = jnp.tile(jnp.arange(GRID_W, dtype=jnp.float32), n_rows)
    half = HEAD_DIM // 2
    inv = ROPE_THETA ** (-jnp.arange(0, half, 2, dtype=jnp.float32) / half)
    return row[:, None] * inv, col[:, None] * inv

def rope_1d(x, ang):
    cos = jnp.cos(ang)[None, :, None, :]
    sin = jnp.sin(ang)[None, :, None, :]
    x1, x2 = jnp.split(x, 2, axis=-1)
    return jnp.concatenate([x1 * cos - x2 * sin, x2 * cos + x1 * sin], axis=-1)

def rope_2d(x, row_ang, col_ang):
    x32 = x.astype(jnp.float32)
    xr, xc = jnp.split(x32, 2, axis=-1)
    return jnp.concatenate([rope_1d(xr, row_ang), rope_1d(xc, col_ang)], axis=-1).astype(x.dtype)

def gqa_attend(q, k, v):
    s = jnp.einsum('bqkgd,bskd->bkgqs', q, k, preferred_element_type=jnp.float32) * (HEAD_DIM ** -0.5)
    p = jax.nn.softmax(s, axis=-1).astype(v.dtype)
    return jnp.einsum('bkgqs,bskd->bqkgd', p, v)

def multiscale_pool(p, pool_w, pool_scale):
    bsz, length, _ = p.shape
    p32 = p.astype(jnp.float32)
    cs = jnp.concatenate([jnp.zeros_like(p32[:, :1]), jnp.cumsum(p32, axis=1)], axis=1)
    t = jnp.arange(length)
    diffs = []
    for g, w in enumerate(POOL_WINDOWS):
        lo = jnp.clip(t - w // 2, 0, length)
        hi = jnp.clip(t + w - w // 2, 0, length)
        sl = slice(g * POOL_GROUP, (g + 1) * POOL_GROUP)
        csg = cs[..., sl]
        mean = (csg[:, hi] - csg[:, lo]) / (hi - lo).astype(jnp.float32)[None, :, None]
        diffs.append(mean - p32[..., sl])
    d = jnp.stack(diffs, axis=2).astype(p.dtype)
    y = jnp.einsum('blgc,gcd->blgd', d, pool_w).reshape(bsz, length, POOL_WIDTH)
    return y * pool_scale

def even_mixer(h, hc, w_in, q_gain, k_gain, pool_w, pool_scale, w_out, row_ang, col_ang, need_ctx_out):
    bsz, seq, _ = h.shape
    n_ctx = hc.shape[1]
    q, k, v, p = jnp.split(h @ w_in, [ATTN_WIDTH, ATTN_WIDTH + KV_WIDTH, ATTN_WIDTH + 2 * KV_WIDTH], axis=-1)
    q = rope_2d(rms_norm_2(q.reshape(bsz, seq, N_Q_HEADS, HEAD_DIM), q_gain), row_ang, col_ang)
    k = rope_2d(rms_norm_2(k.reshape(bsz, seq, N_KV_HEADS, HEAD_DIM), k_gain), row_ang, col_ang)
    v = v.reshape(bsz, seq, N_KV_HEADS, HEAD_DIM)
    if need_ctx_out:
        qc, kc, vc, pc = jnp.split(hc @ w_in, [ATTN_WIDTH, ATTN_WIDTH + KV_WIDTH, ATTN_WIDTH + 2 * KV_WIDTH], axis=-1)
    else:
        kc, vc = jnp.split(hc @ w_in[:, ATTN_WIDTH:ATTN_WIDTH + 2 * KV_WIDTH], [KV_WIDTH], axis=-1)
    kc = rms_norm_2(kc.reshape(bsz, n_ctx, N_KV_HEADS, HEAD_DIM), k_gain)
    vc = vc.reshape(bsz, n_ctx, N_KV_HEADS, HEAD_DIM)
    k_all = jnp.concatenate([kc, k], axis=1)
    v_all = jnp.concatenate([vc, v], axis=1)
    n_blk = seq // Q_BLOCK
    qb = q.reshape(bsz, n_blk, Q_BLOCK, N_KV_HEADS, Q_PER_KV, HEAD_DIM).transpose(1, 0, 2, 3, 4, 5)
    o = lax.map(lambda qq: gqa_attend(qq, k_all, v_all), qb)
    o = o.transpose(1, 0, 2, 3, 4, 5).reshape(bsz, seq, ATTN_WIDTH)
    y = jnp.concatenate([o, multiscale_pool(p, pool_w, pool_scale)], axis=-1) @ w_out
    if need_ctx_out:
        qc = rms_norm_2(qc.reshape(bsz, n_ctx, N_Q_HEADS, HEAD_DIM), q_gain).reshape(bsz, n_ctx, N_KV_HEADS, Q_PER_KV, HEAD_DIM)
        oc = gqa_attend(qc, kc, vc).reshape(bsz, n_ctx, ATTN_WIDTH)
        yc = jnp.concatenate([oc, multiscale_pool(pc, pool_w, pool_scale)], axis=-1) @ w_out
    else:
        yc = None
    return y, yc

def odd_mixer(h, w_in, sg_gain, sg_w, sg_b, conv_w, w_out):
    bsz, length, _ = h.shape
    u, v, hx, bg, cg = jnp.split(h @ w_in, [SG_WIDTH, 2 * SG_WIDTH, 2 * SG_WIDTH + CONV_WIDTH_2, 2 * SG_WIDTH + 2 * CONV_WIDTH_2], axis=-1)
    v = rms_norm_2(v.reshape(bsz, length // SG_CHUNK, SG_CHUNK, SG_GROUPS, SG_GROUP_WIDTH), sg_gain)
    s = jnp.einsum('gpq,bnqgc->bnpgc', sg_w, v) + sg_b.T[:, :, None]
    y_c = u * s.reshape(bsz, length, SG_WIDTH)
    z = cg * hx
    zc = lax.conv_general_dilated(z, conv_w, window_strides=(1,), padding=((CONV_K // 2, CONV_K // 2),),
                                  dimension_numbers=('NWC', 'WIO', 'NWC'), feature_group_count=CONV_WIDTH_2)
    y_d = bg * zc
    return jnp.concatenate([y_c, y_d], axis=-1) @ w_out

def hier_moe(h, rg_w, rg_b, re_w, re_b, w_gate, w_up, w_down):
    shape = h.shape
    t = h.reshape(-1, shape[-1])
    t32 = t.astype(jnp.float32)
    n_tok = t.shape[0]
    g_prob = jax.nn.softmax(t32 @ rg_w.astype(jnp.float32) + rg_b.astype(jnp.float32), axis=-1)
    g_p, g_idx = lax.top_k(g_prob, 1)
    e_logits = (t32 @ re_w.astype(jnp.float32) + re_b.astype(jnp.float32)).reshape(n_tok, N_GROUPS, EXPERTS_PER_GROUP)
    e_sel = jnp.take_along_axis(e_logits, g_idx[:, :, None], axis=1)[:, 0]
    top_p, top_i = lax.top_k(jax.nn.softmax(e_sel, axis=-1), TOP_K)
    top_p = top_p / jnp.sum(top_p, axis=-1, keepdims=True)
    weights = g_p * top_p
    expert_id = g_idx * EXPERTS_PER_GROUP + top_i
    comb = jnp.sum(jax.nn.one_hot(expert_id, N_EXPERTS, dtype=jnp.float32) * weights[..., None], axis=1)

    def step(acc, xs):
        wg, wu, wd, cw = xs
        y = (jax.nn.silu(t @ wg) * (t @ wu)) @ wd
        return acc + y.astype(jnp.float32) * cw[:, None], None

    acc, _ = lax.scan(step, jnp.zeros(t.shape, jnp.float32), (w_gate, w_up, w_down, comb.T))
    return acc.astype(h.dtype).reshape(shape)

def second_inputs(seed: int = 0) -> dict:
    key = jax.random.key(seed)
    ks = jax.random.split(key, 32)
    n_even = (DEPTH_2 + 1) // 2
    n_odd = DEPTH_2 // 2
    f32 = jnp.float32

    def nrm(k, shape, scale):
        return jax.random.normal(k, shape, f32) * scale

    def gain(k, shape, noise=0.05):
        return 1.0 + nrm(k, shape, noise)

    return {
        'x': nrm(ks[0], (BATCH, SEQ, D_MODEL), 1.0),
        'c': nrm(ks[1], (BATCH, D_MODEL), 1.0),
        'ctx': nrm(ks[2], (BATCH, CTX_LEN, D_MODEL), 1.0),
        'c_ctx': nrm(ks[3], (D_MODEL,), 1.0),
        'mod_w': nrm(ks[4], (DEPTH_2, D_MODEL, 6 * D_MODEL), 0.5 * D_MODEL ** -0.5),
        'mod_b': nrm(ks[5], (DEPTH_2, 6 * D_MODEL), 0.02),
        'norm1_g': gain(ks[6], (DEPTH_2, D_MODEL)),
        'norm2_g': gain(ks[7], (DEPTH_2, D_MODEL)),
        'even_w_in': nrm(ks[8], (n_even, D_MODEL, EVEN_IN), D_MODEL ** -0.5),
        'q_gain': gain(ks[9], (n_even, HEAD_DIM)),
        'k_gain': gain(ks[10], (n_even, HEAD_DIM)),
        'pool_w': nrm(ks[11], (n_even, len(POOL_WINDOWS), POOL_GROUP, POOL_GROUP), POOL_GROUP ** -0.5),
        'pool_scale': gain(ks[12], (n_even, POOL_WIDTH), 0.1),
        'even_w_out': nrm(ks[13], (n_even, MIX_WIDTH, D_MODEL), MIX_WIDTH ** -0.5),
        'odd_w_in': nrm(ks[14], (n_odd, D_MODEL, ODD_IN), D_MODEL ** -0.5),
        'sg_gain': gain(ks[15], (n_odd, SG_GROUPS, SG_GROUP_WIDTH)),
        'sg_w': nrm(ks[16], (n_odd, SG_GROUPS, SG_CHUNK, SG_CHUNK), SG_CHUNK ** -0.5),
        'sg_b': gain(ks[17], (n_odd, SG_GROUPS, SG_CHUNK), 0.1),
        'conv_w': nrm(ks[18], (n_odd, CONV_K, 1, CONV_WIDTH_2), CONV_K ** -0.5),
        'odd_w_out': nrm(ks[19], (n_odd, MIX_WIDTH, D_MODEL), MIX_WIDTH ** -0.5),
        'router_g_w': nrm(ks[20], (DEPTH_2, D_MODEL, N_GROUPS), D_MODEL ** -0.5),
        'router_g_b': nrm(ks[21], (DEPTH_2, N_GROUPS), 0.01),
        'router_e_w': nrm(ks[22], (DEPTH_2, D_MODEL, N_EXPERTS), D_MODEL ** -0.5),
        'router_e_b': nrm(ks[23], (DEPTH_2, N_EXPERTS), 0.01),
        'w_gate': nrm(ks[24], (DEPTH_2, N_EXPERTS, D_MODEL, D_EXPERT), D_MODEL ** -0.5),
        'w_up': nrm(ks[25], (DEPTH_2, N_EXPERTS, D_MODEL, D_EXPERT), D_MODEL ** -0.5),
        'w_down': nrm(ks[26], (DEPTH_2, N_EXPERTS, D_EXPERT, D_MODEL), D_EXPERT ** -0.5),
    }

def second_block(x, c, ctx, c_ctx, mod_w, mod_b, norm1_g, norm2_g, even_w_in, q_gain, k_gain, pool_w, pool_scale,
              even_w_out, odd_w_in, sg_gain, sg_w, sg_b, conv_w, odd_w_out, router_g_w, router_g_b,
              router_e_w, router_e_b, w_gate, w_up, w_down):
    seq = x.shape[1]
    ROWS = seq // GRID_W
    row_ang, col_ang = axial_angles(ROWS)
    last_even = 2 * ((DEPTH_2 - 1) // 2)
    h_lat, h_ctx = x, ctx
    for i in range(DEPTH_2):
        j = i // 2
        need_ctx_in = i <= last_even
        need_ctx_out = i < last_even
        sh1, sc1, g1, sh2, sc2, g2 = [m[:, None, :] for m in adaln(c, mod_w[i], mod_b[i])]
        a = modulate(h_lat, norm1_g[i], sh1, sc1)
        if need_ctx_in:
            csh1, csc1, cg1, csh2, csc2, cg2 = adaln(c_ctx, mod_w[i], mod_b[i])
            ac = modulate(h_ctx, norm1_g[i], csh1, csc1)
        if i % 2 == 0:
            y, yc = even_mixer(a, ac, even_w_in[j], q_gain[j], k_gain[j], pool_w[j], pool_scale[j],
                               even_w_out[j], row_ang, col_ang, need_ctx_out)
        else:
            y = odd_mixer(a, odd_w_in[j], sg_gain[j], sg_w[j], sg_b[j], conv_w[j], odd_w_out[j])
            yc = odd_mixer(ac, odd_w_in[j], sg_gain[j], sg_w[j], sg_b[j], conv_w[j], odd_w_out[j]) if need_ctx_out else None
        moe_args = (router_g_w[i], router_g_b[i], router_e_w[i], router_e_b[i], w_gate[i], w_up[i], w_down[i])
        h_lat = h_lat + g1 * y
        h_lat = h_lat + g2 * hier_moe(modulate(h_lat, norm2_g[i], sh2, sc2), *moe_args)
        if need_ctx_out:
            h_ctx = h_ctx + cg1 * yc
            h_ctx = h_ctx + cg2 * hier_moe(modulate(h_ctx, norm2_g[i], csh2, csc2), *moe_args)
    return h_lat


def setup_inputs(seed=0):
    out = dict(first_inputs(seed))
    for name, value in second_inputs(seed + 1).items():
        if name != "x":
            out[name + "_2"] = value
    return out


def reference(
    x, c, positions, w_ada, b_ada, norm_g, ffn1_w_in, ffn1_w_out, ffn2_w_in, ffn2_w_out,
    w_mix_in, w_mix_out, lambda_q, lambda_k, subln_g, conv_w, conv_b, lru_w_gate, lru_b_gate,
    lru_lambda, c_2, ctx_2, c_ctx_2, mod_w_2, mod_b_2, norm1_g_2, norm2_g_2, even_w_in_2,
    q_gain_2, k_gain_2, pool_w_2, pool_scale_2, even_w_out_2, odd_w_in_2, sg_gain_2, sg_w_2,
    sg_b_2, conv_w_2, odd_w_out_2, router_g_w_2, router_g_b_2, router_e_w_2, router_e_b_2,
    w_gate_2, w_up_2, w_down_2,
):
    x = first_block(
        x, c, positions, w_ada, b_ada, norm_g, ffn1_w_in, ffn1_w_out, ffn2_w_in, ffn2_w_out,
        w_mix_in, w_mix_out, lambda_q, lambda_k, subln_g, conv_w, conv_b, lru_w_gate,
        lru_b_gate, lru_lambda,
    )
    return second_block(
        x, c_2, ctx_2, c_ctx_2, mod_w_2, mod_b_2, norm1_g_2, norm2_g_2, even_w_in_2, q_gain_2,
        k_gain_2, pool_w_2, pool_scale_2, even_w_out_2, odd_w_in_2, sg_gain_2, sg_w_2, sg_b_2,
        conv_w_2, odd_w_out_2, router_g_w_2, router_g_b_2, router_e_w_2, router_e_b_2, w_gate_2,
        w_up_2, w_down_2,
    )


_drawn_inputs = setup_inputs


def setup_inputs(seed=0):
    import zlib

    import numpy as np

    out = dict(_drawn_inputs(seed))
    spreads = {}
    factors = {'ctx_2': 5.707,
     'q_gain_2': 8.0,
     'k_gain_2': 8.0,
     'sg_gain_2': 4.797,
     'router_g_b_2': 23.122,
     'router_e_b_2': 24.818,
     'sg_b_2': 3.463}
    for name, (base, spread) in spreads.items():
        noise = np.random.default_rng([zlib.crc32(name.encode()), seed]).standard_normal(out[name].shape)
        drawn = base * np.exp(spread * noise) if base else spread * noise
        out[name] = __import__('jax').numpy.asarray(drawn.astype(out[name].dtype))
    for name, factor in factors.items():
        out[name] = (out[name] * factor).astype(out[name].dtype)
    return out
```

```python
import concourse.bass as bass
from concourse import mybir
from contextlib import ExitStack

F32 = mybir.dt.float32
F32R = mybir.dt.float32r
I32 = mybir.dt.int32
ALU = mybir.AluOpType
ACT = mybir.ActivationFunctionType
AX = mybir.AxisListType

P = 128
D = 1024
KC = D // P
S = 512
TT = S // P
CTX = 256
CT = CTX // P
D_FF = 2816
UNIT = 256
FFN_UNITS = D_FF // UNIT
EXPERTS = 16
HEADS1 = 4
EPS = 1e-6
LAMBDA_INIT = 0.2
TW = 2048
RING = 3

COLS = [("c", 8), ("c2", 8), ("cctx", 8), ("b_ada", 72), ("mod_b", 96), ("norm_g", 48), ("norm1", 16),
        ("norm2", 16), ("subln", 1), ("conv_w", 16), ("conv_b", 4), ("b_gate", 16), ("lam", 8),
        ("q_gain", 1), ("k_gain", 1), ("pool_scale", 4), ("sg_gain", 4), ("conv_w2", 12), ("inv_freq", 1)]
COL = {}
_at = 0
for _name, _n in COLS:
    COL[_name] = _at
    _at += _n
NCOL = _at

UNIT_GROUPS = [2, 2, 8]
STREAM = [("ffn1", UNIT_GROUPS * FFN_UNITS), ("mixin", [2] * 10), ("mixout", [2] * 4),
          ("ffn2", UNIT_GROUPS * FFN_UNITS), ("evenin", [4, 2, 2, 2, 2]), ("evenout", [2] * 4),
          ("moe0", UNIT_GROUPS * EXPERTS), ("oddin", [2] * 10), ("oddout", [2] * 4),
          ("moe1", UNIT_GROUPS * EXPERTS)]
T0, GROUPS_BEFORE = {}, [0]
for _name, _g in STREAM:
    T0[_name] = len(GROUPS_BEFORE) - 1
    for _x in _g:
        GROUPS_BEFORE.append(GROUPS_BEFORE[-1] + _x)
TILES = len(GROUPS_BEFORE) - 1
UNIT0 = {"ffn1": 0, "ffn2": FFN_UNITS, "moe0": 2 * FFN_UNITS, "moe1": 2 * FFN_UNITS + EXPERTS}
UNITS = {"ffn1": FFN_UNITS, "ffn2": FFN_UNITS, "moe0": EXPERTS, "moe1": EXPERTS}

MOD_PER_UNIT = {"ffn1": 5, "ffn2": 4, "moe0": 3, "moe1": 0}
MOD_FIRST = [("ada", 0, 5), ("ada", 5, 5), ("ada", 10, 5), ("ada", 15, 2),
             ("ctx", 0, 4), ("ctx", 4, 4), ("ctx", 8, 4), ("ctx", 12, 4), ("mod0", 44, 4)]
MOD_COND = {"ada": 0, "mod0": 8, "mod1": 8, "ctx": 16}
MOD_OUT = {"ada": 0, "mod0": 72, "mod1": 120, "ctx": 168}
MOD_BIAS = {"ada": COL["b_ada"], "mod0": COL["mod_b"], "mod1": COL["mod_b"] + 48, "ctx": COL["mod_b"]}
MOD_SLOTS = 5
MOD_LOOP = {"ffn1": ("ada", 17), "ffn2": ("mod0", 0), "moe0": ("mod1", 0)}
MB0, MQ0 = {}, {}
_b, _q = len(MOD_FIRST), sum(n for _, _, n in MOD_FIRST)
for _name in ("ffn1", "ffn2", "moe0"):
    MB0[_name], MQ0[_name] = _b, _q
    _b += UNITS[_name]
    _q += UNITS[_name] * MOD_PER_UNIT[_name]


def mod_fills(stage, r):
    n = sum(1 for _, _, k in MOD_FIRST if k > r)
    for name in ("ffn1", "ffn2", "moe0"):
        if name == stage:
            return n
        n += UNITS[name] * (MOD_PER_UNIT[name] > r)


PRIME_SILU, PRIME_GU, PRIME_ADD = 2, 2, 8

NORM = {"ffn1": (0, 0), "ffn1_end": (1, None), "mix": (2, 1), "mix_end": (3, None), "ffn2": (4, 2),
        "ffn2_end": (5, None), "ctx": (6, 3), "even": (7, 4), "moe0": (8, 5), "odd": (9, 6), "moe1": (10, 7)}
XDONE = {"ffn1": 0, "mix": 8, "ffn2": 16, "even": 24, "moe0": 32, "odd": 40, "moe1": 48, "end": 56}
Z0 = {"mixin": 0, "mixout": 20, "evenin": 28, "oddin": 40}


def build(nc, io):
    ctx = ExitStack()
    with ctx:
        def sb(name, shape, dt=F32):
            return ctx.enter_context(nc.sbuf_tensor(name, shape, dt))

        names = set()

        def sem(name):
            names.add(name)
            return ctx.enter_context(nc.semaphore(name))

        w_raw = sb("w_raw", [P, RING, TW])
        w_hi = sb("w_hi", [P, RING, TW], F32R)
        w_lo = sb("w_lo", [P, RING, TW], F32R)
        x = sb("x", [P, KC, S])
        a_hi = sb("a_hi", [P, KC, S], F32R)
        a_lo = sb("a_lo", [P, KC, S], F32R)
        h_hi = sb("h_hi", [P, 2, S], F32R)
        h_lo = sb("h_lo", [P, 2, S], F32R)
        nt = sb("nt", [P, 4, S])
        root = sb("root", [P, S])
        rinv = sb("rinv", [P, S])
        rope = sb("rope", [P, 2, S])
        red = sb("red", [P, MOD_SLOTS, P])
        pv = sb("pv", [P, NCOL])
        cond = sb("cond", [P, 24])
        mods = sb("mods", [P, 184])
        acol = sb("acol", [P, 8 * KC])
        gcol = sb("gcol", [P, 3 * KC])
        misc = sb("misc", [P, 64])
        stat = sb("stat", [P, 5, 32])
        ident = sb("ident", [P, P])
        ones = sb("ones", [P, P])
        ones64 = sb("ones64", [P, P])
        rot1 = sb("rot1", [P, P])
        rot2 = sb("rot2", [P, P])
        rw = sb("rw", [P, KC, 20])
        rw_hi = sb("rw_hi", [P, KC, 20], F32R)
        rw_lo = sb("rw_lo", [P, KC, 20], F32R)
        rb = sb("rb", [P, 2, 20])
        rt = sb("rt", [P, 320])
        K = 256
        arena = sb("arena", [P, 52 * K + 32])

        def ar(start, *shape):
            n = 1
            for d in shape:
                n *= d
            v = arena[:, start:start + n]
            if len(shape) == 2:
                v = v.rearrange("p (a b) -> p a b", b=shape[1])
            if len(shape) == 3:
                v = v.rearrange("p (a b c) -> p a b c", b=shape[1], c=shape[2])
            return v

        yacc = ar(0, KC, S)
        sg = ar(16 * K, 2, S)
        hid = ar(20 * K, 2, S)
        comb_row = ar(24 * K, S)
        comb_pad = ar(26 * K, TT, 32)
        comb_t = ar(26 * K + 128, TT, 32)
        mod_raw = ar(28 * K, MOD_SLOTS, KC, P)
        prod = ar(48 * K, KC, P)
        q1, k1, v1 = ar(0, 4, S), ar(8 * K, 4, S), ar(16 * K, 4, S)
        XRW = S + 3
        xr1 = ar(24 * K, 4, XRW)
        yr1 = ar(32 * K + 16, 4, S)
        bd = ar(40 * K + 16, 4, 4 * P)
        e0, e1 = ar(48 * K + 16, S), ar(50 * K + 16, S)
        pexp1 = ar(24 * K, 4, S)
        wsm1 = ar(32 * K, 2, S)
        wt1 = ar(36 * K, 4, S)
        SK = CTX + S
        q2 = ar(0, 4, S)
        kall, kswap = ar(8 * K, SK), ar(11 * K, SK)
        vz = ar(14 * K, 12, 192)
        PW = S + 16
        p2 = ar(23 * K + 64, 4, PW)
        ctxx = ar(32 * K, KC, CTX)
        ic = ar(41 * K, 4, S)
        poolw = ar(49 * K, 4, P)
        pexp2 = ar(32 * K, 2, SK)
        wt2 = ar(38 * K, 6, S)
        u3, v3 = ar(0, 4, S), ar(8 * K, 4, S)
        ZW = S + 2
        z3 = ar(16 * K, 4, ZW)
        bg3, cg3 = ar(25 * K, 4, S), ar(33 * K, 4, S)
        sgw = ar(41 * K, 4, P)
        sgb = ar(43 * K, 4, P)

        G = ctx.enter_context(nc.psum_tensor("G", [P, 4, S], F32))
        Dn = ctx.enter_context(nc.psum_tensor("Dn", [P, 4, S], F32))
        M = 3

        def sum_bank(name):
            return G[:, 3] if name.endswith("_end") else Dn[:, 2]

        def w_in(buf, slot):
            return buf[:, slot, :].rearrange("p (k n) -> p k n", n=256)

        def w_down(buf, slot):
            return buf[:, slot, :].rearrange("p (k n) -> p k n", n=D)

        raw_full = [sem(f"raw_full{s}") for s in range(RING)]
        weight_hi, weight_lo, group_done = sem("weight_hi"), sem("weight_lo"), sem("group_done")
        mod_full = [sem(f"mod_full{s}") for s in range(MOD_SLOTS)]
        mod_mul, mod_red, mod_sum, mod_out = sem("mod_mul"), sem("mod_red"), sem("mod_sum"), sem("mod_out")
        act_silu, dve_gu, act_hhi, dve_hlo, down_added = (sem(n) for n in (
            "act_silu", "dve_gu", "act_hhi", "dve_hlo", "down_added"))
        dve_comb, comb_full = sem("dve_comb"), sem("comb_full")
        act_sq, pe_ss, act_root, dve_rinv = sem("act_sq"), sem("pe_ss"), sem("act_root"), sem("dve_rinv")
        dve_cols, dve_t, act_af, act_ahi, dve_alo = (sem(n) for n in (
            "dve_cols", "dve_t", "act_af", "act_ahi", "dve_alo"))
        dve_yn, x_done = sem("dve_yn"), sem("x_done")
        act_z = sem("act_z")
        ld_x, ld_pv, ld_const, ld_row = sem("ld_x"), sem("ld_pv"), sem("ld_const"), sem("ld_row")
        ld_mix, ld_ctx, ld_even, ld_rope2, ld_odd = (sem(n) for n in (
            "ld_mix", "ld_ctx", "ld_even", "ld_rope2", "ld_odd"))
        ld_rw = [sem("ld_rw0"), sem("ld_rw1")]
        cond_done, dve_chain, act_chain = sem("cond_done"), sem("dve_chain"), sem("act_chain")
        rope1_ang, rope1_tab = sem("rope1_ang"), sem("rope1_tab")
        yacc_zero, arena_free, arena_back = sem("yacc_zero"), sem("arena_free"), sem("arena_back")
        lam_sum, lam_exp, sp_exp = sem("lam_sum"), sem("lam_exp"), sem("sp_exp")
        m1_pad, m1_gelu, m1_xc, m1_gate, m1_sig, m1_at, m1_m, m1_sqrt, m1_rec = (sem("m1_" + n) for n in (
            "pad", "gelu", "xc", "gate", "sig", "at", "m", "sqrt", "rec"))
        m1_rot, m1_rope, m1_qk, m1_nm, m1_exp, m1_w, m1_tr, m1_wt, m1_pv, m1_o = (sem("m1_" + n) for n in (
            "rot", "rope", "qk", "nm", "exp", "w", "tr", "wt", "pv", "o"))
        m1_ssq, m1_ssp, m1_srt, m1_sub = (sem("m1_" + n) for n in ("ssq", "ssp", "srt", "sub"))
        m2_pad, m2_ssq, m2_ssp, m2_srt, m2_kn, m2_rot, m2_rope, m2_swap = (sem("m2_" + n) for n in (
            "pad", "ssq", "ssp", "srt", "kn", "rot", "rope", "swap"))
        m2_d, m2_pw, m2_ps, m2_pool = (sem("m2_" + n) for n in ("d", "pw", "ps", "pool"))
        m2_qk, m2_nm, m2_exp, m2_w, m2_tr, m2_wt, m2_pv, m2_ohi, m2_olo = (sem("m2_" + n) for n in (
            "qk", "nm", "exp", "w", "tr", "wt", "pv", "ohi", "olo"))
        m3_pad, m3_ss, m3_srt, m3_vn, m3_sg, m3_y = (sem("m3_" + n) for n in (
            "pad", "ss", "srt", "vn", "sg", "y"))
        rt_w, rt_logit, rt_d1, rt_exp1, rt_d2, rt_exp2, rt_comb, rt_store = (sem("rt_" + n) for n in (
            "w", "logit", "d1", "exp1", "d2", "exp2", "comb", "store"))
        st_out = sem("st_out")

        io_w = {n: io[n].rearrange("(k p) n -> p k n", p=P) for n in (
            "ffn1_w_in", "ffn2_w_in", "w_mix_in", "w_mix_out", "even_w_in", "even_w_out",
            "odd_w_in", "odd_w_out", "w_ada")}
        io_down = {n: io[n].rearrange("(u k p) n -> u p k n", k=2, p=P) for n in ("ffn1_w_out", "ffn2_w_out")}
        moe_gate = io["w_gate"].rearrange("l e (k p) n -> (l e) p k n", p=P)
        moe_up = io["w_up"].rearrange("l e (k p) n -> (l e) p k n", p=P)
        moe_down = io["w_down"].rearrange("l e (k p) n -> (l e) p k n", p=P)
        mod_w = {"ada": io_w["w_ada"],
                 "mod0": io["mod_w"][0].rearrange("(k p) n -> p k n", p=P),
                 "mod1": io["mod_w"][1].rearrange("(k p) n -> p k n", p=P)}
        mod_w["ctx"] = mod_w["mod0"]
        comb_dram = io["comb_dram"]

        block = ctx.enter_context(nc.Block())

        @block.sync
        def _(sp):
            def tile(t, source, buf, i=0):
                s = t % RING
                if not isinstance(i, int) or t + 3 * i >= RING:
                    sp.wait_ge(weight_lo, 3 * i + (t - RING + 1))
                sp.dma_start(buf(w_raw, s), source).then_inc(raw_full[s], 16)

            def mod_chunk(r, matrix, col):
                sp.dma_start(mod_raw[:, r], mod_w[matrix][:, :, bass.ds(col * P, P)]).then_inc(mod_full[r], 16)

            def unit_tiles(stage, i):
                t = T0[stage]
                if stage[:3] == "ffn":
                    w = io_w[stage + "_w_in"]
                    src = (w[:, :, bass.ds(i * UNIT, UNIT)], w[:, :, bass.ds(i * UNIT + D_FF, UNIT)],
                           io_down[stage + "_w_out"][i])
                else:
                    e = i + EXPERTS * (stage == "moe1")
                    src = (moe_gate[e], moe_up[e], moe_down[e])
                tile(t, src[0], w_in, i)
                tile(t + 1, src[1], w_in, i)
                tile(t + 2, src[2], w_down, i)
                if stage in ("ffn2", "moe0"):
                    sp.wait_ge(arena_back, 1 + (stage == "moe0"))
                for r in range(MOD_PER_UNIT[stage]):
                    if r == 0:
                        sp.wait_ge(mod_mul, i * MOD_PER_UNIT[stage] + MQ0[stage])
                    matrix, col = MOD_LOOP[stage]
                    mod_chunk(r, matrix, i * MOD_PER_UNIT[stage] + (col + r))
                if stage[:3] == "moe":
                    n = i + EXPERTS * (stage == "moe1")
                    sp.wait_ge(rt_store, 64 * (1 + (stage == "moe1")))
                    sp.wait_ge(dve_comb, 2 * n + 1 + (stage == "moe1"))
                    sp.dma_start(comb_row, comb_dram[n].partition_broadcast(P)).then_inc(comb_full, 16)

            def cols(stage, name, tiles, start=0):
                for j, c in enumerate(tiles):
                    if j < start:
                        continue
                    tile(T0[stage] + j, io_w[name][:, :, c * 256:(c + 1) * 256], w_in)

            sp.dma_start(pv[:], io["params"]).then_inc(ld_pv, 16)
            sp.dma_start(x[:], io["x_t"].rearrange("(k p) n -> p k n", p=P)).then_inc(ld_x, 16)
            for dst, name in ((ident, "ident"), (ones, "ones"), (ones64, "ones64"), (rot1, "rot1"), (rot2, "rot2")):
                sp.dma_start(dst[:], io[name]).then_inc(ld_const, 16)
            sp.dma_start(nt[:, 0].bitcast(I32), io["positions"][0].partition_broadcast(P)).then_inc(ld_row, 16)
            sp.dma_start(nt[:, 1, 0:256], io["lambda_qk"].partition_broadcast(P)).then_inc(ld_row, 16)
            sp.dma_start(rb[:].rearrange("p l n -> p (l n)"), io["router_b"].partition_broadcast(P)).then_inc(ld_row, 16)
            sp.dma_start(rw[:], io["router_w"][0].rearrange("(k p) n -> p k n", p=P)).then_inc(ld_rw[0], 16)
            q, last = 0, {}
            for b, (matrix, col, n) in enumerate(MOD_FIRST):
                for r in range(n):
                    if r in last:
                        sp.wait_ge(mod_mul, last[r] + 1)
                    mod_chunk(r, matrix, col + r)
                    last[r] = q
                    q += 1
            unit_tiles("ffn1", 0)
            with sp.Fori(1, FFN_UNITS) as i:
                unit_tiles("ffn1", i)

            cols("mixin", "w_mix_in", range(RING))
            sp.wait_ge(arena_free, 1)
            sp.dma_start(bd, io["lru_bd"]).then_inc(ld_mix, 16)
            cols("mixin", "w_mix_in", range(10), RING)
            cols("mixout", "w_mix_out", range(4))

            with sp.Fori(0, FFN_UNITS) as i:
                unit_tiles("ffn2", i)

            cols("evenin", "even_w_in", (2, 0, 1))
            sp.wait_ge(arena_free, 2)
            sp.dma_start(ctxx, io["ctx_t"].rearrange("(k p) n -> p k n", p=P)).then_inc(ld_ctx, 16)
            sp.dma_start(poolw, io["pool_w"].rearrange("g c d -> c g d")).then_inc(ld_even, 16)
            sp.dma_start(ic, io["inv_count"].partition_broadcast(P)).then_inc(ld_even, 16)
            sp.dma_start(rope[:], io["rope2"]).then_inc(ld_rope2, 16)
            cols("evenin", "even_w_in", (2, 0, 1, 3, 4), RING)
            cols("evenout", "even_w_out", range(4))

            with sp.Fori(0, EXPERTS) as i:
                unit_tiles("moe0", i)

            cols("oddin", "odd_w_in", range(RING))
            sp.wait_ge(arena_free, 3)
            sp.dma_start(sgw, io["sg_w_t"]).then_inc(ld_odd, 16)
            sp.dma_start(sgb, io["sg_b"].rearrange("g p -> (g p)").partition_broadcast(P)
                         .rearrange("p (g n) -> p g n", n=P)).then_inc(ld_odd, 16)
            sp.wait_ge(rt_w, 2)
            sp.dma_start(rw[:], io["router_w"][1].rearrange("(k p) n -> p k n", p=P)).then_inc(ld_rw[1], 16)
            cols("oddin", "odd_w_in", range(10), RING)
            cols("oddout", "odd_w_out", range(4))

            with sp.Fori(0, EXPERTS) as i:
                unit_tiles("moe1", i)

            out = io["out"].rearrange("(k p) n -> p k n", p=P)
            for k in range(KC):
                sp.wait_ge(x_done, XDONE["end"] - KC + k + 1)
                sp.dma_start(out[:, k], x[:, k]).then_inc(st_out, 16)
            sp.wait_ge(st_out, 16 * KC)

        @block.gpsimd
        def _(pool):
            def split_lo(s, n):
                pool.wait_ge(weight_hi, n)
                nc.gpsimd.tensor_tensor(w_lo[:, s], w_raw[:, s], w_hi[:, s], ALU.subtract).then_inc(weight_lo, 1)

            with pool.Fori(0, TILES // RING) as i:
                for s in range(RING):
                    split_lo(s, RING * i + (s + 1))
            for t in range(TILES - TILES % RING, TILES):
                split_lo(t % RING, t + 1)

        @block.scalar
        def _(act):
            chain = [0]

            def link(ins):
                chain[0] += 1
                ins.then_inc(act_chain, 1)
                act.wait_ge(act_chain, chain[0])

            def hi(t, i=0):
                if isinstance(i, int) and t + 3 * i >= TILES:
                    return
                s = t % RING
                act.wait_ge(raw_full[s], 16 * i + 16 * (t // RING + 1))
                if not isinstance(i, int) or t + 3 * i >= RING:
                    act.wait_ge(group_done, 12 * i + GROUPS_BEFORE[t - 2])
                nc.scalar.activation(w_hi[:, s], w_raw[:, s], ACT.Copy).then_inc(weight_hi, 1)

            def sum_squares(name, src, n=S, ready=None):
                q = NORM[name][0]
                for k in range(KC):
                    if ready:
                        ready(k)
                    if k >= 2:
                        act.wait_ge(pe_ss, KC * q + k - 1)
                    nc.scalar.activation(nt[:, k % 2, 0:n], src[:, k], ACT.Square).then_inc(act_sq, 1)
                act.wait_ge(pe_ss, KC * q + KC)
                nc.scalar.activation(root[:, 0:n], sum_bank(name)[:, 0:n], ACT.Sqrt, bias=misc[:, 0:1],
                                     scale=1.0 / D).then_inc(act_root, 1)

            def modulated(name, shift, n=S):
                m = NORM[name][1]
                act.wait_ge(dve_cols, m + 1)
                for k in range(KC):
                    t = nt[:, 2 + k % 2, 0:n]
                    act.wait_ge(dve_t, KC * m + k + 1)
                    nc.scalar.activation(t, t, ACT.Identity, bias=mods[:, shift + k:shift + k + 1],
                                         scale=acol[:, KC * m + k:KC * m + k + 1]).then_inc(act_af, 1)
                    act.wait_ge(act_af, KC * m + k + 1)
                    nc.scalar.activation(a_hi[:, k, 0:n], t, ACT.Copy).then_inc(act_ahi, 1)

            def unit(stage, i):
                t, u = T0[stage], i + UNIT0[stage]
                last = isinstance(i, int)
                g = 12 * i + GROUPS_BEFORE[t]
                hi(t + 2, i)
                for c in range(2):
                    act.wait_ge(group_done, g + (c + 1))
                    act.wait_ge(dve_gu, 2 * u + (c + 1))
                    nc.scalar.activation(sg[:, c], G[:, c], ACT.Silu).then_inc(act_silu, 1)
                hi(t + 3, i)
                for c in range(2):
                    act.wait_ge(dve_gu, 2 * u + (PRIME_GU + c + 1))
                    nc.scalar.activation(h_hi[:, c], hid[:, c], ACT.Copy).then_inc(act_hhi, 1)
                hi(t + 4, i)

            def units(stage):
                n, first = UNITS[stage], int(stage == "ffn1")
                if first:
                    unit(stage, 0)
                with act.Fori(first, n - 1) as i:
                    unit(stage, i)
                unit(stage, n - 1)

            def tile_step(t, bank, evacuate):
                hi(t + 2)
                for c in range(2):
                    act.wait_ge(group_done, GROUPS_BEFORE[t] + c + 1)
                    evacuate(c)

            act.wait_ge(ld_pv, 16)
            nc.scalar.activation(cond[:], pv[:, 0:24], ACT.Silu).then_inc(cond_done, 1)
            nc.scalar.activation(misc[:, 62:63], pv[:, 0:1], ACT.Copy).then_inc(act_silu, PRIME_SILU)
            act.wait_ge(rope1_ang, 1)
            nc.scalar.activation(rope[:, 1], rope[:, 1], ACT.Sin).then_inc(rope1_tab, 1)
            act.wait_ge(rope1_ang, 2)
            nc.scalar.activation(rope[:, 0], rope[:, 0], ACT.Sin).then_inc(rope1_tab, 1)
            act.wait_ge(lam_sum, 1)
            nc.scalar.activation(misc[:, 2:4], misc[:, 2:4], ACT.Exp).then_inc(lam_exp, 1)
            act.wait_ge(lam_sum, 2)
            nc.scalar.activation(misc[:, 16:24], misc[:, 16:24], ACT.Exp, scale=-1.0).then_inc(sp_exp, 1)

            act.wait_ge(ld_x, 16)
            act.wait_ge(dve_chain, 1)
            sum_squares("ffn1", x)
            hi(0)
            hi(1)
            modulated("ffn1", MOD_OUT["ada"])
            units("ffn1")

            def added(stage):
                return lambda k: act.wait_ge(down_added, PRIME_ADD + 8 * (UNIT0[stage] + UNITS[stage] - 1) + k + 1)
            sum_squares("ffn1_end", yacc, ready=added("ffn1"))

            sum_squares("mix", x, ready=lambda k: act.wait_ge(x_done, XDONE["mix"] + k + 1 - KC + 0))
            modulated("mix", MOD_OUT["ada"] + 24)
            act.wait_ge(m1_pad, 1)

            def evac_mixin(j):
                def go(c):
                    g = 2 * j + c
                    if g < 8:
                        dst, src = (q1, k1)[g // 4][:, g % 4], G[:, g % 4]
                    elif g < 12:
                        dst = v1[:, 2 * c:2 * c + 2, 256 * (j - 4):256 * (j - 3)]
                        src = G[:, g % 4].rearrange("p (t n) -> p t n", n=256)
                    elif g < 16:
                        dst, src = xr1[:, g - 12, 2:2 + S], G[:, g % 4]
                    else:
                        dst, src = yr1[:, g - 16], G[:, g % 4]
                    nc.scalar.activation(dst, src, ACT.Copy).then_inc(act_z, 1)
                return go
            for j in range(10):
                tile_step(T0["mixin"] + j, 0, evac_mixin(j))
            act.wait_ge(act_z, 20)
            nc.scalar.activation(yr1, yr1, ACT.Gelu_apprx_tanh).then_inc(m1_gelu, 1)
            for c in range(4):
                for d in range(2):
                    for g in range(2):
                        col = COL["b_gate"] + (2 * d + g) * 4 + c
                        act.wait_ge(m1_gate, 4 * c + 2 * d + g + 1)
                        if c:
                            act.wait_ge(m1_rec, c)
                        nc.scalar.activation(nt[:, 2 * g + d], G[:, 2 * d + g], ACT.Sigmoid,
                                             bias=pv[:, col:col + 1]).then_inc(m1_sig, 1)
                for d in range(2):
                    a = (root, rinv)[d]
                    sp8 = misc[:, 32 + 4 * d + c:33 + 4 * d + c]
                    act.wait_ge(m1_sig, 4 * c + 4)
                    nc.scalar.activation(a[:], nt[:, d], ACT.Exp, scale=misc[:, 24 + 4 * d + c:25 + 4 * d + c]).then_inc(m1_at, 1)
                    act.wait_ge(m1_at, 4 * c + 2 * d + 1)
                    nc.scalar.activation(nt[:, d], nt[:, d], ACT.Tanh, scale=sp8).then_inc(m1_at, 1)
                for d in range(2):
                    act.wait_ge(m1_m, 2 * c + d + 1)
                    nc.scalar.activation(nt[:, d], nt[:, d], ACT.Sqrt).then_inc(m1_sqrt, 1)

            def exps(n):
                act.wait_ge(m1_nm, n + 1)
                if n >= 2:
                    act.wait_ge(m1_w, n - 1)
                for m in range(2):
                    nc.scalar.activation(pexp1[:, 2 * (n % 2) + m], G[:, 2 * (n % 2) + m], ACT.Exp,
                                         bias=stat[:, 1, 2 * n + m:2 * n + m + 1], scale=0.125,
                                         accum_out=stat[:, 2, 2 * n + m:2 * n + m + 1]).then_inc(m1_exp, 1)

            def weights_t(n):
                h, i = n // 4, n % 4
                act.wait_ge(m1_tr, n + 1)
                if h and i == 0:
                    act.wait_ge(m1_pv, h)
                nc.scalar.activation(wt1[:, :, i * P:(i + 1) * P], Dn[:, n % 2].rearrange("p (k q) -> p k q", q=P),
                                     ACT.Copy).then_inc(m1_wt, 1)

            def head_out(h):
                act.wait_ge(m1_pv, h + 1)
                nc.scalar.activation(q1[:, h], Dn[:, M], ACT.Copy).then_inc(m1_o, 1)
            for n in range(17):
                if n < 16:
                    exps(n)
                if n >= 5 and n % 4 == 1:
                    head_out(n // 4 - 1)
                if n >= 1:
                    weights_t(n - 1)
            head_out(3)
            act.wait_ge(m1_o, 4)
            for h in range(4):
                nc.scalar.activation(nt[:, h], q1[:, h], ACT.Square).then_inc(m1_ssq, 1)
            for h in range(4):
                act.wait_ge(m1_ssp, h + 1)
                nc.scalar.activation(pexp1[:, h], G[:, h], ACT.Sqrt, bias=misc[:, 0:1],
                                     scale=1.0 / P).then_inc(m1_srt, 1)
            for j in range(4):
                def evac_y(c, j=j):
                    nc.scalar.activation(yacc[:, 2 * j + c], G[:, (2 * j + c) % 4], ACT.Copy).then_inc(act_z, 1)
                tile_step(T0["mixout"] + j, 0, evac_y)
            sum_squares("mix_end", yacc, ready=lambda k: act.wait_ge(act_z, Z0["mixout"] + k + 1))

            sum_squares("ffn2", x, ready=lambda k: act.wait_ge(x_done, XDONE["ffn2"] - KC + k + 1))
            modulated("ffn2", MOD_OUT["ada"] + 48)
            units("ffn2")
            sum_squares("ffn2_end", yacc, ready=added("ffn2"))

            act.wait_ge(ld_ctx, 16)
            sum_squares("ctx", ctxx, CTX)
            modulated("ctx", MOD_OUT["ctx"], CTX)
            sum_squares("even", x, ready=lambda k: act.wait_ge(x_done, XDONE["even"] - KC + k + 1))
            t = T0["evenin"]
            g = GROUPS_BEFORE[t]
            hi(t + 2)
            act.wait_ge(m2_pad, 1)
            act.wait_ge(group_done, g + 1)
            nc.scalar.activation(kall[:, 0:CTX], G[:, 0, 0:CTX], ACT.Copy).then_inc(act_z, 1)
            act.wait_ge(group_done, g + 2)
            nc.scalar.activation(vz[:, 0:4, 64:128], G[:, 1, 0:CTX].rearrange("p (t n) -> p t n", n=64),
                                 ACT.Copy).then_inc(act_z, 1)
            modulated("even", MOD_OUT["mod0"])
            act.wait_ge(group_done, g + 3)
            nc.scalar.activation(kall[:, CTX:SK], G[:, 2], ACT.Copy).then_inc(act_z, 1)
            act.wait_ge(group_done, g + 4)
            nc.scalar.activation(vz[:, 4:12, 64:128], G[:, 3].rearrange("p (t n) -> p t n", n=64),
                                 ACT.Copy).then_inc(act_z, 1)

            def head_norm(idx, src, n, ready):
                act.wait_ge(act_z, ready)
                if idx:
                    act.wait_ge(m2_kn, idx)
                nc.scalar.activation(nt[:, 0, 0:n], src, ACT.Square).then_inc(m2_ssq, 1)
                act.wait_ge(m2_ssp, idx + 1)
                nc.scalar.activation(root[:, 0:n], Dn[:, 0, 0:n], ACT.Sqrt, bias=misc[:, 0:1],
                                     scale=1.0 / 64).then_inc(m2_srt, 1)
            head_norm(0, kall[:, 0:CTX], CTX, Z0["evenin"] + 1)
            head_norm(1, kall[:, CTX:SK], S, Z0["evenin"] + 3)
            for j in range(4):
                def evac(c, j=j):
                    g = 2 * j + c
                    dst = q2[:, g] if g < 4 else p2[:, g - 4, 8:8 + S]
                    nc.scalar.activation(dst, G[:, g % 4], ACT.Copy).then_inc(act_z, 1)
                tile_step(t + 1 + j, 0, evac)
                if j in (1, 2):
                    for m in (2 * j - 2, 2 * j - 1):
                        head_norm(2 + m, q2[:, m], S, Z0["evenin"] + 5 + m)
            for g in range(4):
                act.wait_ge(m2_pw, g + 1)
                if g:
                    act.wait_ge(m2_pool, g)
                col = COL["pool_scale"] + g
                nc.scalar.activation(root[:], G[:, g], ACT.Copy, scale=pv[:, col:col + 1]).then_inc(m2_ps, 1)

            def exps2(n):
                act.wait_ge(m2_nm, n + 1)
                if n >= 2:
                    act.wait_ge(m2_tr, n - 1)
                b = 2 * (n % 2)
                nc.scalar.activation(pexp2[:, n % 2], G[:, b:b + 2].rearrange("p a b -> p (a b)")[:, 0:SK], ACT.Exp,
                                     bias=stat[:, 1, n:n + 1], scale=0.125,
                                     accum_out=stat[:, 2, n:n + 1]).then_inc(m2_exp, 1)

            def weights_t2(n):
                h, i = n // 4, n % 4
                act.wait_ge(m2_tr, n + 1)
                if h and i == 0:
                    act.wait_ge(m2_pv, h)
                nc.scalar.activation(wt2[:, :, i * P:(i + 1) * P],
                                     Dn[:, 0:2].rearrange("p a b -> p (a b)")[:, 0:SK].rearrange("p (k q) -> p k q", q=P),
                                     ACT.Copy).then_inc(m2_wt, 1)

            def heads_out(c):
                act.wait_ge(m2_pv, 2 * c + 2)
                nc.scalar.activation(a_hi[:, c], Dn[:, 2 + c % 2], ACT.Copy).then_inc(m2_ohi, 1)
            for n in range(33):
                if n < 32:
                    exps2(n)
                if n >= 9 and n % 8 == 1:
                    heads_out(n // 8 - 1)
                if n >= 1:
                    weights_t2(n - 1)
            heads_out(3)
            for j in range(4):
                hi(T0["evenout"] + j + 2)

            for l in range(2):
                stage = f"moe{l}"
                sum_squares(stage, x, ready=lambda k: act.wait_ge(x_done, XDONE[stage] - KC + k + 1))
                modulated(stage, MOD_OUT[f"mod{l}"] + 24)
                act.wait_ge(ld_rw[l], 16)
                nc.scalar.activation(rw_hi[:], rw[:], ACT.Copy).then_inc(rt_w, 1)
                act.wait_ge(rt_d1, l + 1)
                nc.scalar.activation(rt[:, 96:112], rt[:, 96:112], ACT.Exp).then_inc(rt_exp1, 1)
                act.wait_ge(rt_d2, l + 1)
                nc.scalar.activation(rt[:, 116:120], rt[:, 116:120], ACT.Exp).then_inc(rt_exp2, 1)
                act.wait_ge(rt_comb, l + 1)
                for b in range(4):
                    act.dma_start(comb_dram[l * EXPERTS:(l + 1) * EXPERTS, :]
                                  .rearrange("e (t b j) -> b e t j", b=4, j=32)[b],
                                  comb_t[32 * b:32 * b + EXPERTS]).then_inc(rt_store, 16)
                units(stage)
                if l == 1:
                    break
                sum_squares("odd", x, ready=lambda k: act.wait_ge(x_done, XDONE["odd"] - KC + k + 1))
                modulated("odd", MOD_OUT["mod1"])
                act.wait_ge(m3_pad, 1)

                def evac_odd(j):
                    def go(c):
                        g = 2 * j + c
                        src = G[:, g % 4]
                        if g < 4:
                            dst = u3[:, g]
                        elif g < 8:
                            dst = v3[:, 2 * c:2 * c + 2, 256 * (j - 2):256 * (j - 1)]
                            src = src.rearrange("p (t n) -> p t n", n=256)
                        elif g < 12:
                            dst = z3[:, g - 8, 1:1 + S]
                        else:
                            dst = (bg3, cg3)[(g - 12) // 4][:, g % 4]
                        nc.scalar.activation(dst, src, ACT.Copy).then_inc(act_z, 1)
                    return go
                for j in range(10):
                    tile_step(T0["oddin"] + j, 0, evac_odd(j))
                    if j == 5:
                        act.wait_ge(m3_ss, 4)
                        nc.scalar.activation(stat[:, 1, 0:16], stat[:, 0, 0:16], ACT.Sqrt, bias=misc[:, 0:1],
                                             scale=1.0 / P).then_inc(m3_srt, 1)
                for j in range(4):
                    hi(T0["oddout"] + j + 2)

        @block.vector
        def _(dve):
            V = nc.vector
            chain = [0]

            def link(ins):
                chain[0] += 1
                ins.then_inc(dve_chain, 1)
                dve.wait_ge(dve_chain, chain[0])

            def mod_batch(matrix, n, batch, q, fills):
                c = MOD_COND[matrix]
                for r in range(n):
                    dve.wait_ge(mod_full[r], fills(r))
                    dve.wait_ge(mod_red, q + r) if r or not isinstance(q, int) or q else None
                    V.tensor_tensor(prod, mod_raw[:, r], cond[:, c:c + KC].unsqueeze(2).to_broadcast([P, KC, P]),
                                    ALU.mult).then_inc(mod_mul, 1)
                    dve.wait_ge(mod_mul, q + (r + 1))
                    if r == 0 and not (isinstance(batch, int) and batch == 0):
                        dve.wait_ge(mod_sum, batch)
                    V.tensor_reduce(red[:, r], prod.rearrange("p k n -> p n k"), AX.X, ALU.add).then_inc(mod_red, 1)

            def mod_bias(matrix, n, batch, col):
                dve.wait_ge(mod_sum, batch + 1)
                V.tensor_tensor(mods[:, bass.ds(col + MOD_OUT[matrix], n)], Dn[:, M, 0:n],
                                pv[:, bass.ds(col + MOD_BIAS[matrix], n)], ALU.add).then_inc(mod_out, 1)

            def norm_inverse(name, n=S):
                q = NORM[name][0]
                dve.wait_ge(act_root, q + 1)
                V.reciprocal(rinv[:, 0:n], root[:, 0:n]).then_inc(dve_rinv, 1)
                dve.wait_ge(dve_rinv, q + 1)

            def modulated(name, src, scale_col, gain_col, n=S):
                m = NORM[name][1]
                V.scalar_tensor_tensor(acol[:, KC * m:KC * m + KC], mods[:, scale_col:scale_col + KC], 1.0,
                                       pv[:, gain_col:gain_col + KC], ALU.add, ALU.mult).then_inc(dve_cols, 1)
                norm_inverse(name, n)

                def low(k):
                    dve.wait_ge(act_ahi, KC * m + k + 1)
                    V.tensor_tensor(a_lo[:, k, 0:n], nt[:, 2 + k % 2, 0:n], a_hi[:, k, 0:n],
                                    ALU.subtract).then_inc(dve_alo, 1)
                for k in range(KC):
                    if k >= 2:
                        dve.wait_ge(dve_alo, KC * m + k - 1)
                    V.tensor_tensor(nt[:, 2 + k % 2, 0:n], src[:, k], rinv[:, 0:n], ALU.mult).then_inc(dve_t, 1)
                    if k:
                        low(k - 1)
                low(KC - 1)

            def end_norm(name, s, gate_col, gain_col, weight):
                link(V.scalar_tensor_tensor(gcol[:, KC * s:KC * s + KC], mods[:, gate_col:gate_col + KC], weight,
                                            pv[:, gain_col:gain_col + KC], ALU.mult, ALU.mult))
                norm_inverse(name)
                V.tensor_tensor(yacc, yacc, rinv[:].unsqueeze(1).to_broadcast([P, KC, S]), ALU.mult).then_inc(dve_yn, 1)
                dve.wait_ge(dve_yn, s + 1)
                for k in range(KC):
                    V.scalar_tensor_tensor(x[:, k], yacc[:, k], gcol[:, KC * s + k:KC * s + k + 1], x[:, k],
                                           ALU.mult, ALU.add).then_inc(x_done, 1)

            def unit(stage, i):
                t, u = T0[stage], i + UNIT0[stage]
                g = 12 * i + GROUPS_BEFORE[t]
                n = MOD_PER_UNIT[stage]
                moe = stage[:3] == "moe"
                if n:
                    matrix, col = MOD_LOOP[stage]
                    batch, q = i + MB0[stage], i * n + MQ0[stage]
                    mod_batch(matrix, n, batch, q, lambda r: 16 * i + 16 * (mod_fills(stage, r) + 1))
                if moe:
                    e = i + EXPERTS * (stage == "moe1")
                    dve.wait_ge(comb_full, 16 * e + 16)
                for c in range(2):
                    if moe:
                        dve.wait_ge(act_silu, 2 * u + (PRIME_SILU + c + 1))
                        V.tensor_tensor(sg[:, c], sg[:, c], comb_row, ALU.mult).then_inc(dve_comb, 1)
                for c in range(2):
                    if moe:
                        dve.wait_ge(dve_comb, 2 * e + (c + 2 + (stage == "moe1")))
                    else:
                        dve.wait_ge(act_silu, 2 * u + (PRIME_SILU + c + 1))
                    dve.wait_ge(group_done, g + (2 + c + 1))
                    dve.wait_ge(dve_hlo, 2 * u + 1) if c == 0 else None
                    V.tensor_tensor(hid[:, c], G[:, 2 + c], sg[:, c], ALU.mult).then_inc(dve_gu, 1)
                for c in range(2):
                    dve.wait_ge(act_hhi, 2 * u + (c + 1))
                    V.tensor_tensor(h_lo[:, c], hid[:, c], h_hi[:, c], ALU.subtract).then_inc(dve_hlo, 1)
                for m in range(KC):
                    dve.wait_ge(group_done, g + (4 + m + 1))
                    dve.wait_ge(down_added, 8 * u + (m + 1))
                    V.tensor_tensor(yacc[:, m], yacc[:, m], Dn[:, m % 3], ALU.add).then_inc(down_added, 1)
                if n:
                    mod_bias(matrix, n, batch, i * n + col)

            def units(stage):
                with dve.Fori(0, UNITS[stage]) as i:
                    unit(stage, i)
                dve.wait_ge(down_added, PRIME_ADD + 8 * (UNIT0[stage] + UNITS[stage]))

            def split(src, k):
                link(V.tensor_copy(a_hi[:, k], src))
                return V.tensor_tensor(a_lo[:, k], src, a_hi[:, k], ALU.subtract)

            link(V.memset(misc[:, 0:1], EPS))
            V.memset(misc[:, 60:61], 0.0).then_inc(dve_gu, PRIME_GU)
            V.memset(misc[:, 61:62], 0.0).then_inc(down_added, PRIME_ADD)
            V.memset(misc[:, 63:64], 0.0).then_inc(dve_hlo, 1)
            V.memset(misc[:, 59:60], 0.0).then_inc(dve_comb, 1)
            dve.wait_ge(ld_pv, 16)
            dve.wait_ge(ld_row, 48)
            link(V.tensor_tensor(nt[:, 2, 0:128], nt[:, 1, 0:128], nt[:, 1, 128:256], ALU.mult))
            V.tensor_reduce(misc[:, 2:4], nt[:, 2, 0:128].rearrange("p (m d) -> p m d", m=2), AX.X,
                            ALU.add).then_inc(lam_sum, 1)
            link(V.tensor_copy(nt[:, 3], nt[:, 0].bitcast(I32)))
            fr = COL["inv_freq"]
            link(V.tensor_scalar(nt[:, 3], nt[:, 3], pv[:, fr:fr + 1], None, ALU.mult))
            C1 = 6.28125
            C2 = 0.0019350051879882812
            C3 = 6.283185307179586 - C1 - C2
            MAGIC = 12582912.0
            PI = 3.1415925
            link(V.tensor_scalar(nt[:, 2], nt[:, 3], 0.15915494309189535, MAGIC, ALU.mult, ALU.add))
            link(V.tensor_scalar(nt[:, 2], nt[:, 2], MAGIC, None, ALU.subtract))
            for part in (C1, C2, C3):
                link(V.scalar_tensor_tensor(nt[:, 3], nt[:, 2], -part, nt[:, 3], ALU.mult, ALU.add))
            V.tensor_scalar(rope[:, 1], nt[:, 3], PI, -PI, ALU.min, ALU.max).then_inc(rope1_ang, 1)
            link(V.tensor_scalar(nt[:, 3], nt[:, 3], 1.5707963267948966, None, ALU.add))
            link(V.tensor_scalar(nt[:, 2], nt[:, 3], 3.141592653589793, 6.283185307179586, ALU.is_gt, ALU.mult))
            link(V.tensor_tensor(nt[:, 3], nt[:, 3], nt[:, 2], ALU.subtract))
            V.tensor_scalar(rope[:, 0], nt[:, 3], PI, -PI, ALU.min, ALU.max).then_inc(rope1_ang, 1)
            la = COL["lam"]
            link(V.tensor_scalar(misc[:, 40:48], pv[:, la:la + 8], -1.0, None, ALU.mult))
            V.tensor_tensor(misc[:, 16:24], pv[:, la:la + 8], misc[:, 40:48], ALU.max).then_inc(lam_sum, 1)
            link(V.tensor_scalar(misc[:, 40:48], misc[:, 40:48], 0.0, None, ALU.max))
            dve.wait_ge(sp_exp, 1)
            y, z, z2, s = misc[:, 16:24], misc[:, 24:32], misc[:, 32:40], misc[:, 48:56]
            link(V.tensor_scalar(z, y, 2.0, None, ALU.add))
            link(V.reciprocal(z, z))
            link(V.tensor_tensor(z, z, y, ALU.mult))
            link(V.tensor_tensor(z2, z, z, ALU.mult))
            link(V.tensor_scalar(s, z2, 1.0 / 19, None, ALU.mult))
            for n in range(8, 0, -1):
                link(V.scalar_tensor_tensor(s, s, 1.0 / (2 * n + 1), z2, ALU.add, ALU.mult))
            link(V.scalar_tensor_tensor(s, s, 1.0, z, ALU.add, ALU.mult))
            link(V.scalar_tensor_tensor(s, s, 2.0, misc[:, 40:48], ALU.mult, ALU.add))
            link(V.tensor_scalar(misc[:, 24:32], s, -8.0, None, ALU.mult))
            link(V.tensor_scalar(misc[:, 32:40], s, 8.0, None, ALU.mult))
            dve.wait_ge(lam_exp, 1)
            link(V.tensor_scalar(misc[:, 4:5], misc[:, 3:4], LAMBDA_INIT, None, ALU.subtract))
            link(V.tensor_tensor(misc[:, 4:5], misc[:, 4:5], misc[:, 2:3], ALU.subtract))
            link(V.tensor_scalar(misc[:, 5:6], pv[:, COL["subln"]:COL["subln"] + 1], 1.0 - LAMBDA_INIT, None, ALU.mult))
            dve.wait_ge(cond_done, 1)
            q, filled = 0, [0] * MOD_SLOTS
            for b, (matrix, col, n) in enumerate(MOD_FIRST):
                def fills(r):
                    filled[r] += 1
                    return 16 * filled[r]
                mod_batch(matrix, n, b, q, fills)
                mod_bias(matrix, n, b, col)
                q += n
            dve.wait_ge(mod_out, len(MOD_FIRST))

            NG = COL["norm_g"]
            V.memset(yacc, 0.0).then_inc(yacc_zero, 1)
            dve.wait_ge(yacc_zero, 1)
            modulated("ffn1", x, 8, NG)
            units("ffn1")
            dve.wait_ge(mod_out, MB0["ffn2"])
            end_norm("ffn1_end", 0, 16, NG + 8, 0.5)
            dve.wait_ge(x_done, XDONE["mix"])

            V.memset(misc[:, 58:59], 0.0).then_inc(arena_free, 1)
            link(V.memset(xr1[:, :, 0:2], 0.0))
            V.memset(xr1[:, :, 2 + S:XRW], 0.0).then_inc(m1_pad, 1)
            modulated("mix", x, 24 + 8, NG + 16)
            dve.wait_ge(act_z, 20)
            dve.wait_ge(m1_pad, 1)
            for c in range(4):
                cw, cb = COL["conv_w"] + c, COL["conv_b"] + c
                if c:
                    dve.wait_ge(m1_gate, 4 * c)
                    dve.wait_ge(m1_rec, c)
                link(V.tensor_scalar(e0, xr1[:, c, 0:S], pv[:, cw:cw + 1], pv[:, cb:cb + 1], ALU.mult, ALU.add))
                for tap in range(1, 4):
                    ins = V.scalar_tensor_tensor(e0, xr1[:, c, tap:tap + S], pv[:, cw + 4 * tap:cw + 4 * tap + 1], e0,
                                                 ALU.mult, ALU.add)
                    if tap < 3:
                        link(ins)
                ins.then_inc(m1_xc, 1)
                dve.wait_ge(m1_xc, c + 1)
                for d in range(2):
                    a = (root, rinv)[d]
                    dve.wait_ge(m1_at, 4 * c + 2 * d + 2)
                    link(V.tensor_tensor(e1, a[:], a[:], ALU.mult))
                    link(V.scalar_tensor_tensor(nt[:, d], e1, 1.0, nt[:, d], ALU.add, ALU.mult))
                    V.tensor_scalar(nt[:, d], nt[:, d], 1e-30, None, ALU.max).then_inc(m1_m, 1)
                for d in range(2):
                    a = (root, rinv)[d]
                    link(V.tensor_tensor(nt[:, 2 + d], nt[:, 2 + d], e0, ALU.mult))
                    dve.wait_ge(m1_sqrt, 2 * c + d + 1)
                    link(V.tensor_tensor(nt[:, d], nt[:, d], nt[:, 2 + d], ALU.mult))
                    if d == 0:
                        link(V.tensor_tensor_scan(nt[:, 2], a[:], nt[:, 0], 0.0, ALU.mult, ALU.add))
                    else:
                        link(V.tensor_tensor_scan(nt[:, 3, ::-1], a[:, ::-1], nt[:, 1, ::-1], 0.0, ALU.mult, ALU.add))
                link(V.tensor_tensor(nt[:, 2], nt[:, 2], nt[:, 3], ALU.add))
                dve.wait_ge(m1_gelu, 1)
                link(V.tensor_tensor(e1, nt[:, 2], yr1[:, c], ALU.mult))
                split(e1, 4 + c).then_inc(m1_rec, 1)
            dve.wait_ge(m1_rec, 4)

            def rotate(z, src, tmp, n, ready, value, done, cols=slice(0, S)):
                dve.wait_ge(ready, value)
                link(V.tensor_tensor(tmp, src, rope[:, 1, cols], ALU.mult))
                link(V.tensor_tensor(z, z, rope[:, 0, cols], ALU.mult))
                V.tensor_tensor(z, z, tmp, ALU.add).then_inc(done, 1)
            dve.wait_ge(rope1_tab, 2)
            for idx in range(8):
                if idx >= 4:
                    dve.wait_ge(m1_rope, idx - 3)
                rotate((q1, k1)[idx // 4][:, idx % 4], G[:, idx % 4], nt[:, idx % 4], S, m1_rot, idx + 1, m1_rope)

            def maxima(n):
                dve.wait_ge(m1_qk, 2 * n + 2)
                b = 2 * (n % 2)
                link(V.tensor_reduce(stat[:, 0, 2 * n:2 * n + 2], G[:, b:b + 2], AX.X, ALU.max))
                V.tensor_scalar(stat[:, 1, 2 * n:2 * n + 2], stat[:, 0, 2 * n:2 * n + 2], -0.125, None,
                                ALU.mult).then_inc(m1_nm, 1)

            def mix_weights(n):
                dve.wait_ge(m1_exp, 2 * n + 2)
                c, b = 2 * n, 2 * (n % 2)
                link(V.reciprocal(stat[:, 3, c:c + 2], stat[:, 2, c:c + 2]))
                link(V.tensor_tensor(stat[:, 4, c:c + 1], stat[:, 3, c + 1:c + 2], misc[:, 4:5], ALU.mult))
                if n >= 2:
                    dve.wait_ge(m1_tr, n - 1)
                w = wsm1[:, n % 2]
                link(V.tensor_scalar(w, pexp1[:, b], stat[:, 3, c:c + 1], None, ALU.mult))
                V.scalar_tensor_tensor(w, pexp1[:, b + 1], stat[:, 4, c:c + 1], w, ALU.mult, ALU.add).then_inc(m1_w, 1)
            for n in range(17):
                if n < 16:
                    maxima(n)
                if n:
                    mix_weights(n - 1)
            for h in range(4):
                dve.wait_ge(m1_srt, h + 1)
                link(V.reciprocal(pexp1[:, h], pexp1[:, h]))
                link(V.tensor_tensor(q1[:, h], q1[:, h], pexp1[:, h], ALU.mult))
                link(V.tensor_scalar(q1[:, h], q1[:, h], misc[:, 5:6], None, ALU.mult))
                split(q1[:, h], h).then_inc(m1_sub, 1)
            end_norm("mix_end", 1, 24 + 16, NG + 24, 1.0)
            dve.wait_ge(x_done, XDONE["ffn2"])

            V.memset(yacc, 0.0).then_inc(yacc_zero, 1)
            dve.wait_ge(yacc_zero, 2)
            V.memset(misc[:, 58:59], 0.0).then_inc(arena_back, 1)
            modulated("ffn2", x, 48 + 8, NG + 32)
            units("ffn2")
            dve.wait_ge(mod_out, MB0["moe0"])
            end_norm("ffn2_end", 2, 48 + 16, NG + 40, 0.5)
            dve.wait_ge(x_done, XDONE["even"])

            V.memset(misc[:, 58:59], 0.0).then_inc(arena_free, 1)
            link(V.memset(p2, 0.0))
            V.memset(vz, 0.0).then_inc(m2_pad, 1)
            N1 = COL["norm1"]
            dve.wait_ge(ld_ctx, 16)
            modulated("ctx", ctxx, MOD_OUT["ctx"] + 8, N1, CTX)
            dve.wait_ge(group_done, GROUPS_BEFORE[T0["evenin"]] + 2)
            modulated("even", x, MOD_OUT["mod0"] + 8, N1)
            dve.wait_ge(ld_rope2, 16)

            def head_norm(idx, z, n, gain, turned):
                dve.wait_ge(m2_srt, idx + 1)
                link(V.reciprocal(rinv[:, 0:n], root[:, 0:n]))
                link(V.tensor_tensor(z, z, rinv[:, 0:n], ALU.mult))
                V.tensor_scalar(z, z, pv[:, gain:gain + 1], None, ALU.mult).then_inc(m2_kn, 1)
                dve.wait_ge(m2_kn, idx + 1)
                if turned:
                    rotate(z, Dn[:, 1], nt[:, 1], n, m2_rot, idx, m2_rope)
                    dve.wait_ge(m2_rope, idx)
            head_norm(0, kall[:, 0:CTX], CTX, COL["k_gain"], False)
            head_norm(1, kall[:, CTX:SK], S, COL["k_gain"], True)
            link(V.tensor_copy(kswap[0:64], kall[64:128]))
            V.tensor_copy(kswap[64:128], kall[0:64]).then_inc(m2_swap, 1)
            for m in range(4):
                head_norm(2 + m, q2[:, m], S, COL["q_gain"], True)
            dve.wait_ge(act_z, Z0["evenin"] + 12)
            dve.wait_ge(ld_even, 32)
            flat = nt[:].rearrange("p a b -> p (a b)")
            for g in range(4):
                src, width = p2[:, g], PW
                for lvl in range(g + 1):
                    step = 1 << lvl
                    dst = flat[:, 528 * (lvl % 2):528 * (lvl % 2) + 528]
                    width -= step
                    link(V.tensor_tensor(dst[:, 0:width], src[:, 0:width], src[:, step:step + width], ALU.add))
                    src = dst
                half = 1 << g
                s, d = src[:, 8 - half:8 - half + S], flat[:, 1056 + 0:1056 + S]
                if g:
                    dve.wait_ge(m2_pw, g)
                link(V.tensor_tensor(d, s, ic[:, g], ALU.mult))
                V.tensor_tensor(d, d, p2[:, g, 8:8 + S], ALU.subtract).then_inc(m2_d, 1)
                dve.wait_ge(m2_d, g + 1)
                dve.wait_ge(m2_ps, g + 1)
                split(root[:], 4 + g).then_inc(m2_pool, 1)
            dve.wait_ge(m2_pool, 4)

            def maxima2(n):
                dve.wait_ge(m2_qk, n + 1)
                b = 2 * (n % 2)
                link(V.tensor_reduce(stat[:, 0, n:n + 1], G[:, b:b + 2].rearrange("p a b -> p (a b)")[:, 0:SK], AX.X, ALU.max))
                V.tensor_scalar(stat[:, 1, n:n + 1], stat[:, 0, n:n + 1], -0.125, None, ALU.mult).then_inc(m2_nm, 1)

            def scale2(n):
                dve.wait_ge(m2_exp, n + 1)
                link(V.reciprocal(stat[:, 3, n:n + 1], stat[:, 2, n:n + 1]))
                V.tensor_scalar(pexp2[:, n % 2], pexp2[:, n % 2], stat[:, 3, n:n + 1], None, ALU.mult).then_inc(m2_w, 1)

            def heads_low(c):
                dve.wait_ge(m2_ohi, c + 1)
                V.tensor_tensor(a_lo[:, c], Dn[:, 2 + c % 2], a_hi[:, c], ALU.subtract).then_inc(m2_olo, 1)
            for n in range(33):
                if n < 32:
                    maxima2(n)
                if n:
                    scale2(n - 1)
                if n >= 11 and n % 8 == 3:
                    heads_low(n // 8 - 1)
            heads_low(3)

            def project_residual(stage, gate_col):
                for k in range(KC):
                    dve.wait_ge(group_done, GROUPS_BEFORE[T0[stage]] + k + 1)
                    V.scalar_tensor_tensor(x[:, k], G[:, k % 4], mods[:, gate_col + k:gate_col + k + 1], x[:, k],
                                           ALU.mult, ALU.add).then_inc(x_done, 1)
            project_residual("evenout", MOD_OUT["mod0"] + 16)

            def first_of(oh, eq, tmp):
                link(V.tensor_scalar(tmp, eq[:, :, 0:1], -1.0, 1.0, ALU.mult, ALU.add))
                link(V.tensor_copy(oh[:, :, 0:1], eq[:, :, 0:1]))
                for j in range(1, 4):
                    link(V.tensor_tensor(oh[:, :, j:j + 1], eq[:, :, j:j + 1], tmp, ALU.mult))
                    if j < 3:
                        link(V.tensor_tensor(tmp, tmp, oh[:, :, j:j + 1], ALU.subtract))

            def router(l):
                def r3(at, n):
                    return rt[:, at:at + 4 * n].rearrange("p (t n) -> p t n", n=n)
                logit, gsh, gm = r3(0, 20), r3(96, 4), r3(112, 1)
                e2, gp, tmp = r3(116, 1), r3(120, 1), r3(124, 1)
                eq, gh, oh1, oh2, esel, m1, m2, msk = (r3(128, 4), r3(144, 4), r3(160, 4), r3(176, 4), r3(192, 4),
                                                       r3(208, 1), r3(212, 1), r3(216, 4))
                wide = rt[:, 232:296].rearrange("p (t g j) -> p t g j", g=4, j=4)

                def b(v, n=4):
                    return v.to_broadcast([P, TT, n])
                dve.wait_ge(ld_row, 48)
                dve.wait_ge(rt_logit, l + 1)
                link(V.tensor_tensor(logit, Dn[:, M, 0:80].rearrange("p (t n) -> p t n", n=20),
                                     rb[:, l].unsqueeze(1).to_broadcast([P, TT, 20]), ALU.add))
                lg = logit[:, :, 0:4]
                link(V.tensor_reduce(gm, lg, AX.X, ALU.max))
                V.tensor_tensor(gsh, lg, b(gm), ALU.subtract).then_inc(rt_d1, 1)
                link(V.tensor_tensor(eq, lg, b(gm), ALU.is_equal))
                first_of(gh, eq, tmp)
                le = logit[:, :, 4:20].rearrange("p t (g j) -> p t g j", j=4)
                link(V.tensor_tensor(wide, le, gh.unsqueeze(3).to_broadcast([P, TT, 4, 4]), ALU.mult))
                link(V.tensor_reduce(esel, wide.rearrange("p t g j -> p t j g"), AX.X, ALU.add))
                link(V.tensor_reduce(m1, esel, AX.X, ALU.max))
                link(V.tensor_tensor(eq, esel, b(m1), ALU.is_equal))
                first_of(oh1, eq, tmp)
                link(V.scalar_tensor_tensor(msk, oh1, -1e30, esel, ALU.mult, ALU.add))
                link(V.tensor_reduce(m2, msk, AX.X, ALU.max))
                link(V.tensor_tensor(eq, msk, b(m2), ALU.is_equal))
                first_of(oh2, eq, tmp)
                V.tensor_tensor(e2, m2, m1, ALU.subtract).then_inc(rt_d2, 1)
                dve.wait_ge(rt_exp1, l + 1)
                link(V.tensor_reduce(gp, gsh, AX.X, ALU.add))
                dve.wait_ge(rt_exp2, l + 1)
                link(V.scalar_tensor_tensor(tmp, e2, 1.0, gp, ALU.add, ALU.mult))
                link(V.reciprocal(tmp, tmp))
                link(V.tensor_tensor(oh1, oh1, b(tmp), ALU.mult))
                link(V.tensor_tensor(tmp, tmp, e2, ALU.mult))
                link(V.tensor_tensor(oh2, oh2, b(tmp), ALU.mult))
                link(V.tensor_tensor(oh1, oh1, oh2, ALU.add))
                link(V.memset(comb_pad, 0.0))
                link(V.tensor_tensor(comb_pad[:, :, 0:16].rearrange("p t (g j) -> p t g j", j=4),
                                     gh.unsqueeze(3).to_broadcast([P, TT, 4, 4]),
                                     oh1.unsqueeze(2).to_broadcast([P, TT, 4, 4]), ALU.mult))
                V.transpose(comb_t.rearrange("p t j -> p (t j)"), comb_pad.rearrange("p t j -> p (t j)")).then_inc(rt_comb, 1)
                dve.wait_ge(rt_comb, l + 1)
                V.memset(misc[:, 57:58], 0.0).then_inc(dve_comb, 1) if l == 1 else None

            N2 = COL["norm2"]
            for l in range(2):
                stage = f"moe{l}"
                dve.wait_ge(x_done, XDONE[stage])
                V.memset(yacc, 0.0).then_inc(yacc_zero, 1)
                dve.wait_ge(yacc_zero, 3 + l)
                if l == 0:
                    V.memset(misc[:, 58:59], 0.0).then_inc(arena_back, 1)
                modulated(stage, x, MOD_OUT[f"mod{l}"] + 32, N2 + 8 * l)
                dve.wait_ge(rt_w, 2 * l + 1)
                V.tensor_tensor(rw_lo[:], rw[:], rw_hi[:], ALU.subtract).then_inc(rt_w, 1)
                router(l)
                units(stage)
                for k in range(KC):
                    g = MOD_OUT[f"mod{l}"] + 40 + k
                    V.scalar_tensor_tensor(x[:, k], yacc[:, k], mods[:, g:g + 1], x[:, k],
                                           ALU.mult, ALU.add).then_inc(x_done, 1)
                if l == 1:
                    break
                dve.wait_ge(x_done, XDONE["odd"])
                dve.wait_ge(mod_out, MB0["moe0"] + UNITS["moe0"])
                V.memset(misc[:, 58:59], 0.0).then_inc(arena_free, 1)
                link(V.memset(z3[:, :, 0:1], 0.0))
                V.memset(z3[:, :, 1 + S:ZW], 0.0).then_inc(m3_pad, 1)
                modulated("odd", x, MOD_OUT["mod1"] + 8, N1 + 8)
                dve.wait_ge(act_z, Z0["oddin"] + 8)
                for t in range(TT):
                    link(V.tensor_tensor(nt[:, t], v3[:, t], v3[:, t], ALU.mult))
                    V.tensor_reduce(stat[:, 0, 4 * t:4 * t + 4], nt[:, t].rearrange("p (g n) -> p g n", n=P), AX.X,
                                    ALU.add).then_inc(m3_ss, 1)
                dve.wait_ge(m3_srt, 1)
                link(V.reciprocal(stat[:, 2, 0:16], stat[:, 1, 0:16]))
                for t in range(TT):
                    vt = v3[:, t].rearrange("p (g n) -> p g n", n=P)
                    V.tensor_tensor(vt, vt, stat[:, 2, 4 * t:4 * t + 4].unsqueeze(2).to_broadcast([P, 4, P]),
                                    ALU.mult).then_inc(m3_vn, 1)
                dve.wait_ge(ld_odd, 32)
                dve.wait_ge(m3_vn, 4)
                for g in range(4):
                    gain = COL["sg_gain"] + g
                    dve.wait_ge(m3_sg, g + 1)
                    if g >= 1:
                        dve.wait_ge(m3_y, g)
                    link(V.scalar_tensor_tensor(nt[:, 0].rearrange("p (n c) -> p n c", c=P),
                                                Dn[:, g].rearrange("p (n c) -> p n c", c=P), pv[:, gain:gain + 1],
                                                sgb[:, g].unsqueeze(1).to_broadcast([P, TT, P]), ALU.mult, ALU.add))
                    link(V.tensor_tensor(nt[:, 0], nt[:, 0], u3[:, g], ALU.mult))
                    link(V.tensor_copy(nt[:, 1], nt[:, 0])) if False else None
                    dve.wait_ge(group_done, GROUPS_BEFORE[T0["oddin"] + 10])
                    split(nt[:, 0], g).then_inc(m3_y, 1)
                dve.wait_ge(act_z, Z0["oddin"] + 20)
                for c in range(4):
                    w = COL["conv_w2"] + c
                    dve.wait_ge(m3_y, 4 + c)
                    link(V.tensor_tensor(z3[:, c, 1:1 + S], z3[:, c, 1:1 + S], cg3[:, c], ALU.mult))
                    link(V.tensor_scalar(nt[:, 0], z3[:, c, 0:S], pv[:, w:w + 1], None, ALU.mult))
                    for tap in (1, 2):
                        link(V.scalar_tensor_tensor(nt[:, 0], z3[:, c, tap:tap + S], pv[:, w + 4 * tap:w + 4 * tap + 1],
                                                    nt[:, 0], ALU.mult, ALU.add))
                    link(V.tensor_tensor(nt[:, 0], nt[:, 0], bg3[:, c], ALU.mult))
                    split(nt[:, 0], 4 + c).then_inc(m3_y, 1)
                project_residual("oddout", MOD_OUT["mod1"] + 16)

        @block.tensor
        def _(pe):
            mm = nc.tensor.matmul

            def product(out, weights, acts, first=True, last=True):
                (wh, wl), (ah, al) = weights, acts
                mm(out, wh, ah, start=first, stop=False)
                mm(out, wl, ah, start=False, stop=False)
                return mm(out, wh, al, start=False, stop=last)

            def mod_sums(n, batch, q):
                pe.wait_ge(mod_red, q + n)
                if not isinstance(batch, int) or batch:
                    pe.wait_ge(mod_out, batch)
                for r in range(n):
                    ins = mm(Dn[:, M, r:r + 1], red[:, r], ones[:, 0:1], start=True, stop=True)
                ins.then_inc(mod_sum, 1)

            def sum_squares(name, n=S):
                q = NORM[name][0]
                for k in range(KC):
                    pe.wait_ge(act_sq, KC * q + k + 1)
                    mm(sum_bank(name)[:, 0:n], ones[:], nt[:, k % 2, 0:n], start=(k == 0), stop=(k == KC - 1)).then_inc(pe_ss, 1)

            def in_group(slot, c, out, ready=None, n=S):
                for k in range(KC):
                    if ready is not None:
                        pe.wait_ge(dve_alo, ready + k + 1)
                    cs = slice(c * P, c * P + P)
                    ins = product(out, (w_in(w_hi, slot)[:, k, cs], w_in(w_lo, slot)[:, k, cs]),
                                  (a_hi[:, k, 0:n], a_lo[:, k, 0:n]), k == 0, k == KC - 1)
                return ins

            def token_group(slot, out, t, cs):
                ts = slice(t * P, t * P + P)
                for k in range(KC):
                    ins = product(out, (a_hi[:, k, ts], a_lo[:, k, ts]),
                                  (w_in(w_hi, slot)[:, k, cs], w_in(w_lo, slot)[:, k, cs]), k == 0, k == KC - 1)
                return ins

            def unit(stage, i):
                t, u = T0[stage], i + UNIT0[stage]
                a_ready = KC * NORM[stage][1]
                for j in range(2):
                    pe.wait_ge(weight_lo, 3 * i + (t + j + 1))
                    for c in range(2):
                        pe.wait_ge((act_silu, dve_gu)[j], 2 * u + (c + 1))
                        in_group((t + j) % RING, c, G[:, 2 * j + c],
                                 a_ready if (j == 0 and c == 0) else None).then_inc(group_done, 1)
                pe.wait_ge(weight_lo, 3 * i + (t + 3))
                s = (t + 2) % RING
                for ms in ((0, 1, 2), (3, 4, 5), (6, 7)):
                    for k in range(2):
                        for m in ms:
                            if k == 0:
                                back = {0: 1, 1: 1, 2: -2}.get(m, m - 2)
                                if m < 3:
                                    pe.wait_ge(down_added, 8 * u + (PRIME_ADD - 8 + 8 - 8 + {0: 7, 1: 8, 2: 6}[m]))
                                else:
                                    pe.wait_ge(down_added, 8 * u + (PRIME_ADD + m - 2))
                            if m == 0:
                                pe.wait_ge(dve_hlo, 2 * u + (1 + k + 1))
                            msl = slice(m * P, m * P + P)
                            ins = product(Dn[:, m % 3], (w_down(w_hi, s)[:, k, msl], w_down(w_lo, s)[:, k, msl]),
                                          (h_hi[:, k], h_lo[:, k]), k == 0, k == 1)
                            if k == 1:
                                ins.then_inc(group_done, 1)
                n = MOD_PER_UNIT[stage]
                if n:
                    mod_sums(n, i + MB0[stage], i * n + MQ0[stage])

            def units(stage):
                with pe.Fori(0, UNITS[stage]) as i:
                    unit(stage, i)

            def projection(stage, g0, z, j, groups=None, ready=None):
                t = T0[stage] + j
                pe.wait_ge(weight_lo, t + 1)
                for c in range(2):
                    g = g0 + c
                    if g >= 4:
                        pe.wait_ge(*z(g - 3))
                    if groups:
                        groups(t % RING, c, G[:, g % 4]).then_inc(group_done, 1)
                    else:
                        in_group(t % RING, c, G[:, g % 4], ready if c == 0 else None).then_inc(group_done, 1)

            pe.wait_ge(ld_const, 80)
            q = 0
            sum_squares("ffn1")
            for b, (_, _, n) in enumerate(MOD_FIRST):
                mod_sums(n, b, q)
                q += n
            units("ffn1")
            sum_squares("ffn1_end")

            sum_squares("mix")

            def values1(slot, c, out):
                for t in (2 * c, 2 * c + 1):
                    ins = token_group(slot, out[:, 256 * (t % 2):256 * (t % 2) + 256], t, slice(0, 256))
                return ins
            for j in range(10):
                projection("mixin", 2 * j, lambda n: (act_z, Z0["mixin"] + n), j,
                           values1 if j in (4, 5) else None, KC * NORM["mix"][1] if j == 0 else None)
            pe.wait_ge(ld_mix, 16)
            pe.wait_ge(act_z, 20)
            for c in range(4):
                pe.wait_ge(m1_xc, c + 1)
                for dg in range(4):
                    if c:
                        pe.wait_ge(m1_sig, 4 * (c - 1) + dg + 1)
                    mm(G[:, dg], bd[:, dg, c * P:c * P + P], e0, start=True, stop=True).then_inc(m1_gate, 1)
            for idx in range(8):
                if idx < 4:
                    pe.wait_ge(m1_sig, 12 + idx + 1)
                else:
                    pe.wait_ge(m1_rope, idx - 3)
                mm(G[:, idx % 4], rot1[:], (q1, k1)[idx // 4][:, idx % 4], start=True, stop=True).then_inc(m1_rot, 1)
            pe.wait_ge(m1_rope, 8)

            def scores(n):
                h, i = n // 4, n % 4
                if n >= 2:
                    pe.wait_ge(m1_exp, 2 * n - 2)
                for m in range(2):
                    ps = slice(64 * m, 64 * m + 64)
                    mm(G[:, 2 * (n % 2) + m], q1[ps, h, i * P:(i + 1) * P], k1[ps, h], start=True,
                       stop=True).then_inc(m1_qk, 1)

            def turn(n):
                pe.wait_ge(m1_w, n + 1)
                if n >= 2:
                    pe.wait_ge(m1_wt, n - 1)
                for k in range(4):
                    ins = nc.tensor.transpose(Dn[:, n % 2, k * P:(k + 1) * P], wsm1[:, n % 2, k * P:(k + 1) * P], ident[:])
                ins.then_inc(m1_tr, 1)

            def values_sum(h):
                pe.wait_ge(m1_wt, 4 * h + 4)
                if h:
                    pe.wait_ge(m1_o, h)
                for k in range(4):
                    ins = mm(Dn[:, M], v1[:, k, h * P:(h + 1) * P], wt1[:, k], start=(k == 0), stop=(k == 3))
                ins.then_inc(m1_pv, 1)
            for n in range(17):
                if n < 16:
                    scores(n)
                if n >= 1:
                    turn(n - 1)
                    if n % 4 == 0:
                        values_sum(n // 4 - 1)
            for h in range(4):
                pe.wait_ge(m1_ssq, h + 1)
                pe.wait_ge(m1_exp, 32)
                mm(G[:, h], ones[:], nt[:, h], start=True, stop=True).then_inc(m1_ssp, 1)
            pe.wait_ge(m1_sub, 4)
            pe.wait_ge(m1_rec, 4)
            pe.wait_ge(m1_srt, 4)
            for j in range(4):
                projection("mixout", 2 * j, lambda n: (act_z, Z0["mixout"] + n), j)
            sum_squares("mix_end")

            sum_squares("ffn2")
            units("ffn2")
            sum_squares("ffn2_end")

            sum_squares("ctx", CTX)
            sum_squares("even")
            t = T0["evenin"]
            pe.wait_ge(weight_lo, t + 1)
            s = t % RING
            r = KC * NORM["ctx"][1]
            in_group(s, 0, G[:, 0, 0:CTX], r, CTX).then_inc(group_done, 1)
            for tt in range(CT):
                ins = token_group(s, G[:, 1, tt * P:(tt + 1) * P], tt, slice(P, 2 * P))
            ins.then_inc(group_done, 1)
            in_group(s, 0, G[:, 2], KC * NORM["even"][1]).then_inc(group_done, 1)
            for tt in range(TT):
                ins = token_group(s, G[:, 3, tt * P:(tt + 1) * P], tt, slice(P, 2 * P))
            ins.then_inc(group_done, 1)

            def norm_sums(idx, n):
                pe.wait_ge(m2_ssq, idx + 1)
                if idx:
                    pe.wait_ge(m2_srt, idx)
                mm(Dn[:, 0, 0:n], ones64[:], nt[:, 0, 0:n], start=True, stop=True).then_inc(m2_ssp, 1)

            def turned(idx, z):
                pe.wait_ge(m2_kn, idx + 1)
                if idx > 1:
                    pe.wait_ge(m2_rope, idx - 1)
                mm(Dn[:, 1], rot2[:], z, start=True, stop=True).then_inc(m2_rot, 1)
            z = lambda n: (act_z, Z0["evenin"] + n)
            norm_sums(0, CTX)
            projection("evenin", 4, z, 1)
            norm_sums(1, S)
            projection("evenin", 6, z, 2)
            turned(1, kall[:, CTX:SK])
            norm_sums(2, S)
            turned(2, q2[:, 0])
            norm_sums(3, S)
            projection("evenin", 8, z, 3)
            turned(3, q2[:, 1])
            norm_sums(4, S)
            turned(4, q2[:, 2])
            norm_sums(5, S)
            projection("evenin", 10, z, 4)
            turned(5, q2[:, 3])
            pe.wait_ge(ld_even, 32)
            pe.wait_ge(act_z, Z0["evenin"] + 12)
            for g in range(4):
                pe.wait_ge(m2_d, g + 1)
                mm(G[:, g], poolw[:, g], nt[:].rearrange("p a b -> p (a b)")[:, 1056:1056 + S], start=True,
                   stop=True).then_inc(m2_pw, 1)
            pe.wait_ge(m2_rope, 5)
            pe.wait_ge(m2_swap, 1)
            pe.wait_ge(m2_ps, 4)

            def scores2(n):
                h, i = n // 4, n % 4
                c, half = h // 2, h % 2
                ps = slice(64 * half, 64 * half + 64)
                keys = kall if c // 2 == half else kswap
                if n >= 2:
                    pe.wait_ge(m2_exp, n - 1)
                b = 2 * (n % 2)
                q = q2[ps, c, i * P:(i + 1) * P]
                mm(G[:, b], q, keys[ps, 0:S], start=True, stop=True)
                mm(G[:, b + 1, 0:CTX], q, keys[ps, S:SK], start=True, stop=True).then_inc(m2_qk, 1)

            def turn2(n):
                pe.wait_ge(m2_w, n + 1)
                if n >= 1:
                    pe.wait_ge(m2_wt, n)
                for k in range(6):
                    ins = nc.tensor.transpose(Dn[:, k // 4, (k % 4) * P:(k % 4 + 1) * P],
                                              pexp2[:, n % 2, k * P:(k + 1) * P], ident[:])
                ins.then_inc(m2_tr, 1)

            def values_sum2(h):
                c, half = h // 2, h % 2
                pe.wait_ge(m2_wt, 4 * h + 4)
                if h >= 4 and half == 0:
                    pe.wait_ge(m2_olo, c - 1)
                for k in range(6):
                    v = vz[:, 2 * k + c // 2, 64 * (1 - half):64 * (1 - half) + P]
                    ins = mm(Dn[:, 2 + c % 2], v, wt2[:, k], start=(half == 0 and k == 0), stop=(half == 1 and k == 5))
                ins.then_inc(m2_pv, 1)
            for n in range(33):
                if n < 32:
                    scores2(n)
                if n >= 1:
                    turn2(n - 1)
                    if n % 4 == 0:
                        values_sum2(n // 4 - 1)
            pe.wait_ge(m2_olo, 4)
            pe.wait_ge(m2_pool, 4)
            for j in range(4):
                projection("evenout", 2 * j, lambda n: (x_done, XDONE["even"] + n), j)

            for l in range(2):
                stage = f"moe{l}"
                sum_squares(stage)
                pe.wait_ge(rt_w, 2 * l + 2)
                pe.wait_ge(dve_alo, KC * NORM[stage][1] + KC)
                for tt in range(TT):
                    ts = slice(tt * P, tt * P + P)
                    for k in range(KC):
                        ins = product(Dn[:, M, 20 * tt:20 * tt + 20], (a_hi[:, k, ts], a_lo[:, k, ts]),
                                      (rw_hi[:, k], rw_lo[:, k]), k == 0, k == KC - 1)
                ins.then_inc(rt_logit, 1)
                units(stage)
                if l == 1:
                    break
                sum_squares("odd")

                def values3(slot, c, out):
                    for t in (2 * c, 2 * c + 1):
                        ins = token_group(slot, out[:, 256 * (t % 2):256 * (t % 2) + 256], t, slice(0, 256))
                    return ins
                for j in range(10):
                    projection("oddin", 2 * j, lambda n: (act_z, Z0["oddin"] + n), j,
                               values3 if j in (2, 3) else None, KC * NORM["odd"][1] if j == 0 else None)
                pe.wait_ge(ld_odd, 32)
                pe.wait_ge(m3_vn, 4)
                for g in range(4):
                    for n in range(TT):
                        ins = mm(Dn[:, g, n * P:(n + 1) * P], v3[:, n, g * P:(g + 1) * P], sgw[:, g], start=True, stop=True)
                    ins.then_inc(m3_sg, 1)
                pe.wait_ge(m3_y, 8)
                pe.wait_ge(act_z, Z0["oddin"] + 20)
                for j in range(4):
                    projection("oddout", 2 * j, lambda n: (x_done, XDONE["odd"] + n), j)


def kernel(x, c, positions, w_ada, b_ada, norm_g, ffn1_w_in, ffn1_w_out, ffn2_w_in, ffn2_w_out,
           w_mix_in, w_mix_out, lambda_q, lambda_k, subln_g, conv_w, conv_b, lru_w_gate, lru_b_gate,
           lru_lambda, c_2, ctx_2, c_ctx_2, mod_w_2, mod_b_2, norm1_g_2, norm2_g_2, even_w_in_2,
           q_gain_2, k_gain_2, pool_w_2, pool_scale_2, even_w_out_2, odd_w_in_2, sg_gain_2, sg_w_2,
           sg_b_2, conv_w_2, odd_w_out_2, router_g_w_2, router_g_b_2, router_e_w_2, router_e_b_2,
           w_gate_2, w_up_2, w_down_2):
    import numpy as np
    import concourse.bacc as bacc
    from concourse.bass_utils import run_bass_kernel_spmd as run

    f = np.float32

    def cols(v):
        return np.asarray(v).reshape(-1, P).T

    def twice(v):
        return np.concatenate([np.asarray(v).reshape(1, 64)] * 2, axis=1)

    idx = np.arange(P)
    inv = (f(10000.0) ** (-np.arange(0, 64, 2, dtype=f) / f(64))).astype(f)
    inv_col = inv[idx % 32].reshape(1, P)
    rot1 = np.zeros((P, P), f)
    rot2 = np.zeros((P, P), f)
    for o in range(P):
        rot1[o + 32 if o % 64 < 32 else o - 32, o] = -1.0 if o % 64 < 32 else 1.0
        rot2[o + 16 if o % 32 < 16 else o - 16, o] = -1.0 if o % 32 < 16 else 1.0
    inv2 = (f(10000.0) ** (-np.arange(0, 32, 2, dtype=f) / f(32))).astype(f)
    tok = np.arange(S)
    row, col = (tok // 64).astype(f), (tok % 64).astype(f)
    ang = np.where((idx % 64 < 32)[:, None], row[None, :], col[None, :]).astype(f) * inv2[idx % 16][:, None]
    rope2 = np.stack([np.cos(ang), np.sin(ang)], axis=1).astype(f)
    inv_count = np.stack([1.0 / (np.clip(tok + w - w // 2, 0, S) - np.clip(tok - w // 2, 0, S)).astype(f)
                          for w in (2, 4, 8, 16)]).astype(f)
    block64 = np.kron(np.eye(2, dtype=f), np.ones((64, 64), f))

    params = np.concatenate([cols(v) for v in (
        c, c_2, c_ctx_2, b_ada, mod_b_2, norm_g, norm1_g_2, norm2_g_2, subln_g, conv_w, conv_b, lru_b_gate,
        lru_lambda, twice(q_gain_2), twice(k_gain_2), pool_scale_2, sg_gain_2, conv_w_2, inv_col)], axis=1)
    assert params.shape == (P, NCOL), params.shape
    wg = np.asarray(lru_w_gate)[0]
    bd = np.zeros((P, 4, 4, P), wg.dtype)
    for d in range(2):
        for g in range(2):
            for n in range(8):
                h = 64 * (n % 2)
                bd[h:h + 64, 2 * d + g, n // 2, h:h + 64] = wg[d, g, n]
    arrays = {
        "x_t": np.asarray(x)[0].T, "ctx_t": np.asarray(ctx_2)[0].T, "params": params,
        "positions": np.asarray(positions),
        "lambda_qk": np.concatenate([np.asarray(lambda_q).reshape(-1), np.asarray(lambda_k).reshape(-1)]),
        "router_b": np.concatenate([np.asarray(router_g_b_2), np.asarray(router_e_b_2)], axis=1).reshape(-1),
        "router_w": np.concatenate([np.asarray(router_g_w_2), np.asarray(router_e_w_2)], axis=2),
        "lru_bd": bd.reshape(P, 4, 4 * P), "pool_w": np.asarray(pool_w_2)[0],
        "sg_w_t": np.asarray(sg_w_2)[0].transpose(2, 0, 1), "sg_b": np.asarray(sg_b_2)[0],
        "w_ada": np.asarray(w_ada)[0], "mod_w": np.asarray(mod_w_2),
        "ffn1_w_in": np.asarray(ffn1_w_in)[0], "ffn1_w_out": np.asarray(ffn1_w_out)[0],
        "ffn2_w_in": np.asarray(ffn2_w_in)[0], "ffn2_w_out": np.asarray(ffn2_w_out)[0],
        "w_mix_in": np.asarray(w_mix_in)[0], "w_mix_out": np.asarray(w_mix_out)[0],
        "even_w_in": np.asarray(even_w_in_2)[0], "even_w_out": np.asarray(even_w_out_2)[0],
        "odd_w_in": np.asarray(odd_w_in_2)[0], "odd_w_out": np.asarray(odd_w_out_2)[0],
        "w_gate": np.asarray(w_gate_2), "w_up": np.asarray(w_up_2), "w_down": np.asarray(w_down_2),
        "ident": np.eye(P, dtype=f), "ones": np.ones((P, P), f), "ones64": block64, "rot1": rot1, "rot2": rot2,
        "rope2": rope2, "inv_count": inv_count,
    }
    arrays = {n: np.ascontiguousarray(a) for n, a in arrays.items()}
    nc = bacc.Bacc("TRN2", target_bir_lowering=False, num_devices=1)
    io = {n: nc.dram_tensor(f"in_{n}", a.shape, mybir.dt.from_np(a.dtype), kind="ExternalInput").ap()
          for n, a in arrays.items()}
    io["comb_dram"] = nc.dram_tensor("comb_dram", (2 * EXPERTS, S), F32, kind="Internal").ap()
    io["out"] = nc.dram_tensor("out", (D, S), F32, kind="ExternalOutput").ap()
    build(nc, io)
    r = run(nc, [{f"in_{n}": a for n, a in arrays.items()}], core_ids=[0])
    return np.ascontiguousarray(r.results[0]["out"].T).reshape(1, S, D)
```

```python
import concourse.bass as bass
from concourse import mybir
from contextlib import ExitStack

F32 = mybir.dt.float32
F32R = mybir.dt.float32r
I32 = mybir.dt.int32
ALU = mybir.AluOpType
ACT = mybir.ActivationFunctionType
AX = mybir.AxisListType

P = 128
D = 1024
KC = D // P
S = 512
TT = S // P
CTX = 256
CT = CTX // P
D_FF = 2816
UNIT = 256
FFN_UNITS = D_FF // UNIT
EXPERTS = 16
HEADS1 = 4
EPS = 1e-6
LAMBDA_INIT = 0.2
TW = 2048
RING = 3

COLS = [("c", 8), ("c2", 8), ("cctx", 8), ("b_ada", 72), ("mod_b", 96), ("norm_g", 48), ("norm1", 16),
        ("norm2", 16), ("subln", 1), ("conv_w", 16), ("conv_b", 4), ("b_gate", 16), ("lam", 8),
        ("q_gain", 1), ("k_gain", 1), ("pool_scale", 4), ("sg_gain", 4), ("conv_w2", 12), ("inv_freq", 1)]
COL = {}
_at = 0
for _name, _n in COLS:
    COL[_name] = _at
    _at += _n
NCOL = _at

UNIT_GROUPS = [2, 2, 8]
STREAM = [("ffn1", UNIT_GROUPS * FFN_UNITS), ("mixin", [2] * 10), ("modctx", [2] * 10), ("mixout", [2] * 4),
          ("ffn2", UNIT_GROUPS * FFN_UNITS), ("evenin", [4, 2, 2, 2, 2]), ("evenout", [2] * 4),
          ("moe0", UNIT_GROUPS * EXPERTS), ("oddin", [2] * 10), ("oddout", [2] * 4),
          ("moe1", UNIT_GROUPS * EXPERTS)]
T0, GROUPS_BEFORE = {}, [0]
for _name, _g in STREAM:
    T0[_name] = len(GROUPS_BEFORE) - 1
    for _x in _g:
        GROUPS_BEFORE.append(GROUPS_BEFORE[-1] + _x)
TILES = len(GROUPS_BEFORE) - 1
UNIT0 = {"ffn1": 0, "ffn2": FFN_UNITS, "moe0": 2 * FFN_UNITS, "moe1": 2 * FFN_UNITS + EXPERTS}
UNITS = {"ffn1": FFN_UNITS, "ffn2": FFN_UNITS, "moe0": EXPERTS, "moe1": EXPERTS}

MOD_PER_UNIT = {"ffn1": 5, "ffn2": 4, "moe0": 3, "moe1": 0}
MOD_FIRST = [("ada", 0, 5), ("ada", 5, 5), ("ada", 10, 5), ("ada", 15, 2)]
MOD_VECTOR = [[r for r in range(n) if (c0 + r) % 2 == 0] for _, c0, n in MOD_FIRST]
MODCTX = [(j, 16, 168 + 2 * j) for j in range(8)] + [(22, 8, 72 + 44), (23, 8, 72 + 46)]
MODCTX_STEPS = [3, 3, 2, 2]
MOD_COND = {"ada": 0, "mod0": 8, "mod1": 8, "ctx": 16}
MOD_OUT = {"ada": 0, "mod0": 72, "mod1": 120, "ctx": 168}
MOD_BIAS = {"ada": COL["b_ada"], "mod0": COL["mod_b"], "mod1": COL["mod_b"] + 48, "ctx": COL["mod_b"]}
MOD_SLOTS = 5
MOD_LOOP = {"ffn1": ("ada", 17), "ffn2": ("mod0", 0), "moe0": ("mod1", 0)}
MB0, MQ0 = {}, {}
_b, _q = len(MOD_FIRST), sum(len(v) for v in MOD_VECTOR)
for _name in ("ffn1", "ffn2", "moe0"):
    MB0[_name], MQ0[_name] = _b, _q
    _b += UNITS[_name]
    _q += UNITS[_name] * MOD_PER_UNIT[_name]


def mod_fills(stage, r):
    n = sum(1 for _, _, k in MOD_FIRST if k > r)
    for name in ("ffn1", "ffn2", "moe0"):
        if name == stage:
            return n
        n += UNITS[name] * (MOD_PER_UNIT[name] > r)


PRIME_SILU, PRIME_GU, PRIME_ADD = 2, 2, 8

NORM = {"ffn1": (0, 0), "ffn1_end": (1, None), "mix": (2, 1), "mix_end": (3, None), "ffn2": (4, 2),
        "ffn2_end": (5, None), "ctx": (6, 3), "even": (7, 4), "moe0": (8, 5), "odd": (9, 6), "moe1": (10, 7)}
XDONE = {"ffn1": 0, "mix": 8, "ffn2": 16, "even": 24, "moe0": 32, "odd": 40, "moe1": 48, "end": 56}
Z0 = {"mixin": 0, "mixout": 20, "evenin": 28, "oddin": 40}


def build(nc, io):
    ctx = ExitStack()
    with ctx:
        def sb(name, shape, dt=F32):
            return ctx.enter_context(nc.sbuf_tensor(name, shape, dt))

        names = set()

        def sem(name):
            names.add(name)
            return ctx.enter_context(nc.semaphore(name))

        w_raw = sb("w_raw", [P, RING, TW])
        w_hi = sb("w_hi", [P, RING, TW], F32R)
        w_lo = sb("w_lo", [P, RING, TW], F32R)
        x = sb("x", [P, KC, S])
        a_hi = sb("a_hi", [P, KC, S], F32R)
        a_lo = sb("a_lo", [P, KC, S], F32R)
        h_hi = sb("h_hi", [P, 2, S], F32R)
        h_lo = sb("h_lo", [P, 2, S], F32R)
        nt = sb("nt", [P, 4, S])
        root = sb("root", [P, S])
        rinv = sb("rinv", [P, S])
        rope = sb("rope", [P, 2, S])
        red = sb("red", [P, MOD_SLOTS, P])
        pv = sb("pv", [P, NCOL])
        cond = sb("cond", [P, 24])
        cond_split = sb("cond_split", [P, 24, 2], F32R)
        mods = sb("mods", [P, 184])
        acol = sb("acol", [P, 8 * KC])
        gcol = sb("gcol", [P, 3 * KC])
        misc = sb("misc", [P, 64])
        stat = sb("stat", [P, 5, 32])
        ident = sb("ident", [P, P])
        ones = sb("ones", [P, P])
        ones64 = sb("ones64", [P, P])
        rot1 = sb("rot1", [P, P])
        rot2 = sb("rot2", [P, P])
        rw = sb("rw", [P, KC, 20])
        rw_hi = sb("rw_hi", [P, KC, 20], F32R)
        rw_lo = sb("rw_lo", [P, KC, 20], F32R)
        rb = sb("rb", [P, 2, 20])
        rt = sb("rt", [P, 296])
        K = 256
        arena = sb("arena", [P, 52 * K + 16])

        def ar(start, *shape):
            n = 1
            for d in shape:
                n *= d
            v = arena[:, start:start + n]
            if len(shape) == 2:
                v = v.rearrange("p (a b) -> p a b", b=shape[1])
            if len(shape) == 3:
                v = v.rearrange("p (a b c) -> p a b c", b=shape[1], c=shape[2])
            return v

        yacc = ar(0, KC, S)
        sg = ar(16 * K, 2, S)
        hid = ar(20 * K, 2, S)
        comb_row = ar(24 * K, S)
        comb_pad = ar(26 * K, TT, 32)
        comb_t = ar(26 * K + 128, TT, 32)
        mod_raw = ar(28 * K, MOD_SLOTS, KC, P)
        prod = ar(48 * K, KC, P)
        q1, k1, v1 = ar(0, 4, S), ar(8 * K, 4, S), ar(16 * K, 4, S)
        XRW = S + 3
        xr1 = ar(24 * K, 4, XRW)
        yr1 = ar(32 * K + 16, 4, S)
        bd = ar(40 * K + 16, 4, 4 * P)
        e0, e1 = ar(48 * K + 16, S), ar(50 * K + 16, S)
        pexp1 = ar(24 * K, 6, S)
        wsm1 = ar(36 * K, 2, S)
        wt1 = ar(40 * K, 2, 4, P)
        xc1 = (e0, red[:].rearrange("p a b -> p (a b)")[:, 0:S])
        SK = CTX + S
        q2 = ar(0, 4, S)
        kall, kswap = ar(8 * K, SK), ar(11 * K, SK)
        vz = ar(14 * K, 12, 192)
        PW = S + 16
        p2 = ar(23 * K + 64, 4, PW)
        ctxx = ar(32 * K, KC, CTX)
        ic = ar(41 * K, 4, S)
        poolw = ar(49 * K, 4, P)
        pexp2 = ar(23 * K + 64, 3, SK)
        wt2 = ar(33 * K, 2, 6, P)
        u3, v3 = ar(0, 4, S), ar(8 * K, 4, S)
        ZW = S + 2
        z3 = ar(16 * K, 4, ZW)
        bg3, cg3 = ar(25 * K, 4, S), ar(33 * K, 4, S)
        sgw = ar(41 * K, 4, P)
        sgb = ar(43 * K, 4, P)

        G = ctx.enter_context(nc.psum_tensor("G", [P, 4, S], F32))
        Dn = ctx.enter_context(nc.psum_tensor("Dn", [P, 4, S], F32))
        M = 3

        def down_bank(m):
            return (Dn[:, 0], Dn[:, 1], Dn[:, 2], G[:, 0], G[:, 1], Dn[:, 0], Dn[:, 1], Dn[:, 2])[m]

        def sum_bank(name):
            return G[:, 3] if name.endswith("_end") else Dn[:, 2]

        def w_in(buf, slot):
            return buf[:, slot, :].rearrange("p (k n) -> p k n", n=256)

        def w_down(buf, slot):
            return buf[:, slot, :].rearrange("p (k n) -> p k n", n=D)

        raw_full = [sem(f"raw_full{s}") for s in range(RING)]
        weight_hi, weight_lo, group_done = sem("weight_hi"), sem("weight_lo"), sem("group_done")
        mod_full = [sem(f"mod_full{s}") for s in range(MOD_SLOTS)]
        modctx_out = sem("modctx_out")
        mod_mul, mod_red, mod_sum, mod_out = sem("mod_mul"), sem("mod_red"), sem("mod_sum"), sem("mod_out")
        act_silu, dve_gu, act_hhi, dve_hlo, down_added = (sem(n) for n in (
            "act_silu", "dve_gu", "act_hhi", "dve_hlo", "down_added"))
        dve_comb, comb_full = sem("dve_comb"), sem("comb_full")
        act_sq, pe_ss, act_root, dve_rinv = sem("act_sq"), sem("pe_ss"), sem("act_root"), sem("dve_rinv")
        dve_cols, dve_t, act_af, act_ahi, dve_alo = (sem(n) for n in (
            "dve_cols", "dve_t", "act_af", "act_ahi", "dve_alo"))
        dve_yn, x_done = sem("dve_yn"), sem("x_done")
        act_z = sem("act_z")
        ld_x, ld_pv, ld_const, ld_row = sem("ld_x"), sem("ld_pv"), sem("ld_const"), sem("ld_row")
        ld_mix, ld_ctx, ld_even, ld_rope2, ld_odd = (sem(n) for n in (
            "ld_mix", "ld_ctx", "ld_even", "ld_rope2", "ld_odd"))
        ld_rw = [sem("ld_rw0"), sem("ld_rw1")]
        cond_done, dve_chain, act_chain = sem("cond_done"), sem("dve_chain"), sem("act_chain")
        rope1_ang, rope1_tab = sem("rope1_ang"), sem("rope1_tab")
        yacc_zero, arena_free, arena_back = sem("yacc_zero"), sem("arena_free"), sem("arena_back")
        lam_sum, lam_exp, sp_exp = sem("lam_sum"), sem("lam_exp"), sem("sp_exp")
        m1_pad, m1_gelu, m1_xc, m1_gate, m1_sig, m1_at, m1_m, m1_sqrt, m1_rec = (sem("m1_" + n) for n in (
            "pad", "gelu", "xc", "gate", "sig", "at", "m", "sqrt", "rec"))
        m1_rot, m1_rope, m1_qk, m1_nm, m1_exp, m1_w, m1_tr, m1_wt, m1_pv, m1_o = (sem("m1_" + n) for n in (
            "rot", "rope", "qk", "nm", "exp", "w", "tr", "wt", "pv", "o"))
        m1_ssq, m1_ssp, m1_srt, m1_sub = (sem("m1_" + n) for n in ("ssq", "ssp", "srt", "sub"))
        m2_pad, m2_ssq, m2_ssp, m2_srt, m2_kn, m2_rot, m2_rope, m2_swap = (sem("m2_" + n) for n in (
            "pad", "ssq", "ssp", "srt", "kn", "rot", "rope", "swap"))
        m2_d, m2_pw, m2_ps, m2_pool = (sem("m2_" + n) for n in ("d", "pw", "ps", "pool"))
        m2_qk, m2_nm, m2_exp, m2_w, m2_tr, m2_wt, m2_pv, m2_ohi, m2_olo = (sem("m2_" + n) for n in (
            "qk", "nm", "exp", "w", "tr", "wt", "pv", "ohi", "olo"))
        m3_pad, m3_ss, m3_srt, m3_vn, m3_sg, m3_y = (sem("m3_" + n) for n in (
            "pad", "ss", "srt", "vn", "sg", "y"))
        rt_w, rt_logit, rt_d1, rt_exp1, rt_d2, rt_exp2, rt_comb, rt_store = (sem("rt_" + n) for n in (
            "w", "logit", "d1", "exp1", "d2", "exp2", "comb", "store"))
        st_out = sem("st_out")

        io_w = {n: io[n].rearrange("(k p) n -> p k n", p=P) for n in (
            "ffn1_w_in", "ffn2_w_in", "w_mix_in", "w_mix_out", "even_w_in", "even_w_out",
            "odd_w_in", "odd_w_out", "w_ada")}
        io_down = {n: io[n].rearrange("(u k p) n -> u p k n", k=2, p=P) for n in ("ffn1_w_out", "ffn2_w_out")}
        moe_gate = io["w_gate"].rearrange("l e (k p) n -> (l e) p k n", p=P)
        moe_up = io["w_up"].rearrange("l e (k p) n -> (l e) p k n", p=P)
        moe_down = io["w_down"].rearrange("l e (k p) n -> (l e) p k n", p=P)
        mod_w = {"ada": io_w["w_ada"],
                 "mod0": io["mod_w"][0].rearrange("(k p) n -> p k n", p=P),
                 "mod1": io["mod_w"][1].rearrange("(k p) n -> p k n", p=P)}
        comb_dram = io["comb_dram"]

        block = ctx.enter_context(nc.Block())

        @block.sync
        def _(sp):
            def tile(t, source, buf, i=0):
                s = t % RING
                if not isinstance(i, int) or t + 3 * i >= RING:
                    sp.wait_ge(weight_lo, 3 * i + (t - RING + 1))
                sp.dma_start(buf(w_raw, s), source).then_inc(raw_full[s], 16)

            def mod_chunk(r, matrix, col):
                sp.dma_start(mod_raw[:, r], mod_w[matrix][:, :, bass.ds(col * P, P)]).then_inc(mod_full[r], 16)

            def unit_tiles(stage, i):
                t = T0[stage]
                if stage[:3] == "ffn":
                    w = io_w[stage + "_w_in"]
                    src = (w[:, :, bass.ds(i * UNIT, UNIT)], w[:, :, bass.ds(i * UNIT + D_FF, UNIT)],
                           io_down[stage + "_w_out"][i])
                else:
                    e = i + EXPERTS * (stage == "moe1")
                    src = (moe_gate[e], moe_up[e], moe_down[e])
                tile(t, src[0], w_in, i)
                tile(t + 1, src[1], w_in, i)
                tile(t + 2, src[2], w_down, i)
                if stage in ("ffn2", "moe0"):
                    sp.wait_ge(arena_back, 1 + (stage == "moe0"))
                for r in range(MOD_PER_UNIT[stage]):
                    if r == 0:
                        sp.wait_ge(mod_mul, i * MOD_PER_UNIT[stage] + MQ0[stage])
                        sp.wait_ge(mod_sum, len(MOD_FIRST))
                    matrix, col = MOD_LOOP[stage]
                    mod_chunk(r, matrix, i * MOD_PER_UNIT[stage] + (col + r))
                if stage[:3] == "moe":
                    n = i + EXPERTS * (stage == "moe1")
                    sp.wait_ge(rt_store, 64 * (1 + (stage == "moe1")))
                    sp.wait_ge(dve_comb, 2 * n + 1 + (stage == "moe1"))
                    sp.dma_start(comb_row, comb_dram[n].partition_broadcast(P)).then_inc(comb_full, 16)

            def cols(stage, name, tiles, start=0):
                for j, c in enumerate(tiles):
                    if j < start:
                        continue
                    tile(T0[stage] + j, io_w[name][:, :, c * 256:(c + 1) * 256], w_in)

            sp.dma_start(pv[:], io["params"]).then_inc(ld_pv, 16)
            sp.dma_start(x[:], io["x_t"].rearrange("(k p) n -> p k n", p=P)).then_inc(ld_x, 16)
            for dst, name in ((ident, "ident"), (ones, "ones"), (ones64, "ones64"), (rot1, "rot1"), (rot2, "rot2")):
                sp.dma_start(dst[:], io[name]).then_inc(ld_const, 16)
            sp.dma_start(nt[:, 0].bitcast(I32), io["positions"][0].partition_broadcast(P)).then_inc(ld_row, 16)
            sp.dma_start(nt[:, 1, 0:256], io["lambda_qk"].partition_broadcast(P)).then_inc(ld_row, 16)
            sp.dma_start(rb[:].rearrange("p l n -> p (l n)"), io["router_b"].partition_broadcast(P)).then_inc(ld_row, 16)
            sp.dma_start(rw[:], io["router_w"][0].rearrange("(k p) n -> p k n", p=P)).then_inc(ld_rw[0], 16)
            for b, (matrix, col, n) in enumerate(MOD_FIRST):
                if b:
                    sp.wait_ge(mod_sum, b)
                for r in range(n):
                    mod_chunk(r, matrix, col + r)
            unit_tiles("ffn1", 0)
            with sp.Fori(1, FFN_UNITS) as i:
                unit_tiles("ffn1", i)

            cols("mixin", "w_mix_in", range(RING))
            sp.wait_ge(arena_free, 1)
            sp.dma_start(bd, io["lru_bd"]).then_inc(ld_mix, 16)
            cols("mixin", "w_mix_in", range(10), RING)
            for j, (c, _, _) in enumerate(MODCTX):
                tile(T0["modctx"] + j, mod_w["mod0"][:, :, c * 256:(c + 1) * 256], w_in)
            cols("mixout", "w_mix_out", range(4))

            with sp.Fori(0, FFN_UNITS) as i:
                unit_tiles("ffn2", i)

            cols("evenin", "even_w_in", (2, 0, 1))
            sp.wait_ge(arena_free, 2)
            sp.dma_start(ctxx, io["ctx_t"].rearrange("(k p) n -> p k n", p=P)).then_inc(ld_ctx, 16)
            sp.dma_start(poolw, io["pool_w"].rearrange("g c d -> c g d")).then_inc(ld_even, 16)
            sp.dma_start(ic, io["inv_count"].partition_broadcast(P)).then_inc(ld_even, 16)
            sp.dma_start(rope[:], io["rope2"]).then_inc(ld_rope2, 16)
            cols("evenin", "even_w_in", (2, 0, 1, 3, 4), RING)
            cols("evenout", "even_w_out", range(4))

            with sp.Fori(0, EXPERTS) as i:
                unit_tiles("moe0", i)

            cols("oddin", "odd_w_in", range(RING))
            sp.wait_ge(arena_free, 3)
            sp.dma_start(sgw, io["sg_w_t"]).then_inc(ld_odd, 16)
            sp.dma_start(sgb, io["sg_b"].rearrange("g p -> (g p)").partition_broadcast(P)
                         .rearrange("p (g n) -> p g n", n=P)).then_inc(ld_odd, 16)
            sp.wait_ge(rt_w, 2)
            sp.dma_start(rw[:], io["router_w"][1].rearrange("(k p) n -> p k n", p=P)).then_inc(ld_rw[1], 16)
            cols("oddin", "odd_w_in", range(10), RING)
            cols("oddout", "odd_w_out", range(4))

            with sp.Fori(0, EXPERTS) as i:
                unit_tiles("moe1", i)

            out = io["out"].rearrange("(k p) n -> p k n", p=P)
            for k in range(KC):
                sp.wait_ge(x_done, XDONE["end"] - KC + k + 1)
                sp.dma_start(out[:, k], x[:, k]).then_inc(st_out, 16)
            sp.wait_ge(st_out, 16 * KC)

        @block.gpsimd
        def _(pool):
            def split_lo(s, n):
                pool.wait_ge(weight_hi, n)
                nc.gpsimd.tensor_tensor(w_lo[:, s], w_raw[:, s], w_hi[:, s], ALU.subtract).then_inc(weight_lo, 1)

            with pool.Fori(0, TILES // RING) as i:
                for s in range(RING):
                    split_lo(s, RING * i + (s + 1))
            for t in range(TILES - TILES % RING, TILES):
                split_lo(t % RING, t + 1)

        @block.scalar
        def _(act):
            chain = [0]

            def link(ins):
                chain[0] += 1
                ins.then_inc(act_chain, 1)
                act.wait_ge(act_chain, chain[0])

            def hi(t, i=0):
                if isinstance(i, int) and t + 3 * i >= TILES:
                    return
                s = t % RING
                act.wait_ge(raw_full[s], 16 * i + 16 * (t // RING + 1))
                if not isinstance(i, int) or t + 3 * i >= RING:
                    act.wait_ge(group_done, 12 * i + GROUPS_BEFORE[t - 2])
                nc.scalar.activation(w_hi[:, s], w_raw[:, s], ACT.Copy).then_inc(weight_hi, 1)

            def sum_squares(name, src, n=S, ready=None):
                q = NORM[name][0]
                for k in range(KC):
                    if ready:
                        ready(k)
                    if k >= 2:
                        act.wait_ge(pe_ss, KC * q + k - 1)
                    nc.scalar.activation(nt[:, k % 2, 0:n], src[:, k], ACT.Square).then_inc(act_sq, 1)
                act.wait_ge(pe_ss, KC * q + KC)
                nc.scalar.activation(root[:, 0:n], sum_bank(name)[:, 0:n], ACT.Sqrt, bias=misc[:, 0:1],
                                     scale=1.0 / D).then_inc(act_root, 1)

            def modulated(name, shift, n=S):
                m = NORM[name][1]
                act.wait_ge(dve_cols, m + 1)
                for k in range(KC):
                    t = nt[:, 2 + k % 2, 0:n]
                    act.wait_ge(dve_t, KC * m + k + 1)
                    nc.scalar.activation(t, t, ACT.Identity, bias=mods[:, shift + k:shift + k + 1],
                                         scale=acol[:, KC * m + k:KC * m + k + 1]).then_inc(act_af, 1)
                    act.wait_ge(act_af, KC * m + k + 1)
                    nc.scalar.activation(a_hi[:, k, 0:n], t, ACT.Copy).then_inc(act_ahi, 1)

            def unit(stage, i):
                t, u = T0[stage], i + UNIT0[stage]
                last = isinstance(i, int)
                g = 12 * i + GROUPS_BEFORE[t]
                hi(t + 2, i)
                for c in range(2):
                    act.wait_ge(group_done, g + (c + 1))
                    act.wait_ge(dve_gu, 2 * u + (c + 1))
                    nc.scalar.activation(sg[:, c], G[:, c], ACT.Silu).then_inc(act_silu, 1)
                hi(t + 3, i)
                for c in range(2):
                    act.wait_ge(dve_gu, 2 * u + (PRIME_GU + c + 1))
                    nc.scalar.activation(h_hi[:, c], hid[:, c], ACT.Copy).then_inc(act_hhi, 1)
                hi(t + 4, i)

            def units(stage):
                n, first = UNITS[stage], int(stage == "ffn1")
                if first:
                    unit(stage, 0)
                with act.Fori(first, n - 1) as i:
                    unit(stage, i)
                unit(stage, n - 1)

            def tile_step(t, bank, evacuate):
                hi(t + 2)
                for c in range(2):
                    act.wait_ge(group_done, GROUPS_BEFORE[t] + c + 1)
                    evacuate(c)

            act.wait_ge(ld_pv, 16)
            nc.scalar.activation(cond[:], pv[:, 0:24], ACT.Silu).then_inc(cond_done, 1)
            act.wait_ge(cond_done, 1)
            nc.scalar.activation(cond_split[:, :, 0], cond[:], ACT.Copy).then_inc(cond_done, 1)
            nc.scalar.activation(misc[:, 62:63], pv[:, 0:1], ACT.Copy).then_inc(act_silu, PRIME_SILU)
            act.wait_ge(rope1_ang, 1)
            nc.scalar.activation(rope[:, 1], rope[:, 1], ACT.Sin).then_inc(rope1_tab, 1)
            act.wait_ge(rope1_ang, 2)
            nc.scalar.activation(rope[:, 0], rope[:, 0], ACT.Sin).then_inc(rope1_tab, 1)
            act.wait_ge(lam_sum, 1)
            nc.scalar.activation(misc[:, 2:4], misc[:, 2:4], ACT.Exp).then_inc(lam_exp, 1)
            act.wait_ge(lam_sum, 2)
            nc.scalar.activation(misc[:, 16:24], misc[:, 16:24], ACT.Exp, scale=-1.0).then_inc(sp_exp, 1)

            act.wait_ge(ld_x, 16)
            act.wait_ge(dve_chain, 1)
            sum_squares("ffn1", x)
            hi(0)
            hi(1)
            modulated("ffn1", MOD_OUT["ada"])
            units("ffn1")

            def added(stage):
                return lambda k: act.wait_ge(down_added, PRIME_ADD + 8 * (UNIT0[stage] + UNITS[stage] - 1) + k + 1)
            sum_squares("ffn1_end", yacc, ready=added("ffn1"))

            sum_squares("mix", x, ready=lambda k: act.wait_ge(x_done, XDONE["mix"] + k + 1 - KC + 0))
            modulated("mix", MOD_OUT["ada"] + 24)
            act.wait_ge(m1_pad, 1)

            def evac_mixin(j):
                def go(c):
                    g = 2 * j + c
                    if g < 8:
                        dst, src = (q1, k1)[g // 4][:, g % 4], G[:, g % 4]
                    elif g < 12:
                        dst = v1[:, 2 * c:2 * c + 2, 256 * (j - 4):256 * (j - 3)]
                        src = G[:, g % 4].rearrange("p (t n) -> p t n", n=256)
                    elif g < 16:
                        dst, src = xr1[:, g - 12, 2:2 + S], G[:, g % 4]
                    else:
                        dst, src = yr1[:, g - 16], G[:, g % 4]
                    nc.scalar.activation(dst, src, ACT.Copy, scale=0.125 if g < 4 else 1.0).then_inc(act_z, 1)
                return go
            for j in range(10):
                tile_step(T0["mixin"] + j, 0, evac_mixin(j))
            act.wait_ge(act_z, 20)
            nc.scalar.activation(yr1, yr1, ACT.Gelu_apprx_tanh).then_inc(m1_gelu, 1)
            step = T0["modctx"]
            for c in range(4):
                for d in range(2):
                    for g in range(2):
                        col = COL["b_gate"] + (2 * d + g) * 4 + c
                        act.wait_ge(m1_gate, 4 * c + 2 * d + g + 1)
                        if c:
                            act.wait_ge(m1_rec, c)
                        nc.scalar.activation(nt[:, 2 * g + d], G[:, 2 * d + g], ACT.Sigmoid,
                                             bias=pv[:, col:col + 1]).then_inc(m1_sig, 1)
                for d in range(2):
                    a = (root, rinv)[d]
                    sp8 = misc[:, 32 + 4 * d + c:33 + 4 * d + c]
                    act.wait_ge(m1_sig, 4 * c + 4)
                    nc.scalar.activation(a[:], nt[:, d], ACT.Exp, scale=misc[:, 24 + 4 * d + c:25 + 4 * d + c]).then_inc(m1_at, 1)
                    act.wait_ge(m1_at, 4 * c + 2 * d + 1)
                    nc.scalar.activation(nt[:, d], nt[:, d], ACT.Tanh, scale=sp8).then_inc(m1_at, 1)
                for d in range(2):
                    act.wait_ge(m1_m, 2 * c + d + 1)
                    nc.scalar.activation(nt[:, d], nt[:, d], ACT.Sqrt).then_inc(m1_sqrt, 1)
                for _ in range(MODCTX_STEPS[c]):
                    hi(step + 2)
                    step += 1

            def exps(n):
                act.wait_ge(m1_nm, n + 1)
                if n >= 3:
                    act.wait_ge(m1_w, n - 2)
                for m in range(2):
                    nc.scalar.activation(pexp1[:, 2 * (n % 3) + m], G[:, 2 * (n % 2) + m], ACT.Exp,
                                         bias=stat[:, 1, 2 * n + m:2 * n + m + 1],
                                         accum_out=stat[:, 2, 2 * n + m:2 * n + m + 1]).then_inc(m1_exp, 1)

            def weights_t(n):
                act.wait_ge(m1_tr, n + 1)
                if n >= 2:
                    act.wait_ge(m1_pv, n - 1)
                nc.scalar.activation(wt1[:, n % 2], Dn[:, n % 2].rearrange("p (k q) -> p k q", q=P),
                                     ACT.Copy).then_inc(m1_wt, 1)

            def head_out(h):
                act.wait_ge(m1_pv, 4 * h + 4)
                nc.scalar.activation(q1[:, h], Dn[:, 2 + h % 2], ACT.Copy).then_inc(m1_o, 1)
            for n in range(20):
                if n < 16:
                    exps(n)
                if 2 <= n < 18:
                    weights_t(n - 2)
                if n >= 7 and n % 4 == 3:
                    head_out(n // 4 - 1)
            act.wait_ge(m1_o, 4)
            for h in range(4):
                nc.scalar.activation(nt[:, h], q1[:, h], ACT.Square).then_inc(m1_ssq, 1)
            for h in range(4):
                act.wait_ge(m1_ssp, h + 1)
                nc.scalar.activation(pexp1[:, h], G[:, h], ACT.Sqrt, bias=misc[:, 0:1],
                                     scale=1.0 / P).then_inc(m1_srt, 1)
            for j in range(4):
                def evac_y(c, j=j):
                    nc.scalar.activation(yacc[:, 2 * j + c], G[:, (2 * j + c) % 4], ACT.Copy).then_inc(act_z, 1)
                tile_step(T0["mixout"] + j, 0, evac_y)
            sum_squares("mix_end", yacc, ready=lambda k: act.wait_ge(act_z, Z0["mixout"] + k + 1))

            sum_squares("ffn2", x, ready=lambda k: act.wait_ge(x_done, XDONE["ffn2"] - KC + k + 1))
            modulated("ffn2", MOD_OUT["ada"] + 48)
            units("ffn2")
            sum_squares("ffn2_end", yacc, ready=added("ffn2"))

            act.wait_ge(ld_ctx, 16)
            sum_squares("ctx", ctxx, CTX)
            modulated("ctx", MOD_OUT["ctx"], CTX)
            sum_squares("even", x, ready=lambda k: act.wait_ge(x_done, XDONE["even"] - KC + k + 1))
            t = T0["evenin"]
            g = GROUPS_BEFORE[t]
            hi(t + 2)
            act.wait_ge(m2_pad, 1)
            act.wait_ge(group_done, g + 1)
            nc.scalar.activation(kall[:, 0:CTX], G[:, 0, 0:CTX], ACT.Copy).then_inc(act_z, 1)
            act.wait_ge(group_done, g + 2)
            nc.scalar.activation(vz[:, 0:4, 64:128], G[:, 1, 0:CTX].rearrange("p (t n) -> p t n", n=64),
                                 ACT.Copy).then_inc(act_z, 1)
            modulated("even", MOD_OUT["mod0"])
            act.wait_ge(group_done, g + 3)
            nc.scalar.activation(kall[:, CTX:SK], G[:, 2], ACT.Copy).then_inc(act_z, 1)
            act.wait_ge(group_done, g + 4)
            nc.scalar.activation(vz[:, 4:12, 64:128], G[:, 3].rearrange("p (t n) -> p t n", n=64),
                                 ACT.Copy).then_inc(act_z, 1)

            def head_norm(idx, src, n, ready):
                act.wait_ge(act_z, ready)
                if idx:
                    act.wait_ge(m2_kn, idx)
                nc.scalar.activation(nt[:, 0, 0:n], src, ACT.Square).then_inc(m2_ssq, 1)
                act.wait_ge(m2_ssp, idx + 1)
                nc.scalar.activation(root[:, 0:n], Dn[:, 0, 0:n], ACT.Sqrt, bias=misc[:, 0:1],
                                     scale=1.0 / 64).then_inc(m2_srt, 1)
            head_norm(0, kall[:, 0:CTX], CTX, Z0["evenin"] + 1)
            head_norm(1, kall[:, CTX:SK], S, Z0["evenin"] + 3)
            for j in range(4):
                def evac(c, j=j):
                    g = 2 * j + c
                    dst = q2[:, g] if g < 4 else p2[:, g - 4, 8:8 + S]
                    nc.scalar.activation(dst, G[:, g % 4], ACT.Copy).then_inc(act_z, 1)
                tile_step(t + 1 + j, 0, evac)
                if j in (1, 2):
                    for m in (2 * j - 2, 2 * j - 1):
                        head_norm(2 + m, q2[:, m], S, Z0["evenin"] + 5 + m)
            for g in range(4):
                act.wait_ge(m2_pw, g + 1)
                if g:
                    act.wait_ge(m2_pool, g)
                col = COL["pool_scale"] + g
                nc.scalar.activation(root[:], G[:, g], ACT.Copy, scale=pv[:, col:col + 1]).then_inc(m2_ps, 1)

            def exps2(n):
                act.wait_ge(m2_nm, n + 1)
                if n >= 3:
                    act.wait_ge(m2_tr, n - 2)
                b = 2 * (n % 2)
                nc.scalar.activation(pexp2[:, n % 3], G[:, b:b + 2].rearrange("p a b -> p (a b)")[:, 0:SK], ACT.Exp,
                                     bias=stat[:, 1, n:n + 1], accum_out=stat[:, 2, n:n + 1]).then_inc(m2_exp, 1)

            def weights_t2(n):
                act.wait_ge(m2_tr, n + 1)
                if n >= 2:
                    act.wait_ge(m2_pv, n - 1)
                nc.scalar.activation(wt2[:, n % 2],
                                     Dn[:, 0:2].rearrange("p a b -> p (a b)")[:, 0:SK].rearrange("p (k q) -> p k q", q=P),
                                     ACT.Copy).then_inc(m2_wt, 1)

            def heads_out(c):
                act.wait_ge(m2_pv, 8 * c + 8)
                nc.scalar.activation(a_hi[:, c], Dn[:, 2 + c % 2], ACT.Copy).then_inc(m2_ohi, 1)
            for n in range(36):
                if n < 32:
                    exps2(n)
                if 2 <= n < 34:
                    weights_t2(n - 2)
                if n >= 11 and n % 8 == 3:
                    heads_out(n // 8 - 1)
            for j in range(4):
                hi(T0["evenout"] + j + 2)

            for l in range(2):
                stage = f"moe{l}"
                sum_squares(stage, x, ready=lambda k: act.wait_ge(x_done, XDONE[stage] - KC + k + 1))
                modulated(stage, MOD_OUT[f"mod{l}"] + 24)
                act.wait_ge(ld_rw[l], 16)
                nc.scalar.activation(rw_hi[:], rw[:], ACT.Copy).then_inc(rt_w, 1)
                act.wait_ge(rt_d1, l + 1)
                nc.scalar.activation(rt[:, 96:112], rt[:, 96:112], ACT.Exp).then_inc(rt_exp1, 1)
                act.wait_ge(rt_d2, l + 1)
                nc.scalar.activation(rt[:, 116:120], rt[:, 116:120], ACT.Exp).then_inc(rt_exp2, 1)
                act.wait_ge(rt_comb, l + 1)
                for b in range(4):
                    act.dma_start(comb_dram[l * EXPERTS:(l + 1) * EXPERTS, :]
                                  .rearrange("e (t b j) -> b e t j", b=4, j=32)[b],
                                  comb_t[32 * b:32 * b + EXPERTS]).then_inc(rt_store, 16)
                units(stage)
                if l == 1:
                    break
                sum_squares("odd", x, ready=lambda k: act.wait_ge(x_done, XDONE["odd"] - KC + k + 1))
                modulated("odd", MOD_OUT["mod1"])
                act.wait_ge(m3_pad, 1)

                def evac_odd(j):
                    def go(c):
                        g = 2 * j + c
                        src = G[:, g % 4]
                        if g < 4:
                            dst = u3[:, g]
                        elif g < 8:
                            dst = v3[:, 2 * c:2 * c + 2, 256 * (j - 2):256 * (j - 1)]
                            src = src.rearrange("p (t n) -> p t n", n=256)
                        elif g < 12:
                            dst = z3[:, g - 8, 1:1 + S]
                        else:
                            dst = (bg3, cg3)[(g - 12) // 4][:, g % 4]
                        nc.scalar.activation(dst, src, ACT.Copy).then_inc(act_z, 1)
                    return go
                for j in range(10):
                    tile_step(T0["oddin"] + j, 0, evac_odd(j))
                    if j == 5:
                        act.wait_ge(m3_ss, 4)
                        nc.scalar.activation(stat[:, 1, 0:16], stat[:, 0, 0:16], ACT.Sqrt, bias=misc[:, 0:1],
                                             scale=1.0 / P).then_inc(m3_srt, 1)
                for j in range(4):
                    hi(T0["oddout"] + j + 2)

        @block.vector
        def _(dve):
            V = nc.vector
            chain = [0]

            def link(ins):
                chain[0] += 1
                ins.then_inc(dve_chain, 1)
                dve.wait_ge(dve_chain, chain[0])

            def mod_multiply(matrix, r, q, fill):
                c = MOD_COND[matrix]
                dve.wait_ge(mod_full[r], fill)
                if not isinstance(q, int) or q:
                    dve.wait_ge(mod_red, q)
                V.tensor_tensor(prod, mod_raw[:, r], cond[:, c:c + KC].unsqueeze(2).to_broadcast([P, KC, P]),
                                ALU.mult).then_inc(mod_mul, 1)

            def mod_reduce(r, q):
                dve.wait_ge(mod_mul, q + 1)
                V.tensor_reduce(red[:, r], prod.rearrange("p k n -> p n k"), AX.X, ALU.add).then_inc(mod_red, 1)

            def mod_bias(matrix, n, batch, col):
                dve.wait_ge(mod_sum, batch + 1)
                V.tensor_tensor(mods[:, bass.ds(col + MOD_OUT[matrix], n)], Dn[:, M, 0:n],
                                pv[:, bass.ds(col + MOD_BIAS[matrix], n)], ALU.add).then_inc(mod_out, 1)

            def norm_inverse(name, n=S):
                q = NORM[name][0]
                dve.wait_ge(act_root, q + 1)
                V.reciprocal(rinv[:, 0:n], root[:, 0:n]).then_inc(dve_rinv, 1)
                dve.wait_ge(dve_rinv, q + 1)

            def modulated(name, src, scale_col, gain_col, n=S):
                m = NORM[name][1]
                V.scalar_tensor_tensor(acol[:, KC * m:KC * m + KC], mods[:, scale_col:scale_col + KC], 1.0,
                                       pv[:, gain_col:gain_col + KC], ALU.add, ALU.mult).then_inc(dve_cols, 1)
                norm_inverse(name, n)

                def low(k):
                    dve.wait_ge(act_ahi, KC * m + k + 1)
                    V.tensor_tensor(a_lo[:, k, 0:n], nt[:, 2 + k % 2, 0:n], a_hi[:, k, 0:n],
                                    ALU.subtract).then_inc(dve_alo, 1)
                for k in range(KC):
                    if k >= 2:
                        dve.wait_ge(dve_alo, KC * m + k - 1)
                    V.tensor_tensor(nt[:, 2 + k % 2, 0:n], src[:, k], rinv[:, 0:n], ALU.mult).then_inc(dve_t, 1)
                    if k:
                        low(k - 1)
                low(KC - 1)

            def end_norm(name, s, gate_col, gain_col, weight):
                link(V.scalar_tensor_tensor(gcol[:, KC * s:KC * s + KC], mods[:, gate_col:gate_col + KC], weight,
                                            pv[:, gain_col:gain_col + KC], ALU.mult, ALU.mult))
                norm_inverse(name)
                V.tensor_tensor(yacc, yacc, rinv[:].unsqueeze(1).to_broadcast([P, KC, S]), ALU.mult).then_inc(dve_yn, 1)
                dve.wait_ge(dve_yn, s + 1)
                for k in range(KC):
                    V.scalar_tensor_tensor(x[:, k], yacc[:, k], gcol[:, KC * s + k:KC * s + k + 1], x[:, k],
                                           ALU.mult, ALU.add).then_inc(x_done, 1)

            def unit(stage, i):
                t, u = T0[stage], i + UNIT0[stage]
                g = 12 * i + GROUPS_BEFORE[t]
                n = MOD_PER_UNIT[stage]
                moe = stage[:3] == "moe"
                if n:
                    matrix, col = MOD_LOOP[stage]
                    batch, q = i + MB0[stage], i * n + MQ0[stage]
                    fill = lambda r: 16 * i + 16 * (mod_fills(stage, r) + 1)
                    dve.wait_ge(mod_sum, batch)
                    for r in range(n):
                        mod_multiply(matrix, r, q + r, fill(r))
                        mod_reduce(r, q + r)
                if moe:
                    e = i + EXPERTS * (stage == "moe1")
                    dve.wait_ge(comb_full, 16 * e + 16)
                for c in range(2):
                    if moe:
                        dve.wait_ge(act_silu, 2 * u + (PRIME_SILU + c + 1))
                        V.tensor_tensor(sg[:, c], sg[:, c], comb_row, ALU.mult).then_inc(dve_comb, 1)
                for c in range(2):
                    if moe:
                        dve.wait_ge(dve_comb, 2 * e + (c + 2 + (stage == "moe1")))
                    else:
                        dve.wait_ge(act_silu, 2 * u + (PRIME_SILU + c + 1))
                    dve.wait_ge(group_done, g + (2 + c + 1))
                    dve.wait_ge(dve_hlo, 2 * u + 1) if c == 0 else None
                    V.tensor_tensor(hid[:, c], G[:, 2 + c], sg[:, c], ALU.mult).then_inc(dve_gu, 1)
                    dve.wait_ge(act_hhi, 2 * u + (c + 1))
                    V.tensor_tensor(h_lo[:, c], hid[:, c], h_hi[:, c], ALU.subtract).then_inc(dve_hlo, 1)
                for m in range(KC):
                    dve.wait_ge(group_done, g + (4 + m + 1))
                    dve.wait_ge(down_added, 8 * u + (m + 1))
                    V.tensor_tensor(yacc[:, m], yacc[:, m], down_bank(m), ALU.add).then_inc(down_added, 1)
                if n:
                    mod_bias(matrix, n, batch, i * n + col)

            def units(stage):
                with dve.Fori(0, UNITS[stage]) as i:
                    unit(stage, i)
                dve.wait_ge(down_added, PRIME_ADD + 8 * (UNIT0[stage] + UNITS[stage]))

            def split(src, k):
                link(V.tensor_copy(a_hi[:, k], src))
                return V.tensor_tensor(a_lo[:, k], src, a_hi[:, k], ALU.subtract)

            link(V.memset(misc[:, 0:1], EPS))
            V.memset(misc[:, 60:61], 0.0).then_inc(dve_gu, PRIME_GU)
            V.memset(misc[:, 61:62], 0.0).then_inc(down_added, PRIME_ADD)
            V.memset(misc[:, 63:64], 0.0).then_inc(dve_hlo, 1)
            V.memset(misc[:, 59:60], 0.0).then_inc(dve_comb, 1)
            dve.wait_ge(ld_pv, 16)
            dve.wait_ge(ld_row, 48)
            link(V.tensor_tensor(nt[:, 2, 0:128], nt[:, 1, 0:128], nt[:, 1, 128:256], ALU.mult))
            V.tensor_reduce(misc[:, 2:4], nt[:, 2, 0:128].rearrange("p (m d) -> p m d", m=2), AX.X,
                            ALU.add).then_inc(lam_sum, 1)
            link(V.tensor_copy(nt[:, 3], nt[:, 0].bitcast(I32)))
            fr = COL["inv_freq"]
            link(V.tensor_scalar(nt[:, 3], nt[:, 3], pv[:, fr:fr + 1], None, ALU.mult))
            C1 = 6.28125
            C2 = 0.0019350051879882812
            C3 = 6.283185307179586 - C1 - C2
            MAGIC = 12582912.0
            PI = 3.1415925
            link(V.tensor_scalar(nt[:, 2], nt[:, 3], 0.15915494309189535, MAGIC, ALU.mult, ALU.add))
            link(V.tensor_scalar(nt[:, 2], nt[:, 2], MAGIC, None, ALU.subtract))
            for part in (C1, C2, C3):
                link(V.scalar_tensor_tensor(nt[:, 3], nt[:, 2], -part, nt[:, 3], ALU.mult, ALU.add))
            V.tensor_scalar(rope[:, 1], nt[:, 3], PI, -PI, ALU.min, ALU.max).then_inc(rope1_ang, 1)
            link(V.tensor_scalar(nt[:, 3], nt[:, 3], 1.5707963267948966, None, ALU.add))
            link(V.tensor_scalar(nt[:, 2], nt[:, 3], 3.141592653589793, 6.283185307179586, ALU.is_gt, ALU.mult))
            link(V.tensor_tensor(nt[:, 3], nt[:, 3], nt[:, 2], ALU.subtract))
            V.tensor_scalar(rope[:, 0], nt[:, 3], PI, -PI, ALU.min, ALU.max).then_inc(rope1_ang, 1)
            la = COL["lam"]
            link(V.tensor_scalar(misc[:, 40:48], pv[:, la:la + 8], -1.0, None, ALU.mult))
            V.tensor_tensor(misc[:, 16:24], pv[:, la:la + 8], misc[:, 40:48], ALU.max).then_inc(lam_sum, 1)
            link(V.tensor_scalar(misc[:, 40:48], misc[:, 40:48], 0.0, None, ALU.max))
            dve.wait_ge(sp_exp, 1)
            y, z, z2, s = misc[:, 16:24], misc[:, 24:32], misc[:, 32:40], misc[:, 48:56]
            link(V.tensor_scalar(z, y, 2.0, None, ALU.add))
            link(V.reciprocal(z, z))
            link(V.tensor_tensor(z, z, y, ALU.mult))
            link(V.tensor_tensor(z2, z, z, ALU.mult))
            link(V.tensor_scalar(s, z2, 1.0 / 19, None, ALU.mult))
            for n in range(8, 0, -1):
                link(V.scalar_tensor_tensor(s, s, 1.0 / (2 * n + 1), z2, ALU.add, ALU.mult))
            link(V.scalar_tensor_tensor(s, s, 1.0, z, ALU.add, ALU.mult))
            link(V.scalar_tensor_tensor(s, s, 2.0, misc[:, 40:48], ALU.mult, ALU.add))
            link(V.tensor_scalar(misc[:, 24:32], s, -8.0, None, ALU.mult))
            link(V.tensor_scalar(misc[:, 32:40], s, 8.0, None, ALU.mult))
            dve.wait_ge(lam_exp, 1)
            link(V.tensor_scalar(misc[:, 4:5], misc[:, 3:4], LAMBDA_INIT, None, ALU.subtract))
            link(V.tensor_tensor(misc[:, 4:5], misc[:, 4:5], misc[:, 2:3], ALU.subtract))
            link(V.tensor_scalar(misc[:, 5:6], pv[:, COL["subln"]:COL["subln"] + 1], 1.0 - LAMBDA_INIT, None, ALU.mult))
            dve.wait_ge(cond_done, 2)
            V.tensor_tensor(cond_split[:, :, 1], cond[:], cond_split[:, :, 0], ALU.subtract).then_inc(cond_done, 1)
            q = 0
            for b, (matrix, col, n) in enumerate(MOD_FIRST):
                if b:
                    dve.wait_ge(mod_sum, b)
                for r in MOD_VECTOR[b]:
                    mod_multiply(matrix, r, q, 16 * (1 + sum(k > r for _, _, k in MOD_FIRST[:b])))
                    mod_reduce(r, q)
                    q += 1
                mod_bias(matrix, n, b, col)
            dve.wait_ge(mod_out, len(MOD_FIRST))

            NG = COL["norm_g"]
            V.memset(yacc, 0.0).then_inc(yacc_zero, 1)
            dve.wait_ge(yacc_zero, 1)
            modulated("ffn1", x, 8, NG)
            units("ffn1")
            dve.wait_ge(mod_out, MB0["ffn2"])
            end_norm("ffn1_end", 0, 16, NG + 8, 0.5)
            dve.wait_ge(x_done, XDONE["mix"])

            V.memset(misc[:, 58:59], 0.0).then_inc(arena_free, 1)
            link(V.memset(xr1[:, :, 0:2], 0.0))
            V.memset(xr1[:, :, 2 + S:XRW], 0.0).then_inc(m1_pad, 1)
            modulated("mix", x, 24 + 8, NG + 16)
            dve.wait_ge(act_z, 20)
            dve.wait_ge(m1_pad, 1)

            def convolve(c):
                cw, cb = COL["conv_w"] + c, COL["conv_b"] + c
                e0 = xc1[c % 2]
                link(V.tensor_scalar(e0, xr1[:, c, 0:S], pv[:, cw:cw + 1], pv[:, cb:cb + 1], ALU.mult, ALU.add))
                for tap in range(1, 4):
                    ins = V.scalar_tensor_tensor(e0, xr1[:, c, tap:tap + S], pv[:, cw + 4 * tap:cw + 4 * tap + 1], e0,
                                                 ALU.mult, ALU.add)
                    if tap < 3:
                        link(ins)
                ins.then_inc(m1_xc, 1)
                dve.wait_ge(m1_xc, c + 1)
            convolve(0)
            for c in range(4):
                e0 = xc1[c % 2]
                for d in range(2):
                    a = (root, rinv)[d]
                    dve.wait_ge(m1_at, 4 * c + 2 * d + 2)
                    link(V.tensor_tensor(e1, a[:], a[:], ALU.mult))
                    link(V.scalar_tensor_tensor(nt[:, d], e1, 1.0, nt[:, d], ALU.add, ALU.mult))
                    V.tensor_scalar(nt[:, d], nt[:, d], 1e-30, None, ALU.max).then_inc(m1_m, 1)
                if c < 3:
                    convolve(c + 1)
                for d in range(2):
                    a = (root, rinv)[d]
                    link(V.tensor_tensor(nt[:, 2 + d], nt[:, 2 + d], e0, ALU.mult))
                    dve.wait_ge(m1_sqrt, 2 * c + d + 1)
                    link(V.tensor_tensor(nt[:, d], nt[:, d], nt[:, 2 + d], ALU.mult))
                    if d == 0:
                        link(V.tensor_tensor_scan(nt[:, 2], a[:], nt[:, 0], 0.0, ALU.mult, ALU.add))
                    else:
                        link(V.tensor_tensor_scan(nt[:, 3, ::-1], a[:, ::-1], nt[:, 1, ::-1], 0.0, ALU.mult, ALU.add))
                link(V.tensor_tensor(nt[:, 2], nt[:, 2], nt[:, 3], ALU.add))
                dve.wait_ge(m1_gelu, 1)
                link(V.tensor_tensor(e1, nt[:, 2], yr1[:, c], ALU.mult))
                split(e1, 4 + c).then_inc(m1_rec, 1)
            dve.wait_ge(m1_rec, 4)
            dve.wait_ge(group_done, GROUPS_BEFORE[T0["mixout"]])
            for j, (c, _, dst) in enumerate(MODCTX):
                pr = Dn[:, 2, 4 * j:4 * j + 4].rearrange("p (c n) -> p c n", n=2)
                link(V.tensor_reduce(mods[:, dst:dst + 2], pr, AX.X, ALU.add))
                mb = COL["mod_b"] + 2 * c
                ins = V.tensor_tensor(mods[:, dst:dst + 2], mods[:, dst:dst + 2], pv[:, mb:mb + 2], ALU.add)
                ins.then_inc(modctx_out, 1)
            dve.wait_ge(modctx_out, len(MODCTX))

            def rotate(z, src, tmp, n, ready, value, done, cols=slice(0, S)):
                dve.wait_ge(ready, value)
                link(V.tensor_tensor(tmp, src, rope[:, 1, cols], ALU.mult))
                link(V.tensor_tensor(z, z, rope[:, 0, cols], ALU.mult))
                V.tensor_tensor(z, z, tmp, ALU.add).then_inc(done, 1)
            dve.wait_ge(rope1_tab, 2)
            for idx in range(8):
                if idx >= 4:
                    dve.wait_ge(m1_rope, idx - 3)
                rotate((q1, k1)[idx // 4][:, idx % 4], G[:, idx % 4], nt[:, idx % 4], S, m1_rot, idx + 1, m1_rope)

            def maxima(n):
                dve.wait_ge(m1_qk, 2 * n + 2)
                b = 2 * (n % 2)
                V.tensor_reduce(stat[:, 1, 2 * n:2 * n + 2], G[:, b:b + 2], AX.X, ALU.max,
                                negate=True).then_inc(m1_nm, 1)

            def mix_weights(n):
                dve.wait_ge(m1_exp, 2 * n + 2)
                c, b = 2 * n, 2 * (n % 3)
                link(V.reciprocal(stat[:, 3, c:c + 2], stat[:, 2, c:c + 2]))
                link(V.tensor_tensor(stat[:, 4, c:c + 1], stat[:, 3, c + 1:c + 2], misc[:, 4:5], ALU.mult))
                if n >= 2:
                    dve.wait_ge(m1_tr, n - 1)
                w = wsm1[:, n % 2]
                link(V.tensor_scalar(w, pexp1[:, b], stat[:, 3, c:c + 1], None, ALU.mult))
                V.scalar_tensor_tensor(w, pexp1[:, b + 1], stat[:, 4, c:c + 1], w, ALU.mult, ALU.add).then_inc(m1_w, 1)
            for n in range(17):
                if n < 16:
                    maxima(n)
                if n:
                    mix_weights(n - 1)
            for h in range(4):
                dve.wait_ge(m1_srt, h + 1)
                link(V.reciprocal(pexp1[:, h], pexp1[:, h]))
                link(V.tensor_tensor(q1[:, h], q1[:, h], pexp1[:, h], ALU.mult))
                link(V.tensor_scalar(q1[:, h], q1[:, h], misc[:, 5:6], None, ALU.mult))
                split(q1[:, h], h).then_inc(m1_sub, 1)
            end_norm("mix_end", 1, 24 + 16, NG + 24, 1.0)
            dve.wait_ge(x_done, XDONE["ffn2"])

            V.memset(yacc, 0.0).then_inc(yacc_zero, 1)
            dve.wait_ge(yacc_zero, 2)
            V.memset(misc[:, 58:59], 0.0).then_inc(arena_back, 1)
            modulated("ffn2", x, 48 + 8, NG + 32)
            units("ffn2")
            dve.wait_ge(mod_out, MB0["moe0"])
            end_norm("ffn2_end", 2, 48 + 16, NG + 40, 0.5)
            dve.wait_ge(x_done, XDONE["even"])

            V.memset(misc[:, 58:59], 0.0).then_inc(arena_free, 1)
            link(V.memset(p2, 0.0))
            V.memset(vz, 0.0).then_inc(m2_pad, 1)
            N1 = COL["norm1"]
            dve.wait_ge(ld_ctx, 16)
            modulated("ctx", ctxx, MOD_OUT["ctx"] + 8, N1, CTX)
            dve.wait_ge(group_done, GROUPS_BEFORE[T0["evenin"]] + 2)
            modulated("even", x, MOD_OUT["mod0"] + 8, N1)
            dve.wait_ge(ld_rope2, 16)

            def head_norm(idx, z, n, gain, turned):
                dve.wait_ge(m2_srt, idx + 1)
                link(V.reciprocal(rinv[:, 0:n], root[:, 0:n]))
                link(V.tensor_tensor(z, z, rinv[:, 0:n], ALU.mult))
                V.tensor_scalar(z, z, pv[:, gain:gain + 1], 0.125 if gain == COL["q_gain"] else 1.0, ALU.mult,
                                ALU.mult).then_inc(m2_kn, 1)
                dve.wait_ge(m2_kn, idx + 1)
                if turned:
                    rotate(z, Dn[:, 1], nt[:, 1], n, m2_rot, idx, m2_rope)
                    dve.wait_ge(m2_rope, idx)
            head_norm(0, kall[:, 0:CTX], CTX, COL["k_gain"], False)
            head_norm(1, kall[:, CTX:SK], S, COL["k_gain"], True)
            link(V.tensor_copy(kswap[0:64], kall[64:128]))
            V.tensor_copy(kswap[64:128], kall[0:64]).then_inc(m2_swap, 1)
            for m in range(4):
                head_norm(2 + m, q2[:, m], S, COL["q_gain"], True)
            dve.wait_ge(act_z, Z0["evenin"] + 12)
            dve.wait_ge(ld_even, 32)
            flat = nt[:].rearrange("p a b -> p (a b)")
            for g in range(4):
                src, width = p2[:, g], PW
                for lvl in range(g + 1):
                    step = 1 << lvl
                    dst = flat[:, 528 * (lvl % 2):528 * (lvl % 2) + 528]
                    width -= step
                    link(V.tensor_tensor(dst[:, 0:width], src[:, 0:width], src[:, step:step + width], ALU.add))
                    src = dst
                half = 1 << g
                s, d = src[:, 8 - half:8 - half + S], flat[:, 1056 + 0:1056 + S]
                if g:
                    dve.wait_ge(m2_pw, g)
                link(V.tensor_tensor(d, s, ic[:, g], ALU.mult))
                V.tensor_tensor(d, d, p2[:, g, 8:8 + S], ALU.subtract).then_inc(m2_d, 1)
                dve.wait_ge(m2_d, g + 1)
                dve.wait_ge(m2_ps, g + 1)
                split(root[:], 4 + g).then_inc(m2_pool, 1)
            dve.wait_ge(m2_pool, 4)

            def maxima2(n):
                dve.wait_ge(m2_qk, n + 1)
                b = 2 * (n % 2)
                V.tensor_reduce(stat[:, 1, n:n + 1], G[:, b:b + 2].rearrange("p a b -> p (a b)")[:, 0:SK], AX.X,
                                ALU.max, negate=True).then_inc(m2_nm, 1)

            def scale2(n):
                dve.wait_ge(m2_exp, n + 1)
                link(V.reciprocal(stat[:, 3, n:n + 1], stat[:, 2, n:n + 1]))
                V.tensor_scalar(pexp2[:, n % 3], pexp2[:, n % 3], stat[:, 3, n:n + 1], None, ALU.mult).then_inc(m2_w, 1)

            def heads_low(c):
                dve.wait_ge(m2_ohi, c + 1)
                V.tensor_tensor(a_lo[:, c], Dn[:, 2 + c % 2], a_hi[:, c], ALU.subtract).then_inc(m2_olo, 1)
            for n in range(38):
                if n < 32:
                    maxima2(n)
                if 1 <= n < 33:
                    scale2(n - 1)
                if n >= 13 and n % 8 == 5:
                    heads_low(n // 8 - 1)

            def project_residual(stage, gate_col):
                for k in range(KC):
                    dve.wait_ge(group_done, GROUPS_BEFORE[T0[stage]] + k + 1)
                    V.scalar_tensor_tensor(x[:, k], G[:, k % 4], mods[:, gate_col + k:gate_col + k + 1], x[:, k],
                                           ALU.mult, ALU.add).then_inc(x_done, 1)
            project_residual("evenout", MOD_OUT["mod0"] + 16)

            def first_of(oh, eq, tmp):
                link(V.tensor_scalar(tmp, eq[:, :, 0:1], -1.0, 1.0, ALU.mult, ALU.add))
                link(V.tensor_copy(oh[:, :, 0:1], eq[:, :, 0:1]))
                for j in range(1, 4):
                    link(V.tensor_tensor(oh[:, :, j:j + 1], eq[:, :, j:j + 1], tmp, ALU.mult))
                    if j < 3:
                        link(V.tensor_tensor(tmp, tmp, oh[:, :, j:j + 1], ALU.subtract))

            def router(l):
                def r3(at, n):
                    return rt[:, at:at + 4 * n].rearrange("p (t n) -> p t n", n=n)
                logit, gsh, gm = r3(0, 20), r3(96, 4), r3(112, 1)
                e2, gp, tmp = r3(116, 1), r3(120, 1), r3(124, 1)
                eq, gh, oh1, oh2, esel, m1, m2, msk = (r3(128, 4), r3(144, 4), r3(160, 4), r3(176, 4), r3(192, 4),
                                                       r3(208, 1), r3(212, 1), r3(216, 4))
                wide = rt[:, 232:296].rearrange("p (t g j) -> p t g j", g=4, j=4)

                def b(v, n=4):
                    return v.to_broadcast([P, TT, n])
                dve.wait_ge(ld_row, 48)
                dve.wait_ge(rt_logit, l + 1)
                link(V.tensor_tensor(logit, Dn[:, M, 0:80].rearrange("p (t n) -> p t n", n=20),
                                     rb[:, l].unsqueeze(1).to_broadcast([P, TT, 20]), ALU.add))
                lg = logit[:, :, 0:4]
                link(V.tensor_reduce(gm, lg, AX.X, ALU.max))
                V.tensor_tensor(gsh, lg, b(gm), ALU.subtract).then_inc(rt_d1, 1)
                link(V.tensor_tensor(eq, lg, b(gm), ALU.is_equal))
                first_of(gh, eq, tmp)
                le = logit[:, :, 4:20].rearrange("p t (g j) -> p t g j", j=4)
                link(V.tensor_tensor(wide, le, gh.unsqueeze(3).to_broadcast([P, TT, 4, 4]), ALU.mult))
                link(V.tensor_reduce(esel, wide.rearrange("p t g j -> p t j g"), AX.X, ALU.add))
                link(V.tensor_reduce(m1, esel, AX.X, ALU.max))
                link(V.tensor_tensor(eq, esel, b(m1), ALU.is_equal))
                first_of(oh1, eq, tmp)
                link(V.scalar_tensor_tensor(msk, oh1, -1e30, esel, ALU.mult, ALU.add))
                link(V.tensor_reduce(m2, msk, AX.X, ALU.max))
                link(V.tensor_tensor(eq, msk, b(m2), ALU.is_equal))
                first_of(oh2, eq, tmp)
                V.tensor_tensor(e2, m2, m1, ALU.subtract).then_inc(rt_d2, 1)
                dve.wait_ge(rt_exp1, l + 1)
                link(V.tensor_reduce(gp, gsh, AX.X, ALU.add))
                dve.wait_ge(rt_exp2, l + 1)
                link(V.scalar_tensor_tensor(tmp, e2, 1.0, gp, ALU.add, ALU.mult))
                link(V.reciprocal(tmp, tmp))
                link(V.tensor_tensor(oh1, oh1, b(tmp), ALU.mult))
                link(V.tensor_tensor(tmp, tmp, e2, ALU.mult))
                link(V.tensor_tensor(oh2, oh2, b(tmp), ALU.mult))
                link(V.tensor_tensor(oh1, oh1, oh2, ALU.add))
                link(V.memset(comb_pad, 0.0))
                link(V.tensor_tensor(comb_pad[:, :, 0:16].rearrange("p t (g j) -> p t g j", j=4),
                                     gh.unsqueeze(3).to_broadcast([P, TT, 4, 4]),
                                     oh1.unsqueeze(2).to_broadcast([P, TT, 4, 4]), ALU.mult))
                V.transpose(comb_t.rearrange("p t j -> p (t j)"), comb_pad.rearrange("p t j -> p (t j)")).then_inc(rt_comb, 1)
                dve.wait_ge(rt_comb, l + 1)
                V.memset(misc[:, 57:58], 0.0).then_inc(dve_comb, 1) if l == 1 else None

            N2 = COL["norm2"]
            for l in range(2):
                stage = f"moe{l}"
                dve.wait_ge(x_done, XDONE[stage])
                V.memset(yacc, 0.0).then_inc(yacc_zero, 1)
                dve.wait_ge(yacc_zero, 3 + l)
                if l == 0:
                    V.memset(misc[:, 58:59], 0.0).then_inc(arena_back, 1)
                modulated(stage, x, MOD_OUT[f"mod{l}"] + 32, N2 + 8 * l)
                dve.wait_ge(rt_w, 2 * l + 1)
                V.tensor_tensor(rw_lo[:], rw[:], rw_hi[:], ALU.subtract).then_inc(rt_w, 1)
                router(l)
                units(stage)
                for k in range(KC):
                    g = MOD_OUT[f"mod{l}"] + 40 + k
                    V.scalar_tensor_tensor(x[:, k], yacc[:, k], mods[:, g:g + 1], x[:, k],
                                           ALU.mult, ALU.add).then_inc(x_done, 1)
                if l == 1:
                    break
                dve.wait_ge(x_done, XDONE["odd"])
                dve.wait_ge(mod_out, MB0["moe0"] + UNITS["moe0"])
                V.memset(misc[:, 58:59], 0.0).then_inc(arena_free, 1)
                link(V.memset(z3[:, :, 0:1], 0.0))
                V.memset(z3[:, :, 1 + S:ZW], 0.0).then_inc(m3_pad, 1)
                modulated("odd", x, MOD_OUT["mod1"] + 8, N1 + 8)
                dve.wait_ge(act_z, Z0["oddin"] + 8)
                for t in range(TT):
                    link(V.tensor_tensor(nt[:, t], v3[:, t], v3[:, t], ALU.mult))
                    V.tensor_reduce(stat[:, 0, 4 * t:4 * t + 4], nt[:, t].rearrange("p (g n) -> p g n", n=P), AX.X,
                                    ALU.add).then_inc(m3_ss, 1)
                dve.wait_ge(m3_srt, 1)
                link(V.reciprocal(stat[:, 2, 0:16], stat[:, 1, 0:16]))
                for t in range(TT):
                    vt = v3[:, t].rearrange("p (g n) -> p g n", n=P)
                    V.tensor_tensor(vt, vt, stat[:, 2, 4 * t:4 * t + 4].unsqueeze(2).to_broadcast([P, 4, P]),
                                    ALU.mult).then_inc(m3_vn, 1)
                dve.wait_ge(ld_odd, 32)
                dve.wait_ge(m3_vn, 4)
                for g in range(4):
                    gain = COL["sg_gain"] + g
                    dve.wait_ge(m3_sg, g + 1)
                    if g >= 1:
                        dve.wait_ge(m3_y, g)
                    link(V.scalar_tensor_tensor(nt[:, 0].rearrange("p (n c) -> p n c", c=P),
                                                Dn[:, g].rearrange("p (n c) -> p n c", c=P), pv[:, gain:gain + 1],
                                                sgb[:, g].unsqueeze(1).to_broadcast([P, TT, P]), ALU.mult, ALU.add))
                    link(V.tensor_tensor(nt[:, 0], nt[:, 0], u3[:, g], ALU.mult))
                    link(V.tensor_copy(nt[:, 1], nt[:, 0])) if False else None
                    dve.wait_ge(group_done, GROUPS_BEFORE[T0["oddin"] + 10])
                    split(nt[:, 0], g).then_inc(m3_y, 1)
                dve.wait_ge(act_z, Z0["oddin"] + 20)
                for c in range(4):
                    w = COL["conv_w2"] + c
                    dve.wait_ge(m3_y, 4 + c)
                    link(V.tensor_tensor(z3[:, c, 1:1 + S], z3[:, c, 1:1 + S], cg3[:, c], ALU.mult))
                    link(V.tensor_scalar(nt[:, 0], z3[:, c, 0:S], pv[:, w:w + 1], None, ALU.mult))
                    for tap in (1, 2):
                        link(V.scalar_tensor_tensor(nt[:, 0], z3[:, c, tap:tap + S], pv[:, w + 4 * tap:w + 4 * tap + 1],
                                                    nt[:, 0], ALU.mult, ALU.add))
                    link(V.tensor_tensor(nt[:, 0], nt[:, 0], bg3[:, c], ALU.mult))
                    split(nt[:, 0], 4 + c).then_inc(m3_y, 1)
                project_residual("oddout", MOD_OUT["mod1"] + 16)

        @block.tensor
        def _(pe):
            mm = nc.tensor.matmul

            def product(out, weights, acts, first=True, last=True):
                (wh, wl), (ah, al) = weights, acts
                mm(out, wh, ah, start=first, stop=False)
                mm(out, wl, ah, start=False, stop=False)
                return mm(out, wh, al, start=False, stop=last)

            def mod_sums(n, batch, q):
                pe.wait_ge(mod_red, q + n)
                if not isinstance(batch, int) or batch:
                    pe.wait_ge(mod_out, batch)
                for r in range(n):
                    ins = mm(Dn[:, M, r:r + 1], red[:, r], ones[:, 0:1], start=True, stop=True)
                ins.then_inc(mod_sum, 1)

            def sum_squares(name, n=S):
                q = NORM[name][0]
                for k in range(KC):
                    pe.wait_ge(act_sq, KC * q + k + 1)
                    mm(sum_bank(name)[:, 0:n], ones[:], nt[:, k % 2, 0:n], start=(k == 0), stop=(k == KC - 1)).then_inc(pe_ss, 1)

            def in_pair(slot, outs, ready):
                for k in range(KC):
                    pe.wait_ge(dve_alo, ready + k + 1)
                    for c in range(2):
                        cs = slice(c * P, c * P + P)
                        ins = product(outs[c], (w_in(w_hi, slot)[:, k, cs], w_in(w_lo, slot)[:, k, cs]),
                                      (a_hi[:, k], a_lo[:, k]), k == 0, k == KC - 1)
                        if k == KC - 1:
                            ins.then_inc(group_done, 1)

            def in_group(slot, c, out, ready=None, n=S):
                for k in range(KC):
                    if ready is not None:
                        pe.wait_ge(dve_alo, ready + k + 1)
                    cs = slice(c * P, c * P + P)
                    ins = product(out, (w_in(w_hi, slot)[:, k, cs], w_in(w_lo, slot)[:, k, cs]),
                                  (a_hi[:, k, 0:n], a_lo[:, k, 0:n]), k == 0, k == KC - 1)
                return ins

            def token_group(slot, out, t, cs):
                ts = slice(t * P, t * P + P)
                for k in range(KC):
                    ins = product(out, (a_hi[:, k, ts], a_lo[:, k, ts]),
                                  (w_in(w_hi, slot)[:, k, cs], w_in(w_lo, slot)[:, k, cs]), k == 0, k == KC - 1)
                return ins

            def unit(stage, i):
                t, u = T0[stage], i + UNIT0[stage]
                a_ready = KC * NORM[stage][1]
                pe.wait_ge(weight_lo, 3 * i + (t + 1))
                pe.wait_ge(act_silu, 2 * u + 2)
                pe.wait_ge(down_added, 8 * u + (PRIME_ADD - 8 + 5))
                in_pair(t % RING, (G[:, 0], G[:, 1]), a_ready)
                pe.wait_ge(weight_lo, 3 * i + (t + 2))
                for c in range(2):
                    pe.wait_ge(dve_gu, 2 * u + (c + 1))
                    in_group((t + 1) % RING, c, G[:, 2 + c]).then_inc(group_done, 1)
                pe.wait_ge(weight_lo, 3 * i + (t + 3))
                s = (t + 2) % RING
                for ms in (range(5), range(5, KC)):
                    for k in range(2):
                        for m in ms:
                            if k == 0:
                                if m < 3:
                                    pe.wait_ge(down_added, 8 * u + (PRIME_ADD - 8 + m + 6))
                                elif m < 5:
                                    pe.wait_ge(act_silu, 2 * u + (PRIME_SILU + 2))
                                else:
                                    pe.wait_ge(down_added, 8 * u + (PRIME_ADD + m - 4))
                            ws = slice(m * P, m * P + P)
                            wh, wl = w_down(w_hi, s)[:, k, ws], w_down(w_lo, s)[:, k, ws]
                            if k == 0 or ms[0]:
                                if k == 0 and m == 0:
                                    pe.wait_ge(dve_hlo, 2 * u + 2)
                                ins = product(down_bank(m), (wh, wl), (h_hi[:, k], h_lo[:, k]), k == 0, k == 1)
                                if k == 1:
                                    ins.then_inc(group_done, 1)
                            else:
                                if m == 0:
                                    pe.wait_ge(act_hhi, 2 * u + 2)
                                mm(down_bank(m), wh, h_hi[:, 1], start=False, stop=False)
                                mm(down_bank(m), wl, h_hi[:, 1], start=False, stop=False)
                        if k == 1 and not ms[0]:
                            pe.wait_ge(dve_hlo, 2 * u + 3)
                            for m in ms:
                                mm(down_bank(m), w_down(w_hi, s)[:, 1, m * P:m * P + P], h_lo[:, 1], start=False,
                                   stop=True).then_inc(group_done, 1)
                n = MOD_PER_UNIT[stage]
                if n:
                    mod_sums(n, i + MB0[stage], i * n + MQ0[stage])

            def units(stage):
                with pe.Fori(0, UNITS[stage]) as i:
                    unit(stage, i)

            def projection(stage, g0, z, j, groups=None, ready=None):
                t = T0[stage] + j
                pe.wait_ge(weight_lo, t + 1)
                if ready is not None:
                    in_pair(t % RING, (G[:, 0], G[:, 1]), ready)
                    return
                for c in range(2):
                    g = g0 + c
                    if g >= 4:
                        pe.wait_ge(*z(g - 3))
                    if groups:
                        groups(t % RING, c, G[:, g % 4]).then_inc(group_done, 1)
                    else:
                        in_group(t % RING, c, G[:, g % 4]).then_inc(group_done, 1)

            pe.wait_ge(ld_const, 80)
            q = 0
            for b, (_, _, n) in enumerate(MOD_FIRST):
                if b:
                    pe.wait_ge(mod_out, b)
                else:
                    pe.wait_ge(cond_done, 1)
                for r in range(n):
                    if r in MOD_VECTOR[b]:
                        continue
                    pe.wait_ge(mod_full[r], 16 * (1 + sum(k > r for _, _, k in MOD_FIRST[:b])))
                    for k in range(KC):
                        mm(Dn[:, M, r:r + 1], mod_raw[:, r, k], cond[:, k:k + 1], start=(k == 0), stop=(k == KC - 1))
                for r in MOD_VECTOR[b]:
                    q += 1
                    pe.wait_ge(mod_red, q)
                    ins = mm(Dn[:, M, r:r + 1], red[:, r], ones[:, 0:1], start=True, stop=True)
                ins.then_inc(mod_sum, 1)
                if b == 1:
                    sum_squares("ffn1")
            units("ffn1")
            sum_squares("ffn1_end")

            sum_squares("mix")

            def values1(slot, c, out):
                for t in (2 * c, 2 * c + 1):
                    ins = token_group(slot, out[:, 256 * (t % 2):256 * (t % 2) + 256], t, slice(0, 256))
                return ins
            for j in range(10):
                projection("mixin", 2 * j, lambda n: (act_z, Z0["mixin"] + n), j,
                           values1 if j in (4, 5) else None, KC * NORM["mix"][1] if j == 0 else None)
            pe.wait_ge(ld_mix, 16)
            pe.wait_ge(act_z, 20)

            def modctx(j):
                _, cc, _ = MODCTX[j]
                t = T0["modctx"] + j
                pe.wait_ge(weight_lo, t + 1)
                for c in range(2):
                    out = Dn[:, 2, 4 * j + 2 * c:4 * j + 2 * c + 2]
                    for k in range(KC):
                        for n, w in enumerate((w_hi, w_lo)):
                            ins = mm(out, w_in(w, t % RING)[:, k, c * P:c * P + P], cond_split[:, cc + k],
                                     start=(k == 0 and n == 0), stop=(k == KC - 1 and n == 1))
                    ins.then_inc(group_done, 1)
            for c in range(4):
                pe.wait_ge(m1_xc, c + 1)
                for dg in range(4):
                    if c:
                        pe.wait_ge(m1_sig, 4 * (c - 1) + dg + 1)
                    mm(G[:, dg], bd[:, dg, c * P:c * P + P], xc1[c % 2], start=True, stop=True).then_inc(m1_gate, 1)
                for j in range(sum(MODCTX_STEPS[:c]), sum(MODCTX_STEPS[:c + 1])):
                    modctx(j)
            for idx in range(8):
                if idx < 4:
                    pe.wait_ge(m1_sig, 12 + idx + 1)
                else:
                    pe.wait_ge(m1_rope, idx - 3)
                mm(G[:, idx % 4], rot1[:], (q1, k1)[idx // 4][:, idx % 4], start=True, stop=True).then_inc(m1_rot, 1)
            pe.wait_ge(m1_rope, 8)

            def scores(n):
                h, i = n // 4, n % 4
                if n >= 2:
                    pe.wait_ge(m1_exp, 2 * n - 2)
                for m in range(2):
                    ps = slice(64 * m, 64 * m + 64)
                    mm(G[:, 2 * (n % 2) + m], q1[ps, h, i * P:(i + 1) * P], k1[ps, h], start=True,
                       stop=True).then_inc(m1_qk, 1)

            def turn(n):
                pe.wait_ge(m1_w, n + 1)
                if n >= 2:
                    pe.wait_ge(m1_wt, n - 1)
                for k in range(4):
                    ins = nc.tensor.transpose(Dn[:, n % 2, k * P:(k + 1) * P], wsm1[:, n % 2, k * P:(k + 1) * P], ident[:])
                ins.then_inc(m1_tr, 1)

            def values_sum(n):
                h, i = n // 4, n % 4
                pe.wait_ge(m1_wt, n + 1)
                if i == 0 and h >= 2:
                    pe.wait_ge(m1_o, h - 1)
                for k in range(4):
                    ins = mm(Dn[:, 2 + h % 2, i * P:(i + 1) * P], v1[:, k, h * P:(h + 1) * P], wt1[:, n % 2, k],
                             start=(k == 0), stop=(k == 3))
                ins.then_inc(m1_pv, 1)
            for n in range(19):
                if n < 16:
                    scores(n)
                if 2 <= n < 18:
                    turn(n - 2)
                if n >= 3:
                    values_sum(n - 3)
            for h in range(4):
                pe.wait_ge(m1_ssq, h + 1)
                pe.wait_ge(m1_exp, 32)
                mm(G[:, h], ones[:], nt[:, h], start=True, stop=True).then_inc(m1_ssp, 1)
            pe.wait_ge(m1_sub, 4)
            pe.wait_ge(m1_rec, 4)
            pe.wait_ge(m1_srt, 4)
            for j in range(4):
                projection("mixout", 2 * j, lambda n: (act_z, Z0["mixout"] + n), j)
            sum_squares("mix_end")

            sum_squares("ffn2")
            units("ffn2")
            sum_squares("ffn2_end")

            sum_squares("ctx", CTX)
            sum_squares("even")
            t = T0["evenin"]
            pe.wait_ge(weight_lo, t + 1)
            s = t % RING
            r = KC * NORM["ctx"][1]
            in_group(s, 0, G[:, 0, 0:CTX], r, CTX).then_inc(group_done, 1)
            for tt in range(CT):
                ins = token_group(s, G[:, 1, tt * P:(tt + 1) * P], tt, slice(P, 2 * P))
            ins.then_inc(group_done, 1)
            in_group(s, 0, G[:, 2], KC * NORM["even"][1]).then_inc(group_done, 1)
            for tt in range(TT):
                ins = token_group(s, G[:, 3, tt * P:(tt + 1) * P], tt, slice(P, 2 * P))
            ins.then_inc(group_done, 1)

            def norm_sums(idx, n):
                pe.wait_ge(m2_ssq, idx + 1)
                if idx:
                    pe.wait_ge(m2_srt, idx)
                mm(Dn[:, 0, 0:n], ones64[:], nt[:, 0, 0:n], start=True, stop=True).then_inc(m2_ssp, 1)

            def turned(idx, z):
                pe.wait_ge(m2_kn, idx + 1)
                if idx > 1:
                    pe.wait_ge(m2_rope, idx - 1)
                mm(Dn[:, 1], rot2[:], z, start=True, stop=True).then_inc(m2_rot, 1)
            z = lambda n: (act_z, Z0["evenin"] + n)
            norm_sums(0, CTX)
            projection("evenin", 4, z, 1)
            norm_sums(1, S)
            projection("evenin", 6, z, 2)
            turned(1, kall[:, CTX:SK])
            norm_sums(2, S)
            turned(2, q2[:, 0])
            norm_sums(3, S)
            projection("evenin", 8, z, 3)
            turned(3, q2[:, 1])
            norm_sums(4, S)
            turned(4, q2[:, 2])
            norm_sums(5, S)
            projection("evenin", 10, z, 4)
            turned(5, q2[:, 3])
            pe.wait_ge(ld_even, 32)
            pe.wait_ge(act_z, Z0["evenin"] + 12)
            for g in range(4):
                pe.wait_ge(m2_d, g + 1)
                mm(G[:, g], poolw[:, g], nt[:].rearrange("p a b -> p (a b)")[:, 1056:1056 + S], start=True,
                   stop=True).then_inc(m2_pw, 1)
            pe.wait_ge(m2_rope, 5)
            pe.wait_ge(m2_swap, 1)
            pe.wait_ge(m2_ps, 4)

            def scores2(n):
                c, i, half = n // 8, n // 2 % 4, n % 2
                ps = slice(64 * half, 64 * half + 64)
                keys = kall if c // 2 == half else kswap
                if n >= 2:
                    pe.wait_ge(m2_exp, n - 1)
                b = 2 * (n % 2)
                q = q2[ps, c, i * P:(i + 1) * P]
                mm(G[:, b], q, keys[ps, 0:S], start=True, stop=True)
                mm(G[:, b + 1, 0:CTX], q, keys[ps, S:SK], start=True, stop=True).then_inc(m2_qk, 1)

            def turn2(n):
                pe.wait_ge(m2_w, n + 1)
                if n >= 1:
                    pe.wait_ge(m2_wt, n)
                for k in range(6):
                    ins = nc.tensor.transpose(Dn[:, k // 4, (k % 4) * P:(k % 4 + 1) * P],
                                              pexp2[:, n % 3, k * P:(k + 1) * P], ident[:])
                ins.then_inc(m2_tr, 1)

            def values_sum2(n):
                c, i, half = n // 8, n // 2 % 4, n % 2
                pe.wait_ge(m2_wt, n + 1)
                if c >= 2 and n % 8 == 0:
                    pe.wait_ge(m2_olo, c - 1)
                for k in range(6):
                    v = vz[:, 2 * k + c // 2, 64 * (1 - half):64 * (1 - half) + P]
                    ins = mm(Dn[:, 2 + c % 2, i * P:(i + 1) * P], v, wt2[:, n % 2, k], start=(half == 0 and k == 0),
                             stop=(half == 1 and k == 5))
                ins.then_inc(m2_pv, 1)
            for n in range(35):
                if n < 32:
                    scores2(n)
                if 2 <= n < 34:
                    turn2(n - 2)
                if n >= 3:
                    values_sum2(n - 3)
            pe.wait_ge(m2_olo, 4)
            pe.wait_ge(m2_pool, 4)
            for j in range(4):
                projection("evenout", 2 * j, lambda n: (x_done, XDONE["even"] + n), j)

            for l in range(2):
                stage = f"moe{l}"
                sum_squares(stage)
                pe.wait_ge(rt_w, 2 * l + 2)
                pe.wait_ge(dve_alo, KC * NORM[stage][1] + KC)
                for tt in range(TT):
                    ts = slice(tt * P, tt * P + P)
                    for k in range(KC):
                        ins = product(Dn[:, M, 20 * tt:20 * tt + 20], (a_hi[:, k, ts], a_lo[:, k, ts]),
                                      (rw_hi[:, k], rw_lo[:, k]), k == 0, k == KC - 1)
                ins.then_inc(rt_logit, 1)
                units(stage)
                if l == 1:
                    break
                sum_squares("odd")

                def values3(slot, c, out):
                    for t in (2 * c, 2 * c + 1):
                        ins = token_group(slot, out[:, 256 * (t % 2):256 * (t % 2) + 256], t, slice(0, 256))
                    return ins
                for j in range(10):
                    projection("oddin", 2 * j, lambda n: (act_z, Z0["oddin"] + n), j,
                               values3 if j in (2, 3) else None, KC * NORM["odd"][1] if j == 0 else None)
                pe.wait_ge(ld_odd, 32)
                pe.wait_ge(m3_vn, 4)
                for g in range(4):
                    for n in range(TT):
                        ins = mm(Dn[:, g, n * P:(n + 1) * P], v3[:, n, g * P:(g + 1) * P], sgw[:, g], start=True, stop=True)
                    ins.then_inc(m3_sg, 1)
                pe.wait_ge(m3_y, 8)
                pe.wait_ge(act_z, Z0["oddin"] + 20)
                for j in range(4):
                    projection("oddout", 2 * j, lambda n: (x_done, XDONE["odd"] + n), j)


def kernel(x, c, positions, w_ada, b_ada, norm_g, ffn1_w_in, ffn1_w_out, ffn2_w_in, ffn2_w_out,
           w_mix_in, w_mix_out, lambda_q, lambda_k, subln_g, conv_w, conv_b, lru_w_gate, lru_b_gate,
           lru_lambda, c_2, ctx_2, c_ctx_2, mod_w_2, mod_b_2, norm1_g_2, norm2_g_2, even_w_in_2,
           q_gain_2, k_gain_2, pool_w_2, pool_scale_2, even_w_out_2, odd_w_in_2, sg_gain_2, sg_w_2,
           sg_b_2, conv_w_2, odd_w_out_2, router_g_w_2, router_g_b_2, router_e_w_2, router_e_b_2,
           w_gate_2, w_up_2, w_down_2):
    import numpy as np
    import concourse.bacc as bacc
    from concourse.bass_utils import run_bass_kernel_spmd as run

    f = np.float32

    def cols(v):
        return np.asarray(v).reshape(-1, P).T

    def twice(v):
        return np.concatenate([np.asarray(v).reshape(1, 64)] * 2, axis=1)

    idx = np.arange(P)
    inv = (f(10000.0) ** (-np.arange(0, 64, 2, dtype=f) / f(64))).astype(f)
    inv_col = inv[idx % 32].reshape(1, P)
    rot1 = np.zeros((P, P), f)
    rot2 = np.zeros((P, P), f)
    for o in range(P):
        rot1[o + 32 if o % 64 < 32 else o - 32, o] = -1.0 if o % 64 < 32 else 1.0
        rot2[o + 16 if o % 32 < 16 else o - 16, o] = -1.0 if o % 32 < 16 else 1.0
    inv2 = (f(10000.0) ** (-np.arange(0, 32, 2, dtype=f) / f(32))).astype(f)
    tok = np.arange(S)
    row, col = (tok // 64).astype(f), (tok % 64).astype(f)
    ang = np.where((idx % 64 < 32)[:, None], row[None, :], col[None, :]).astype(f) * inv2[idx % 16][:, None]
    rope2 = np.stack([np.cos(ang), np.sin(ang)], axis=1).astype(f)
    inv_count = np.stack([1.0 / (np.clip(tok + w - w // 2, 0, S) - np.clip(tok - w // 2, 0, S)).astype(f)
                          for w in (2, 4, 8, 16)]).astype(f)
    block64 = np.kron(np.eye(2, dtype=f), np.ones((64, 64), f))

    params = np.concatenate([cols(v) for v in (
        c, c_2, c_ctx_2, b_ada, mod_b_2, norm_g, norm1_g_2, norm2_g_2, subln_g, conv_w, conv_b, lru_b_gate,
        lru_lambda, twice(q_gain_2), twice(k_gain_2), pool_scale_2, sg_gain_2, conv_w_2, inv_col)], axis=1)
    assert params.shape == (P, NCOL), params.shape
    wg = np.asarray(lru_w_gate)[0]
    bd = np.zeros((P, 4, 4, P), wg.dtype)
    for d in range(2):
        for g in range(2):
            for n in range(8):
                h = 64 * (n % 2)
                bd[h:h + 64, 2 * d + g, n // 2, h:h + 64] = wg[d, g, n]
    arrays = {
        "x_t": np.asarray(x)[0].T, "ctx_t": np.asarray(ctx_2)[0].T, "params": params,
        "positions": np.asarray(positions),
        "lambda_qk": np.concatenate([np.asarray(lambda_q).reshape(-1), np.asarray(lambda_k).reshape(-1)]),
        "router_b": np.concatenate([np.asarray(router_g_b_2), np.asarray(router_e_b_2)], axis=1).reshape(-1),
        "router_w": np.concatenate([np.asarray(router_g_w_2), np.asarray(router_e_w_2)], axis=2),
        "lru_bd": bd.reshape(P, 4, 4 * P), "pool_w": np.asarray(pool_w_2)[0],
        "sg_w_t": np.asarray(sg_w_2)[0].transpose(2, 0, 1), "sg_b": np.asarray(sg_b_2)[0],
        "w_ada": np.asarray(w_ada)[0], "mod_w": np.asarray(mod_w_2),
        "ffn1_w_in": np.asarray(ffn1_w_in)[0], "ffn1_w_out": np.asarray(ffn1_w_out)[0],
        "ffn2_w_in": np.asarray(ffn2_w_in)[0], "ffn2_w_out": np.asarray(ffn2_w_out)[0],
        "w_mix_in": np.asarray(w_mix_in)[0], "w_mix_out": np.asarray(w_mix_out)[0],
        "even_w_in": np.asarray(even_w_in_2)[0], "even_w_out": np.asarray(even_w_out_2)[0],
        "odd_w_in": np.asarray(odd_w_in_2)[0], "odd_w_out": np.asarray(odd_w_out_2)[0],
        "w_gate": np.asarray(w_gate_2), "w_up": np.asarray(w_up_2), "w_down": np.asarray(w_down_2),
        "ident": np.eye(P, dtype=f), "ones": np.ones((P, P), f), "ones64": block64, "rot1": rot1, "rot2": rot2,
        "rope2": rope2, "inv_count": inv_count,
    }
    arrays = {n: np.ascontiguousarray(a) for n, a in arrays.items()}
    nc = bacc.Bacc("TRN2", target_bir_lowering=False, num_devices=1)
    io = {n: nc.dram_tensor(f"in_{n}", a.shape, mybir.dt.from_np(a.dtype), kind="ExternalInput").ap()
          for n, a in arrays.items()}
    io["comb_dram"] = nc.dram_tensor("comb_dram", (2 * EXPERTS, S), F32, kind="Internal").ap()
    io["out"] = nc.dram_tensor("out", (D, S), F32, kind="ExternalOutput").ap()
    build(nc, io)
    r = run(nc, [{f"in_{n}": a for n, a in arrays.items()}], core_ids=[0])
    return np.ascontiguousarray(r.results[0]["out"].T).reshape(1, S, D)
```

```python
import concourse.bass as bass
from concourse import mybir
from contextlib import ExitStack

F32 = mybir.dt.float32
F32R = mybir.dt.float32r
I32 = mybir.dt.int32
ALU = mybir.AluOpType
ACT = mybir.ActivationFunctionType
AX = mybir.AxisListType

P = 128
D = 1024
KC = D // P
S = 512
TT = S // P
CTX = 256
CT = CTX // P
D_FF = 2816
UNIT = 256
FFN_UNITS = D_FF // UNIT
EXPERTS = 16
HEADS1 = 4
EPS = 1e-6
LAMBDA_INIT = 0.2
TW = 2048
RING = 3

COLS = [("c", 8), ("c2", 8), ("cctx", 8), ("b_ada", 72), ("mod_b", 96), ("norm_g", 48), ("norm1", 16),
        ("norm2", 16), ("subln", 1), ("conv_w", 16), ("conv_b", 4), ("b_gate", 16), ("lam", 8),
        ("q_gain", 1), ("k_gain", 1), ("pool_scale", 4), ("sg_gain", 4), ("conv_w2", 12), ("inv_freq", 1)]
COL = {}
_at = 0
for _name, _n in COLS:
    COL[_name] = _at
    _at += _n
NCOL = _at

UNIT_GROUPS = [2, 2, 8]
STREAM = [("ffn1", UNIT_GROUPS * FFN_UNITS), ("mixin", [2] * 10), ("modctx", [2] * 10), ("mixout", [2] * 4),
          ("ffn2", UNIT_GROUPS * FFN_UNITS), ("evenin", [4, 2, 2, 2, 2]), ("evenout", [2] * 4),
          ("moe0", UNIT_GROUPS * EXPERTS), ("oddin", [2] * 10), ("oddout", [2] * 4),
          ("moe1", UNIT_GROUPS * EXPERTS)]
T0, GROUPS_BEFORE = {}, [0]
for _name, _g in STREAM:
    T0[_name] = len(GROUPS_BEFORE) - 1
    for _x in _g:
        GROUPS_BEFORE.append(GROUPS_BEFORE[-1] + _x)
TILES = len(GROUPS_BEFORE) - 1
UNIT0 = {"ffn1": 0, "ffn2": FFN_UNITS, "moe0": 2 * FFN_UNITS, "moe1": 2 * FFN_UNITS + EXPERTS}
UNITS = {"ffn1": FFN_UNITS, "ffn2": FFN_UNITS, "moe0": EXPERTS, "moe1": EXPERTS}

MOD_PER_UNIT = {"ffn1": 5, "ffn2": 4, "moe0": 3, "moe1": 0}
MOD_FIRST = [("ada", 0, 5), ("ada", 5, 5), ("ada", 10, 5), ("ada", 15, 2)]
MOD_VECTOR = [[r for r in range(n) if (c0 + r) % 2 == 0] for _, c0, n in MOD_FIRST]
MODCTX = [(j, 16, 168 + 2 * j) for j in range(8)] + [(22, 8, 72 + 44), (23, 8, 72 + 46)]
MIXIN_COLS = (6, 7, 8, 9, 0, 1, 2, 3, 4, 5)
EVENIN_COLS = (2, 0, 1, 4, 3)
ODDIN_COLS = (0, 1, 2, 3, 4, 5, 8, 9, 6, 7)
POOL_ORDER = (2, 3, 1, 0)
POOL_STEPS = (2, 4, 6, 8)
MOD_COND = {"ada": 0, "mod0": 8, "mod1": 8, "ctx": 16}
MOD_OUT = {"ada": 0, "mod0": 72, "mod1": 120, "ctx": 168}
MOD_BIAS = {"ada": COL["b_ada"], "mod0": COL["mod_b"], "mod1": COL["mod_b"] + 48, "ctx": COL["mod_b"]}
MOD_SLOTS = 5
MOD_LOOP = {"ffn1": ("ada", 17), "ffn2": ("mod0", 0), "moe0": ("mod1", 0)}
MB0, MQ0 = {}, {}
_b, _q = len(MOD_FIRST), sum(len(v) for v in MOD_VECTOR)
for _name in ("ffn1", "ffn2", "moe0"):
    MB0[_name], MQ0[_name] = _b, _q
    _b += UNITS[_name]
    _q += UNITS[_name] * MOD_PER_UNIT[_name]


def mod_fills(stage, r):
    n = sum(1 for _, _, k in MOD_FIRST if k > r)
    for name in ("ffn1", "ffn2", "moe0"):
        if name == stage:
            return n
        n += UNITS[name] * (MOD_PER_UNIT[name] > r)


PRIME_SILU, PRIME_GU, PRIME_ADD = 2, 2, 8

NORM = {"ffn1": (0, 0), "ffn1_end": (1, None), "mix": (2, 1), "mix_end": (3, None), "ffn2": (4, 2),
        "ctx": (5, 3), "ffn2_end": (6, None), "even": (7, 4), "moe0": (8, 5), "odd": (9, 6), "moe1": (10, 7)}
XDONE = {"ffn1": 0, "mix": 8, "ffn2": 16, "even": 24, "moe0": 32, "odd": 40, "moe1": 48, "end": 56}
Z0 = {"mixin": 0, "mixout": 20, "evenin": 28, "oddin": 40}


def build(nc, io):
    ctx = ExitStack()
    with ctx:
        def sb(name, shape, dt=F32):
            return ctx.enter_context(nc.sbuf_tensor(name, shape, dt))

        names = set()

        def sem(name):
            names.add(name)
            return ctx.enter_context(nc.semaphore(name))

        w_raw = sb("w_raw", [P, RING, TW])
        w_hi = sb("w_hi", [P, RING, TW], F32R)
        w_lo = sb("w_lo", [P, RING, TW], F32R)
        x = sb("x", [P, KC, S])
        a_hi = sb("a_hi", [P, KC, S], F32R)
        a_lo = sb("a_lo", [P, KC, S], F32R)
        h_hi = sb("h_hi", [P, 2, S], F32R)
        h_lo = sb("h_lo", [P, 2, S], F32R)
        nt = sb("nt", [P, 4, S])
        root = sb("root", [P, S])
        rinv = sb("rinv", [P, S])
        rope = sb("rope", [P, 2, S])
        red = sb("red", [P, MOD_SLOTS, P])
        pv = sb("pv", [P, NCOL])
        cond = sb("cond", [P, 24])
        cond_split = sb("cond_split", [P, 24, 2], F32R)
        mods = sb("mods", [P, 184])
        acol = sb("acol", [P, 8 * KC])
        gcol = sb("gcol", [P, 3 * KC])
        misc = sb("misc", [P, 64])
        stat = sb("stat", [P, 5, 32])
        ident = sb("ident", [P, P])
        ones = sb("ones", [P, P])
        ones64 = sb("ones64", [P, P])
        rot1 = sb("rot1", [P, P])
        rot2 = sb("rot2", [P, P])
        rw = sb("rw", [P, KC, 20])
        rw_hi = sb("rw_hi", [P, KC, 20], F32R)
        rw_lo = sb("rw_lo", [P, KC, 20], F32R)
        rb = sb("rb", [P, 2, 20])
        rt = sb("rt", [P, 296])
        K = 256
        arena = sb("arena", [P, 52 * K + 16])

        def ar(start, *shape):
            n = 1
            for d in shape:
                n *= d
            v = arena[:, start:start + n]
            if len(shape) == 2:
                v = v.rearrange("p (a b) -> p a b", b=shape[1])
            if len(shape) == 3:
                v = v.rearrange("p (a b c) -> p a b c", b=shape[1], c=shape[2])
            return v

        yacc = ar(0, KC, S)
        sg = ar(16 * K, 2, S)
        hid = ar(20 * K, 2, S)
        comb_row = ar(24 * K, S)
        comb_pad = ar(26 * K, TT, 32)
        comb_t = ar(26 * K + 128, TT, 32)
        mod_raw = ar(28 * K, MOD_SLOTS, KC, P)
        prod = ar(48 * K, KC, P)
        rank = misc[:, 8:12].unsqueeze(1)
        q1, k1, v1 = ar(0, 4, S), ar(8 * K, 4, S), ar(16 * K, 4, S)
        XRW = S + 3
        xr1 = ar(24 * K, 4, XRW)
        yr1 = ar(32 * K + 16, 4, S)
        bd = ar(40 * K + 16, 4, 4 * P)
        e0, e1 = ar(48 * K + 16, S), ar(50 * K + 16, S)
        mod_rows = ar(40 * K + 16, 2 * 10, P)
        pexp1 = ar(24 * K, 6, S)
        wsm1 = ar(36 * K, 2, S)
        wt1 = ar(40 * K, 2, 4, P)
        xc1 = (e0, red[:].rearrange("p a b -> p (a b)")[:, 0:S])
        SK = CTX + S
        q2 = ar(0, 4, S)
        kall, kswap = ar(8 * K, SK), ar(11 * K, SK)
        vz = ar(14 * K, 12, 192)
        PW = S + 16
        p2 = ar(23 * K + 64, 4, PW)
        windows = (ar(38 * K + 64, PW), red[:].rearrange("p a b -> p (a b)")[:, 0:PW])
        ctxx = ar(32 * K, KC, CTX)
        ic = ar(41 * K, 4, S)
        poolw = ar(49 * K, 4, P)
        pexp2 = ar(23 * K + 64, 3, SK)
        wt2 = ar(32 * K + 64, 2, 6, P)
        v2f = (ar(40 * K, CTX), ar(32 * K, S))
        m2_roots = (root, nt[:, 3])
        u3, v3 = ar(0, 4, S), ar(8 * K, 4, S)
        ZW = S + 2
        z3 = ar(16 * K, 4, ZW)
        bg3, cg3 = ar(25 * K, 4, S), ar(33 * K, 4, S)
        sgw = ar(41 * K, 4, P)
        sgb = ar(43 * K, 4, P)

        G = ctx.enter_context(nc.psum_tensor("G", [P, 4, S], F32))
        Dn = ctx.enter_context(nc.psum_tensor("Dn", [P, 4, S], F32))
        M = 3

        def down_bank(m):
            return (Dn[:, 0], Dn[:, 1], Dn[:, 2], G[:, 0], G[:, 1], Dn[:, 0], Dn[:, 1], Dn[:, 2])[m]

        def sum_bank(name):
            return G[:, 3] if name.endswith("_end") else G[:, 2] if name == "ctx" else Dn[:, 2]

        def w_in(buf, slot):
            return buf[:, slot, :].rearrange("p (k n) -> p k n", n=256)

        def w_down(buf, slot):
            return buf[:, slot, :].rearrange("p (k n) -> p k n", n=D)

        raw_full = [sem(f"raw_full{s}") for s in range(RING)]
        weight_hi, weight_lo, group_done = sem("weight_hi"), sem("weight_lo"), sem("group_done")
        mod_full = [sem(f"mod_full{s}") for s in range(MOD_SLOTS)]
        mod_direct = sem("mod_direct")
        mod_mul, mod_red, mod_sum, mod_out = sem("mod_mul"), sem("mod_red"), sem("mod_sum"), sem("mod_out")
        act_silu, dve_gu, act_hhi, dve_hlo, down_added = (sem(n) for n in (
            "act_silu", "dve_gu", "act_hhi", "dve_hlo", "down_added"))
        dve_comb, comb_full = sem("dve_comb"), sem("comb_full")
        act_sq, pe_ss, act_root, dve_rinv = sem("act_sq"), sem("pe_ss"), sem("act_root"), sem("dve_rinv")
        dve_cols, dve_t, act_af, act_ahi, dve_alo = (sem(n) for n in (
            "dve_cols", "dve_t", "act_af", "act_ahi", "dve_alo"))
        dve_yn, x_done = sem("dve_yn"), sem("x_done")
        act_z = sem("act_z")
        ld_x, ld_pv, ld_const, ld_row = sem("ld_x"), sem("ld_pv"), sem("ld_const"), sem("ld_row")
        ld_mix, ld_ctx, ld_even, ld_rope2, ld_odd = (sem(n) for n in (
            "ld_mix", "ld_ctx", "ld_even", "ld_rope2", "ld_odd"))
        ld_rw = [sem("ld_rw0"), sem("ld_rw1")]
        cond_done, dve_chain, act_chain, pool_chain = (sem(n) for n in ("cond_done", "dve_chain", "act_chain", "pool_chain"))
        rope1_ang, rope1_tab = sem("rope1_ang"), sem("rope1_tab")
        arena_free, arena_back = sem("arena_free"), sem("arena_back")
        lam_sum, lam_exp, sp_exp = sem("lam_sum"), sem("lam_exp"), sem("sp_exp")
        m1_pad, m1_yhi, m1_xc, m1_gate, m1_sig, m1_at, m1_m, m1_sqrt, m1_rec = (sem("m1_" + n) for n in (
            "pad", "yhi", "xc", "gate", "sig", "at", "m", "sqrt", "rec"))
        m1_rot, m1_rope, m1_qk, m1_nm, m1_exp, m1_w, m1_tr, m1_wt, m1_pv, m1_o = (sem("m1_" + n) for n in (
            "rot", "rope", "qk", "nm", "exp", "w", "tr", "wt", "pv", "o"))
        m1_row, m1_col, m1_ylo, m1_ssq, m1_ssp, m1_srt, m1_inv, m1_bc, m1_sub, m1_shi, m1_slo = (sem("m1_" + n) for n in (
            "row", "col", "ylo", "ssq", "ssp", "srt", "inv", "bc", "sub", "shi", "slo"))
        m2_pad, m2_ssq, m2_ssp, m2_srt, m2_kn, m2_rot, m2_rope, m2_swap = (sem("m2_" + n) for n in (
            "pad", "ssq", "ssp", "srt", "kn", "rot", "rope", "swap"))
        m2_d, m2_pw, m2_ps, m2_phi, m2_pool, m2_vf, m2_vtr = (sem("m2_" + n) for n in (
            "d", "pw", "ps", "phi", "pool", "vf", "vtr"))
        m2_qk, m2_nm, m2_exp, m2_w, m2_tr, m2_wt, m2_pv, m2_ohi, m2_olo = (sem("m2_" + n) for n in (
            "qk", "nm", "exp", "w", "tr", "wt", "pv", "ohi", "olo"))
        m3_pad, m3_ss, m3_srt, m3_vn, m3_sg, m3_y, m3_hi, m3_lo = (sem("m3_" + n) for n in (
            "pad", "ss", "srt", "vn", "sg", "y", "hi", "lo"))
        rt_w, rt_rows, rt_copy, rt_logit, rt_d1, rt_exp1, rt_d2, rt_exp2, rt_comb, rt_store = (sem("rt_" + n) for n in (
            "w", "rows", "copy", "logit", "d1", "exp1", "d2", "exp2", "comb", "store"))
        st_out = sem("st_out")

        io_w = {n: io[n].rearrange("(k p) n -> p k n", p=P) for n in (
            "ffn1_w_in", "ffn2_w_in", "w_mix_in", "w_mix_out", "even_w_in", "even_w_out",
            "odd_w_in", "odd_w_out", "w_ada")}
        io_down = {n: io[n].rearrange("(u k p) n -> u p k n", k=2, p=P) for n in ("ffn1_w_out", "ffn2_w_out")}
        moe_gate = io["w_gate"].rearrange("l e (k p) n -> (l e) p k n", p=P)
        moe_up = io["w_up"].rearrange("l e (k p) n -> (l e) p k n", p=P)
        moe_down = io["w_down"].rearrange("l e (k p) n -> (l e) p k n", p=P)
        mod_w = {"ada": io_w["w_ada"],
                 "mod0": io["mod_w"][0].rearrange("(k p) n -> p k n", p=P),
                 "mod1": io["mod_w"][1].rearrange("(k p) n -> p k n", p=P)}
        comb_dram = io["comb_dram"]

        block = ctx.enter_context(nc.Block())

        @block.sync
        def _(sp):
            def tile(t, source, buf, i=0):
                s = t % RING
                if not isinstance(i, int) or t + 3 * i >= RING:
                    sp.wait_ge(weight_lo, 3 * i + (t - RING + 1))
                sp.dma_start(buf(w_raw, s), source).then_inc(raw_full[s], 16)

            def mod_chunk(r, matrix, col):
                sp.dma_start(mod_raw[:, r], mod_w[matrix][:, :, bass.ds(col * P, P)]).then_inc(mod_full[r], 16)

            def unit_tiles(stage, i):
                t = T0[stage]
                if stage[:3] == "ffn":
                    w = io_w[stage + "_w_in"]
                    src = (w[:, :, bass.ds(i * UNIT, UNIT)], w[:, :, bass.ds(i * UNIT + D_FF, UNIT)],
                           io_down[stage + "_w_out"][i])
                else:
                    e = i + EXPERTS * (stage == "moe1")
                    src = (moe_gate[e], moe_up[e], moe_down[e])
                tile(t, src[0], w_in, i)
                tile(t + 1, src[1], w_in, i)
                tile(t + 2, src[2], w_down, i)
                if stage in ("ffn2", "moe0"):
                    sp.wait_ge(arena_back, 1 + (stage == "moe0"))
                for r in range(MOD_PER_UNIT[stage]):
                    if r == 0:
                        sp.wait_ge(mod_mul, i * MOD_PER_UNIT[stage] + MQ0[stage])
                        sp.wait_ge(mod_sum, len(MOD_FIRST))
                    matrix, col = MOD_LOOP[stage]
                    mod_chunk(r, matrix, i * MOD_PER_UNIT[stage] + (col + r))

            def cols(stage, name, tiles, start=0):
                for j, c in enumerate(tiles):
                    if j < start:
                        continue
                    tile(T0[stage] + j, io_w[name][:, :, c * 256:(c + 1) * 256], w_in)

            sp.dma_start(pv[:], io["params"]).then_inc(ld_pv, 16)
            sp.dma_start(x[:], io["x_t"].rearrange("(k p) n -> p k n", p=P)).then_inc(ld_x, 16)
            for dst, name in ((ident, "ident"), (ones, "ones"), (ones64, "ones64"), (rot1, "rot1"), (rot2, "rot2")):
                sp.dma_start(dst[:], io[name]).then_inc(ld_const, 16)
            sp.dma_start(nt[:, 0].bitcast(I32), io["positions"][0].partition_broadcast(P)).then_inc(ld_row, 16)
            sp.dma_start(nt[:, 1, 0:256], io["lambda_qk"].partition_broadcast(P)).then_inc(ld_row, 16)
            sp.dma_start(rb[:].rearrange("p l n -> p (l n)"), io["router_b"].partition_broadcast(P)).then_inc(ld_row, 16)
            sp.dma_start(rw[:], io["router_w"][0].rearrange("(k p) n -> p k n", p=P)).then_inc(ld_rw[0], 16)
            for b, (matrix, col, n) in enumerate(MOD_FIRST):
                for r in range(n):
                    if b:
                        by_vector = r in MOD_VECTOR[b - 1]
                        before = sum(len(v) for v in MOD_VECTOR[:b - 1])
                        if by_vector:
                            sp.wait_ge(mod_mul, before + MOD_VECTOR[b - 1].index(r) + 1)
                        else:
                            direct = sum(k for _, _, k in MOD_FIRST[:b - 1]) - before
                            sp.wait_ge(mod_direct, direct + r - sum(v < r for v in MOD_VECTOR[b - 1]) + 1)
                    mod_chunk(r, matrix, col + r)
            unit_tiles("ffn1", 0)
            with sp.Fori(1, FFN_UNITS) as i:
                unit_tiles("ffn1", i)

            cols("mixin", "w_mix_in", MIXIN_COLS[:RING])
            sp.wait_ge(arena_free, 1)
            sp.dma_start(bd, io["lru_bd"]).then_inc(ld_mix, 16)
            cols("mixin", "w_mix_in", MIXIN_COLS, RING)
            for j, (c, _, _) in enumerate(MODCTX):
                tile(T0["modctx"] + j, mod_w["mod0"][:, :, c * 256:(c + 1) * 256], w_in)
            cols("mixout", "w_mix_out", range(4))

            with sp.Fori(0, FFN_UNITS) as i:
                unit_tiles("ffn2", i)

            cols("evenin", "even_w_in", EVENIN_COLS[:RING])
            sp.wait_ge(mod_mul, MQ0["moe0"])
            sp.dma_start(ctxx, io["ctx_t"].rearrange("(k p) n -> p k n", p=P)).then_inc(ld_ctx, 16)
            sp.wait_ge(arena_free, 2)
            sp.dma_start(poolw, io["pool_w"].rearrange("g c d -> c g d")).then_inc(ld_even, 16)
            sp.dma_start(ic, io["inv_count"].partition_broadcast(P)).then_inc(ld_even, 16)
            sp.dma_start(rope[:], io["rope2"]).then_inc(ld_rope2, 16)
            cols("evenin", "even_w_in", EVENIN_COLS, RING)
            cols("evenout", "even_w_out", range(4))

            with sp.Fori(0, EXPERTS) as i:
                unit_tiles("moe0", i)

            cols("oddin", "odd_w_in", ODDIN_COLS[:RING])
            sp.wait_ge(arena_free, 3)
            sp.dma_start(sgw, io["sg_w_t"]).then_inc(ld_odd, 16)
            sp.dma_start(sgb, io["sg_b"].rearrange("g p -> (g p)").partition_broadcast(P)
                         .rearrange("p (g n) -> p g n", n=P)).then_inc(ld_odd, 16)
            sp.wait_ge(rt_w, 2)
            sp.dma_start(rw[:], io["router_w"][1].rearrange("(k p) n -> p k n", p=P)).then_inc(ld_rw[1], 16)
            cols("oddin", "odd_w_in", ODDIN_COLS, RING)
            cols("oddout", "odd_w_out", range(4))

            with sp.Fori(0, EXPERTS) as i:
                unit_tiles("moe1", i)

            out = io["out"].rearrange("(k p) n -> p k n", p=P)
            for k in range(KC):
                sp.wait_ge(x_done, XDONE["end"] - KC + k + 1)
                sp.dma_start(out[:, k], x[:, k]).then_inc(st_out, 16)
            sp.wait_ge(st_out, 16 * KC)

        @block.gpsimd
        def _(pool):
            def split_lo(s, n):
                pool.wait_ge(weight_hi, n)
                nc.gpsimd.tensor_tensor(w_lo[:, s], w_raw[:, s], w_hi[:, s], ALU.subtract).then_inc(weight_lo, 1)

            def split_tiles(first, end):
                t = first
                while t % RING:
                    split_lo(t % RING, t + 1)
                    t += 1
                with pool.Fori(0, (end - t) // RING) as i:
                    for s in range(RING):
                        split_lo(s, RING * i + (t + s + 1))
                for t in range(end - (end - t) % RING, end):
                    split_lo(t % RING, t + 1)

            split_tiles(0, T0["evenout"] + 1)
            links = [0]

            def link(ins):
                links[0] += 1
                ins.then_inc(pool_chain, 1)
                pool.wait_ge(pool_chain, links[0])
            pool.wait_ge(ld_even, 32)
            for n, g in enumerate(POOL_ORDER):
                pool.wait_ge(act_z, Z0["evenin"] + (9, 10, 12, 12)[n])
                src, width = p2[:, g], PW
                for lvl in range(g + 1):
                    step = 1 << lvl
                    dst = windows[lvl % 2]
                    width -= step
                    link(nc.gpsimd.tensor_tensor(dst[:, 0:width], src[:, 0:width], src[:, step:step + width], ALU.add))
                    src = dst
                half = 1 << g
                link(nc.gpsimd.tensor_tensor(ic[:, g], src[:, 8 - half:8 - half + S], ic[:, g], ALU.mult))
                nc.gpsimd.tensor_tensor(ic[:, g], ic[:, g], p2[:, g, 8:8 + S], ALU.subtract).then_inc(m2_d, 1)
            split_tiles(T0["evenout"] + 1, TILES)

        @block.scalar
        def _(act):
            chain = [0]

            def link(ins):
                chain[0] += 1
                ins.then_inc(act_chain, 1)
                act.wait_ge(act_chain, chain[0])

            def hi(t, i=0):
                if isinstance(i, int) and t + 3 * i >= TILES:
                    return
                s = t % RING
                act.wait_ge(raw_full[s], 16 * i + 16 * (t // RING + 1))
                if not isinstance(i, int) or t + 3 * i >= RING:
                    act.wait_ge(group_done, 12 * i + GROUPS_BEFORE[t - 2])
                nc.scalar.activation(w_hi[:, s], w_raw[:, s], ACT.Copy).then_inc(weight_hi, 1)

            def sum_squares(name, src, n=S, ready=None, after=None):
                q = NORM[name][0]
                for k in range(KC):
                    if ready:
                        ready(k)
                    if k >= 2:
                        act.wait_ge(pe_ss, KC * q + k - 1)
                    nc.scalar.activation(nt[:, k % 2, 0:n], src[:, k], ACT.Square).then_inc(act_sq, 1)
                    if after:
                        after(k)
                act.wait_ge(pe_ss, KC * q + KC)
                nc.scalar.activation(root[:, 0:n], sum_bank(name)[:, 0:n], ACT.Sqrt, bias=misc[:, 0:1],
                                     scale=1.0 / D).then_inc(act_root, 1)

            def modulated(name, shift, n=S):
                for k in range(KC):
                    modulated_chunk(name, shift, k, n)

            def modulated_chunk(name, shift, k, n=S):
                m = NORM[name][1]
                act.wait_ge(dve_cols, m + 1)
                if True:
                    t = nt[:, 2 + k % 2, 0:n]
                    act.wait_ge(dve_t, KC * m + k + 1)
                    nc.scalar.activation(t, t, ACT.Identity, bias=mods[:, shift + k:shift + k + 1],
                                         scale=acol[:, KC * m + k:KC * m + k + 1]).then_inc(act_af, 1)
                    act.wait_ge(act_af, KC * m + k + 1)
                    nc.scalar.activation(a_hi[:, k, 0:n], t, ACT.Copy).then_inc(act_ahi, 1)

            def unit(stage, i, router=None):
                t, u = T0[stage], i + UNIT0[stage]
                g = 12 * i + GROUPS_BEFORE[t]
                hi(t + 2, i)
                for c in range(2):
                    act.wait_ge(group_done, g + (c + 1))
                    act.wait_ge(dve_gu, 2 * u + (c + 1))
                    nc.scalar.activation(sg[:, c], G[:, c], ACT.Silu).then_inc(act_silu, 1)
                if router:
                    router()
                hi(t + 3, i)
                for c in range(2):
                    act.wait_ge(dve_gu, 2 * u + (PRIME_GU + c + 1))
                    nc.scalar.activation(h_hi[:, c], hid[:, c], ACT.Copy).then_inc(act_hhi, 1)
                if stage[:3] == "moe" and not (isinstance(i, int) and i == EXPERTS - 1):
                    load_comb(i + (EXPERTS * (stage == "moe1") + 1))
                hi(t + 4, i)

            def load_comb(row):
                act.dma_start(comb_row, comb_dram[row].partition_broadcast(P)).then_inc(comb_full, 16)

            def units(stage, router=None):
                n = UNITS[stage]
                unit(stage, 0, router)
                with act.Fori(1, n - 1) as i:
                    unit(stage, i)
                unit(stage, n - 1)

            def tile_step(t, evacuate):
                hi(t + 2)
                for c in range(2):
                    act.wait_ge(group_done, GROUPS_BEFORE[t] + c + 1)
                    evacuate(c)

            act.wait_ge(ld_pv, 16)
            nc.scalar.activation(cond[:], pv[:, 0:24], ACT.Silu).then_inc(cond_done, 1)
            act.wait_ge(cond_done, 1)
            nc.scalar.activation(cond_split[:, :, 0], cond[:], ACT.Copy).then_inc(cond_done, 1)
            nc.scalar.activation(misc[:, 62:63], pv[:, 0:1], ACT.Copy).then_inc(act_silu, PRIME_SILU)
            act.wait_ge(rope1_ang, 1)
            nc.scalar.activation(rope[:, 1], rope[:, 1], ACT.Sin).then_inc(rope1_tab, 1)
            act.wait_ge(rope1_ang, 2)
            nc.scalar.activation(rope[:, 0], rope[:, 0], ACT.Sin).then_inc(rope1_tab, 1)
            act.wait_ge(lam_sum, 1)
            nc.scalar.activation(misc[:, 2:4], misc[:, 2:4], ACT.Exp).then_inc(lam_exp, 1)
            act.wait_ge(lam_sum, 2)
            nc.scalar.activation(misc[:, 16:24], misc[:, 16:24], ACT.Exp, scale=-1.0).then_inc(sp_exp, 1)

            act.wait_ge(ld_x, 16)
            act.wait_ge(dve_chain, 1)
            sum_squares("ffn1", x)
            hi(0)
            hi(1)
            modulated("ffn1", MOD_OUT["ada"])
            units("ffn1")

            def added(stage):
                return lambda k: act.wait_ge(down_added, PRIME_ADD + 8 * (UNIT0[stage] + UNITS[stage] - 1) + k + 1)
            sum_squares("ffn1_end", yacc, ready=added("ffn1"))

            sum_squares("mix", x, ready=lambda k: act.wait_ge(x_done, XDONE["mix"] + k + 1 - KC + 0))
            modulated("mix", MOD_OUT["ada"] + 24)
            act.wait_ge(m1_pad, 1)

            def evac_mixin(j):
                def go(c):
                    g = 2 * j + c
                    src, f, scale = G[:, g % 4], ACT.Copy, 1.0
                    if g < 4:
                        dst = xr1[:, g, 2:2 + S]
                    elif g < 8:
                        dst, f = yr1[:, g - 4], ACT.Gelu_apprx_tanh
                    elif g < 12:
                        dst, scale = q1[:, g - 8], 0.125
                    elif g < 16:
                        dst = k1[:, g - 12]
                    else:
                        dst = v1[:, 2 * c:2 * c + 2, 256 * (j - 8):256 * (j - 7)]
                        src = src.rearrange("p (t n) -> p t n", n=256)
                    nc.scalar.activation(dst, src, f, scale=scale).then_inc(act_z, 1)
                return go

            def rg_gates(c):
                for d in range(2):
                    for g in range(2):
                        col = COL["b_gate"] + (2 * d + g) * 4 + c
                        act.wait_ge(m1_gate, 4 * c + 2 * d + g + 1)
                        if c:
                            act.wait_ge(m1_rec, c)
                        nc.scalar.activation(nt[:, 2 * g + d], Dn[:, 2 * d + g], ACT.Sigmoid,
                                             bias=pv[:, col:col + 1]).then_inc(m1_sig, 1)
                for d in range(2):
                    a = (root, rinv)[d]
                    sp8 = misc[:, 32 + 4 * d + c:33 + 4 * d + c]
                    act.wait_ge(m1_sig, 4 * c + 4)
                    nc.scalar.activation(a[:], nt[:, d], ACT.Exp, scale=misc[:, 24 + 4 * d + c:25 + 4 * d + c]).then_inc(m1_at, 1)
                    act.wait_ge(m1_at, 4 * c + 2 * d + 1)
                    nc.scalar.activation(nt[:, d], nt[:, d], ACT.Tanh, scale=sp8).then_inc(m1_at, 1)

            def rg_roots(c):
                for d in range(2):
                    act.wait_ge(m1_m, 2 * c + d + 1)
                    nc.scalar.activation(nt[:, d], nt[:, d], ACT.Sqrt).then_inc(m1_sqrt, 1)
            for j in range(10):
                tile_step(T0["mixin"] + j, evac_mixin(j))
                if j % 2 and j < 9:
                    rg_gates(j // 2)
                if j % 2 == 0 and j:
                    rg_roots(j // 2 - 1)
            def modctx_row(j):
                act.wait_ge(group_done, GROUPS_BEFORE[T0["modctx"] + j + 1])
                nc.scalar.activation(mod_rows[0:2, 2 * j:2 * j + 2], Dn[0:2, 2 + j % 2, 0:256].rearrange("p (c n) -> p c n", n=P),
                                     ACT.Copy).then_inc(m1_row, 1)
            for j in range(10):
                hi(T0["modctx"] + j + 2)
                if j:
                    modctx_row(j - 1)
                if j == 0:
                    act.wait_ge(group_done, GROUPS_BEFORE[T0["modctx"]])
                if j < 4:
                    act.wait_ge(m1_rec, j + 1)
                    nc.scalar.activation(a_hi[:, 4 + j], yr1[:, j], ACT.Copy).then_inc(m1_yhi, 1)
            modctx_row(9)

            def exps(n):
                act.wait_ge(m1_nm, n + 1)
                if n >= 3:
                    act.wait_ge(m1_w, n - 2)
                for m in range(2):
                    nc.scalar.activation(pexp1[:, 2 * (n % 3) + m], G[:, 2 * (n % 2) + m], ACT.Exp,
                                         bias=stat[:, 1, 2 * n + m:2 * n + m + 1],
                                         accum_out=stat[:, 2, 2 * n + m:2 * n + m + 1]).then_inc(m1_exp, 1)

            def weights_t(n):
                act.wait_ge(m1_tr, n + 1)
                if n >= 2:
                    act.wait_ge(m1_pv, n - 1)
                nc.scalar.activation(wt1[:, n % 2], Dn[:, n % 2].rearrange("p (k q) -> p k q", q=P),
                                     ACT.Copy).then_inc(m1_wt, 1)

            def head_out(h):
                act.wait_ge(m1_pv, 4 * h + 4)
                nc.scalar.activation(q1[:, h], Dn[:, 2 + h % 2], ACT.Copy).then_inc(m1_o, 1)
                act.wait_ge(m1_o, h + 1)
                nc.scalar.activation(nt[:, h], q1[:, h], ACT.Square).then_inc(m1_ssq, 1)
            for n in range(20):
                if n < 16:
                    exps(n)
                if 2 <= n < 18:
                    weights_t(n - 2)
                if n >= 7 and n % 4 == 3:
                    head_out(n // 4 - 1)
            act.wait_ge(m1_ssp, 1)
            nc.scalar.activation(stat[:, 0, 0:16], Dn[:, 0, 0:16], ACT.Sqrt, bias=misc[:, 0:1],
                                 scale=1.0 / P).then_inc(m1_srt, 1)
            for h in range(4):
                act.wait_ge(m1_sub, h + 1)
                nc.scalar.activation(a_hi[:, h], q1[:, h], ACT.Copy).then_inc(m1_shi, 1)
            for j in range(4):
                def evac_y(c, j=j):
                    nc.scalar.activation(yacc[:, 2 * j + c], G[:, (2 * j + c) % 4], ACT.Copy).then_inc(act_z, 1)
                tile_step(T0["mixout"] + j, evac_y)
            sum_squares("mix_end", yacc, ready=lambda k: act.wait_ge(act_z, Z0["mixout"] + k + 1))

            sum_squares("ffn2", x, ready=lambda k: act.wait_ge(x_done, XDONE["ffn2"] - KC + k + 1))
            modulated("ffn2", MOD_OUT["ada"] + 48)
            units("ffn2")
            act.wait_ge(ld_ctx, 16)
            sum_squares("ctx", ctxx, CTX)
            sum_squares("ffn2_end", yacc, ready=added("ffn2"),
                        after=lambda k: modulated_chunk("ctx", MOD_OUT["ctx"], k, CTX))

            HEADS2 = [(kall[:, 0:CTX], CTX, 1), (kall[:, CTX:SK], S, 3)] + [(q2[:, m], S, 5 + m) for m in range(4)]

            def m2_square(idx):
                src, n, ready = HEADS2[idx]
                act.wait_ge(act_z, Z0["evenin"] + ready)
                if idx >= 2:
                    act.wait_ge(m2_ssp, idx - 1)
                nc.scalar.activation(nt[:, idx % 2, 0:n], src, ACT.Square).then_inc(m2_ssq, 1)

            def m2_root(idx):
                n = HEADS2[idx][1]
                act.wait_ge(m2_ssp, idx + 1)
                if idx >= 2:
                    act.wait_ge(m2_kn, idx - 1)
                nc.scalar.activation(m2_roots[idx % 2][:, 0:n], Dn[:, 3 * (idx % 2), 0:n], ACT.Sqrt, bias=misc[:, 0:1],
                                     scale=1.0 / 64).then_inc(m2_srt, 1)

            sum_squares("even", x, ready=lambda k: act.wait_ge(x_done, XDONE["even"] - KC + k + 1))
            t = T0["evenin"]
            g = GROUPS_BEFORE[t]
            hi(t + 2)
            act.wait_ge(m2_pad, 1)

            def keys_values(first, n, width, keys, banks, heads):
                act.wait_ge(group_done, first + 1)
                nc.scalar.activation(v2f[n], G[:, banks[1], 0:width], ACT.Copy).then_inc(m2_vf, 1)
                act.wait_ge(group_done, first + 2)
                nc.scalar.activation(keys, G[:, banks[0], 0:width], ACT.Copy).then_inc(act_z, 1)
                act.wait_ge(m2_vtr, n + 1)
                nc.scalar.activation(vz[:, heads, 64:128], G[:, banks[1], 0:width].rearrange("p (t n) -> p t n", n=64),
                                     ACT.Copy).then_inc(act_z, 1)
            keys_values(g, 0, CTX, kall[:, 0:CTX], (0, 1), slice(0, 4))
            m2_square(0)
            modulated("even", MOD_OUT["mod0"])
            m2_root(0)
            keys_values(g + 2, 1, S, kall[:, CTX:SK], (2, 3), slice(4, 12))
            m2_square(1)
            for j in range(4):
                def evac(c, j=j):
                    g = 2 * j + c
                    dst = q2[:, g] if g < 4 else p2[:, (2, 3, 0, 1)[g - 4], 8:8 + S]
                    nc.scalar.activation(dst, G[:, g % 4], ACT.Copy).then_inc(act_z, 1)
                    if g < 5:
                        m2_root(g + 1)
                    if g < 4:
                        m2_square(g + 2)
                tile_step(t + 1 + j, evac)
            def pool_out(n):
                g = POOL_ORDER[n]
                act.wait_ge(m2_pw, n + 1)
                col = COL["pool_scale"] + g
                nc.scalar.activation(ic[:, g], Dn[:, 3], ACT.Copy, scale=pv[:, col:col + 1]).then_inc(m2_ps, 1)
                act.wait_ge(m2_ps, n + 1)
                nc.scalar.activation(a_hi[:, 4 + g], ic[:, g], ACT.Copy).then_inc(m2_phi, 1)

            def exps2(n):
                act.wait_ge(m2_nm, n + 1)
                if n < 3:
                    act.wait_ge(m2_d, 2 + n)
                else:
                    act.wait_ge(m2_tr, n - 2)
                b = 2 * (n % 2)
                nc.scalar.activation(pexp2[:, 2 - n % 3], G[:, b:b + 2].rearrange("p a b -> p (a b)")[:, 0:SK], ACT.Exp,
                                     bias=stat[:, 1, n:n + 1], accum_out=stat[:, 2, n:n + 1]).then_inc(m2_exp, 1)

            def weights_t2(n):
                act.wait_ge(m2_tr, n + 1)
                if n >= 2:
                    act.wait_ge(m2_pv, n - 1)
                nc.scalar.activation(wt2[:, n % 2],
                                     Dn[:, 0:2].rearrange("p a b -> p (a b)")[:, 0:SK].rearrange("p (k q) -> p k q", q=P),
                                     ACT.Copy).then_inc(m2_wt, 1)

            def heads_out(c):
                act.wait_ge(m2_pv, 8 * c + 8)
                nc.scalar.activation(a_hi[:, c], Dn[:, 2 + c % 2], ACT.Copy).then_inc(m2_ohi, 1)
            for n in range(36):
                if n < 32:
                    exps2(n)
                if 2 <= n < 34:
                    weights_t2(n - 2)
                if n - 1 in POOL_STEPS:
                    pool_out(POOL_STEPS.index(n - 1))
                if n >= 11 and n % 8 == 3:
                    heads_out(n // 8 - 1)
            for j in range(4):
                hi(T0["evenout"] + j + 2)

            for l in range(2):
                stage = f"moe{l}"
                act.wait_ge(ld_rw[l], 16)
                nc.scalar.activation(rw_hi[:], rw[:], ACT.Copy).then_inc(rt_w, 1)
                sum_squares(stage, x, ready=lambda k: act.wait_ge(x_done, XDONE[stage] - KC + k + 1))
                modulated(stage, MOD_OUT[f"mod{l}"] + 24)

                def router(l=l):
                    act.wait_ge(rt_d1, l + 1)
                    nc.scalar.activation(rt[:, 96:112], rt[:, 96:112], ACT.Exp).then_inc(rt_exp1, 1)
                    act.wait_ge(rt_d2, l + 1)
                    nc.scalar.activation(rt[:, 116:120], rt[:, 116:120], ACT.Exp).then_inc(rt_exp2, 1)
                    act.wait_ge(rt_comb, l + 1)
                    for b in range(4):
                        act.dma_start(comb_dram[l * EXPERTS:(l + 1) * EXPERTS, :]
                                      .rearrange("e (t b j) -> b e t j", b=4, j=32)[b],
                                      comb_t[32 * b:32 * b + EXPERTS]).then_inc(rt_store, 16)
                    act.wait_ge(rt_store, 64 * (l + 1))
                    load_comb(EXPERTS * l)
                units(stage, router)
                if l == 1:
                    break
                sum_squares("odd", x, ready=lambda k: act.wait_ge(x_done, XDONE["odd"] - KC + k + 1))
                modulated("odd", MOD_OUT["mod1"])
                act.wait_ge(m3_pad, 1)

                def evac_odd(j):
                    def go(c):
                        g = 2 * j + c
                        src = G[:, g % 4]
                        if g < 4:
                            dst = u3[:, g]
                        elif g < 8:
                            dst = v3[:, 2 * c:2 * c + 2, 256 * (j - 2):256 * (j - 1)]
                            src = src.rearrange("p (t n) -> p t n", n=256)
                        elif g < 12:
                            dst = z3[:, g - 8, 1:1 + S]
                        else:
                            dst = (cg3, bg3)[(g - 12) // 4][:, g % 4]
                        nc.scalar.activation(dst, src, ACT.Copy).then_inc(act_z, 1)
                    return go
                for j in range(10):
                    tile_step(T0["oddin"] + j, evac_odd(j))
                    if j == 4:
                        act.wait_ge(m3_ss, 4)
                        nc.scalar.activation(stat[:, 1, 0:16], stat[:, 0, 0:16], ACT.Sqrt, bias=misc[:, 0:1],
                                             scale=1.0 / P).then_inc(m3_srt, 1)
                for k in range(KC):
                    act.wait_ge(m3_y, k + 1)
                    src = u3[:, k] if k < 4 else bg3[:, k - 4]
                    nc.scalar.activation(a_hi[:, k], src, ACT.Copy).then_inc(m3_hi, 1)
                for j in range(4):
                    hi(T0["oddout"] + j + 2)

        @block.vector
        def _(dve):
            V = nc.vector
            chain = [0]

            def link(ins):
                chain[0] += 1
                ins.then_inc(dve_chain, 1)
                dve.wait_ge(dve_chain, chain[0])

            def mod_multiply(matrix, r, q, fill):
                c = MOD_COND[matrix]
                dve.wait_ge(mod_full[r], fill)
                if not isinstance(q, int) or q:
                    dve.wait_ge(mod_red, q)
                V.tensor_tensor(prod, mod_raw[:, r], cond[:, c:c + KC].unsqueeze(2).to_broadcast([P, KC, P]),
                                ALU.mult).then_inc(mod_mul, 1)

            def mod_reduce(r, q):
                dve.wait_ge(mod_mul, q + 1)
                V.tensor_reduce(red[:, r], prod.rearrange("p k n -> p n k"), AX.X, ALU.add).then_inc(mod_red, 1)

            def mod_bias(matrix, n, batch, col):
                dve.wait_ge(mod_sum, batch + 1)
                V.tensor_tensor(mods[:, bass.ds(col + MOD_OUT[matrix], n)], Dn[:, M, 0:n],
                                pv[:, bass.ds(col + MOD_BIAS[matrix], n)], ALU.add).then_inc(mod_out, 1)

            def norm_inverse(name, n=S):
                q = NORM[name][0]
                dve.wait_ge(act_root, q + 1)
                V.reciprocal(rinv[:, 0:n], root[:, 0:n]).then_inc(dve_rinv, 1)
                dve.wait_ge(dve_rinv, q + 1)

            def modulated(name, src, scale_col, gain_col, n=S):
                m = NORM[name][1]
                V.scalar_tensor_tensor(acol[:, KC * m:KC * m + KC], mods[:, scale_col:scale_col + KC], 1.0,
                                       pv[:, gain_col:gain_col + KC], ALU.add, ALU.mult).then_inc(dve_cols, 1)
                norm_inverse(name, n)

                def low(k):
                    dve.wait_ge(act_ahi, KC * m + k + 1)
                    V.tensor_tensor(a_lo[:, k, 0:n], nt[:, 2 + k % 2, 0:n], a_hi[:, k, 0:n],
                                    ALU.subtract).then_inc(dve_alo, 1)
                for k in range(KC):
                    if k >= 2:
                        dve.wait_ge(dve_alo, KC * m + k - 1)
                    V.tensor_tensor(nt[:, 2 + k % 2, 0:n], src[:, k], rinv[:, 0:n], ALU.mult).then_inc(dve_t, 1)
                    if k:
                        low(k - 1)
                low(KC - 1)

            def end_norm(name, s, gate_col, gain_col, weight):
                link(V.scalar_tensor_tensor(gcol[:, KC * s:KC * s + KC], mods[:, gate_col:gate_col + KC], weight,
                                            pv[:, gain_col:gain_col + KC], ALU.mult, ALU.mult))
                norm_inverse(name)

                def add(k):
                    dve.wait_ge(dve_yn, KC * s + k + 1)
                    V.scalar_tensor_tensor(x[:, k], yacc[:, k], gcol[:, KC * s + k:KC * s + k + 1], x[:, k],
                                           ALU.mult, ALU.add).then_inc(x_done, 1)
                for k in range(KC):
                    V.tensor_tensor(yacc[:, k], yacc[:, k], rinv[:], ALU.mult).then_inc(dve_yn, 1)
                    if k:
                        add(k - 1)
                add(KC - 1)

            def unit(stage, i, route=None):
                t, u = T0[stage], i + UNIT0[stage]
                g = 12 * i + GROUPS_BEFORE[t]
                n = MOD_PER_UNIT[stage]
                first = isinstance(i, int)
                if route:
                    route()
                moe = stage[:3] == "moe"
                if n:
                    matrix, col = MOD_LOOP[stage]
                    batch, q = i + MB0[stage], i * n + MQ0[stage]
                    fill = lambda r: 16 * i + 16 * (mod_fills(stage, r) + 1)
                    dve.wait_ge(mod_sum, batch)
                    for r in range(n):
                        mod_multiply(matrix, r, q + r, fill(r))
                        mod_reduce(r, q + r)
                if moe:
                    e = i + EXPERTS * (stage == "moe1")
                    dve.wait_ge(comb_full, 16 * e + 16)
                for c in range(2):
                    if moe:
                        dve.wait_ge(act_silu, 2 * u + (PRIME_SILU + c + 1))
                        V.tensor_tensor(sg[:, c], sg[:, c], comb_row, ALU.mult).then_inc(dve_comb, 1)
                for c in range(2):
                    if moe:
                        dve.wait_ge(dve_comb, 2 * e + (c + 1))
                    else:
                        dve.wait_ge(act_silu, 2 * u + (PRIME_SILU + c + 1))
                    dve.wait_ge(group_done, g + (2 + c + 1))
                    if c == 0:
                        dve.wait_ge(dve_hlo, 2 * u + 1)
                    V.tensor_tensor(hid[:, c], G[:, 2 + c], sg[:, c], ALU.mult).then_inc(dve_gu, 1)
                    dve.wait_ge(act_hhi, 2 * u + (c + 1))
                    V.tensor_tensor(h_lo[:, c], hid[:, c], h_hi[:, c], ALU.subtract).then_inc(dve_hlo, 1)
                for m in range(KC):
                    dve.wait_ge(group_done, g + (4 + m + 1))
                    dve.wait_ge(down_added, 8 * u + (m + 1))
                    if first:
                        V.tensor_copy(yacc[:, m], down_bank(m)).then_inc(down_added, 1)
                    else:
                        V.tensor_tensor(yacc[:, m], yacc[:, m], down_bank(m), ALU.add).then_inc(down_added, 1)
                if n:
                    mod_bias(matrix, n, batch, i * n + col)

            def units(stage, route=None, after_first=None):
                unit(stage, 0, route)
                if after_first:
                    after_first()
                with dve.Fori(1, UNITS[stage]) as i:
                    unit(stage, i)
                dve.wait_ge(down_added, PRIME_ADD + 8 * (UNIT0[stage] + UNITS[stage]))

            def split(src, k):
                link(V.tensor_copy(a_hi[:, k], src))
                return V.tensor_tensor(a_lo[:, k], src, a_hi[:, k], ALU.subtract)

            link(V.memset(misc[:, 0:1], EPS))
            for j in range(4):
                V.memset(misc[:, 8 + j:9 + j], float(4 - j))
            V.memset(misc[:, 60:61], 0.0).then_inc(dve_gu, PRIME_GU)
            V.memset(misc[:, 61:62], 0.0).then_inc(down_added, PRIME_ADD)
            V.memset(misc[:, 63:64], 0.0).then_inc(dve_hlo, 1)
            dve.wait_ge(ld_pv, 16)
            def prepare():
                dve.wait_ge(ld_row, 48)
                link(V.tensor_tensor(nt[:, 2, 0:128], nt[:, 1, 0:128], nt[:, 1, 128:256], ALU.mult))
                V.tensor_reduce(misc[:, 2:4], nt[:, 2, 0:128].rearrange("p (m d) -> p m d", m=2), AX.X,
                                ALU.add).then_inc(lam_sum, 1)
                link(V.tensor_copy(nt[:, 3], nt[:, 0].bitcast(I32)))
                fr = COL["inv_freq"]
                link(V.tensor_scalar(nt[:, 3], nt[:, 3], pv[:, fr:fr + 1], None, ALU.mult))
                C1 = 6.28125
                C2 = 0.0019350051879882812
                C3 = 6.283185307179586 - C1 - C2
                MAGIC = 12582912.0
                PI = 3.1415925
                link(V.tensor_scalar(nt[:, 2], nt[:, 3], 0.15915494309189535, MAGIC, ALU.mult, ALU.add))
                link(V.tensor_scalar(nt[:, 2], nt[:, 2], MAGIC, None, ALU.subtract))
                for part in (C1, C2, C3):
                    link(V.scalar_tensor_tensor(nt[:, 3], nt[:, 2], -part, nt[:, 3], ALU.mult, ALU.add))
                V.tensor_scalar(rope[:, 1], nt[:, 3], PI, -PI, ALU.min, ALU.max).then_inc(rope1_ang, 1)
                link(V.tensor_scalar(nt[:, 3], nt[:, 3], 1.5707963267948966, None, ALU.add))
                link(V.tensor_scalar(nt[:, 2], nt[:, 3], 3.141592653589793, 6.283185307179586, ALU.is_gt, ALU.mult))
                link(V.tensor_tensor(nt[:, 3], nt[:, 3], nt[:, 2], ALU.subtract))
                V.tensor_scalar(rope[:, 0], nt[:, 3], PI, -PI, ALU.min, ALU.max).then_inc(rope1_ang, 1)
                la = COL["lam"]
                link(V.tensor_scalar(misc[:, 40:48], pv[:, la:la + 8], -1.0, None, ALU.mult))
                V.tensor_tensor(misc[:, 16:24], pv[:, la:la + 8], misc[:, 40:48], ALU.max).then_inc(lam_sum, 1)
                link(V.tensor_scalar(misc[:, 40:48], misc[:, 40:48], 0.0, None, ALU.max))

            def finish_lambda():
                dve.wait_ge(sp_exp, 1)
                y, z, z2, s = misc[:, 16:24], misc[:, 24:32], misc[:, 32:40], misc[:, 48:56]
                link(V.tensor_scalar(z, y, 2.0, None, ALU.add))
                link(V.reciprocal(z, z))
                link(V.tensor_tensor(z, z, y, ALU.mult))
                link(V.tensor_tensor(z2, z, z, ALU.mult))
                link(V.tensor_scalar(s, z2, 1.0 / 19, None, ALU.mult))
                for n in range(8, 0, -1):
                    link(V.scalar_tensor_tensor(s, s, 1.0 / (2 * n + 1), z2, ALU.add, ALU.mult))
                link(V.scalar_tensor_tensor(s, s, 1.0, z, ALU.add, ALU.mult))
                link(V.scalar_tensor_tensor(s, s, 2.0, misc[:, 40:48], ALU.mult, ALU.add))
                link(V.tensor_scalar(misc[:, 24:32], s, -8.0, None, ALU.mult))
                link(V.tensor_scalar(misc[:, 32:40], s, 8.0, None, ALU.mult))
                dve.wait_ge(lam_exp, 1)
                link(V.tensor_scalar(misc[:, 4:5], misc[:, 3:4], LAMBDA_INIT, None, ALU.subtract))
                link(V.tensor_tensor(misc[:, 4:5], misc[:, 4:5], misc[:, 2:3], ALU.subtract))
                link(V.tensor_scalar(misc[:, 5:6], pv[:, COL["subln"]:COL["subln"] + 1], 1.0 - LAMBDA_INIT, None, ALU.mult))

            dve.wait_ge(cond_done, 2)
            V.tensor_tensor(cond_split[:, :, 1], cond[:], cond_split[:, :, 0], ALU.subtract).then_inc(cond_done, 1)
            q = 0
            for b, (matrix, col, n) in enumerate(MOD_FIRST):
                if b:
                    dve.wait_ge(mod_sum, b)
                for r in MOD_VECTOR[b]:
                    mod_multiply(matrix, r, q, 16 * (1 + sum(k > r for _, _, k in MOD_FIRST[:b])))
                    mod_reduce(r, q)
                    q += 1
                mod_bias(matrix, n, b, col)
                if b == 0:
                    prepare()
            dve.wait_ge(mod_out, len(MOD_FIRST))

            NG = COL["norm_g"]
            modulated("ffn1", x, 8, NG)
            units("ffn1", after_first=finish_lambda)
            dve.wait_ge(mod_out, MB0["ffn2"])
            end_norm("ffn1_end", 0, 16, NG + 8, 0.5)
            dve.wait_ge(x_done, XDONE["mix"])

            V.memset(misc[:, 58:59], 0.0).then_inc(arena_free, 1)
            link(V.memset(xr1[:, :, 0:2], 0.0))
            V.memset(xr1[:, :, 2 + S:XRW], 0.0).then_inc(m1_pad, 1)
            modulated("mix", x, 24 + 8, NG + 16)
            dve.wait_ge(m1_pad, 1)

            def convolve(c):
                cw, cb = COL["conv_w"] + c, COL["conv_b"] + c
                e0 = xc1[c % 2]
                dve.wait_ge(act_z, c + 1)
                link(V.tensor_scalar(e0, xr1[:, c, 0:S], pv[:, cw:cw + 1], pv[:, cb:cb + 1], ALU.mult, ALU.add))
                for tap in range(1, 4):
                    ins = V.scalar_tensor_tensor(e0, xr1[:, c, tap:tap + S], pv[:, cw + 4 * tap:cw + 4 * tap + 1], e0,
                                                 ALU.mult, ALU.add)
                    if tap < 3:
                        link(ins)
                ins.then_inc(m1_xc, 1)
                dve.wait_ge(m1_xc, c + 1)
            convolve(0)
            for c in range(4):
                e0 = xc1[c % 2]
                for d in range(2):
                    a = (root, rinv)[d]
                    dve.wait_ge(m1_at, 4 * c + 2 * d + 2)
                    link(V.tensor_tensor(e1, a[:], a[:], ALU.mult))
                    link(V.scalar_tensor_tensor(nt[:, d], e1, 1.0, nt[:, d], ALU.add, ALU.mult))
                    V.tensor_scalar(nt[:, d], nt[:, d], 1e-30, None, ALU.max).then_inc(m1_m, 1)
                if c < 3:
                    convolve(c + 1)
                for d in range(2):
                    a = (root, rinv)[d]
                    link(V.tensor_tensor(nt[:, 2 + d], nt[:, 2 + d], e0, ALU.mult))
                    dve.wait_ge(m1_sqrt, 2 * c + d + 1)
                    link(V.tensor_tensor(nt[:, d], nt[:, d], nt[:, 2 + d], ALU.mult))
                    if d == 0:
                        link(V.tensor_tensor_scan(nt[:, 2], a[:], nt[:, 0], 0.0, ALU.mult, ALU.add))
                    else:
                        link(V.tensor_tensor_scan(nt[:, 3, ::-1], a[:, ::-1], nt[:, 1, ::-1], 0.0, ALU.mult, ALU.add))
                link(V.tensor_tensor(nt[:, 2], nt[:, 2], nt[:, 3], ALU.add))
                dve.wait_ge(act_z, 4 + c + 1)
                V.tensor_tensor(yr1[:, c], nt[:, 2], yr1[:, c], ALU.mult).then_inc(m1_rec, 1)

            def rotate(z, src, tmp, n, ready, value, done, cols=slice(0, S)):
                dve.wait_ge(ready, value)
                link(V.tensor_tensor(tmp, src, rope[:, 1, cols], ALU.mult))
                link(V.tensor_tensor(z, z, rope[:, 0, cols], ALU.mult))
                V.tensor_tensor(z, z, tmp, ALU.add).then_inc(done, 1)
            dve.wait_ge(rope1_tab, 2)
            for idx in range(8):
                if idx >= 4:
                    dve.wait_ge(m1_rope, idx - 3)
                rotate((q1, k1)[idx // 4][:, idx % 4], G[:, idx % 4], nt[:, idx % 4], S, m1_rot, idx + 1, m1_rope)
                if idx % 2:
                    c = idx // 2
                    dve.wait_ge(m1_yhi, c + 1)
                    V.tensor_tensor(a_lo[:, 4 + c], yr1[:, c], a_hi[:, 4 + c], ALU.subtract).then_inc(m1_ylo, 1)
            dve.wait_ge(m1_col, 10)
            for j0, j1 in ((0, 8), (8, 10)):
                c, _, dst = MODCTX[j0]
                n = 2 * (j1 - j0)
                link(V.tensor_reduce(mods[:, dst:dst + n], Dn[:, 1, 4 * j0:4 * j1].rearrange("p (c n) -> p c n", n=2),
                                     AX.X, ALU.add))
                mb = COL["mod_b"] + 2 * c
                link(V.tensor_tensor(mods[:, dst:dst + n], mods[:, dst:dst + n], pv[:, mb:mb + n], ALU.add))

            def maxima(n):
                dve.wait_ge(m1_qk, 2 * n + 2)
                b = 2 * (n % 2)
                V.tensor_reduce(stat[:, 1, 2 * n:2 * n + 2], G[:, b:b + 2], AX.X, ALU.max,
                                negate=True).then_inc(m1_nm, 1)

            def mix_weights(n):
                dve.wait_ge(m1_exp, 2 * n + 2)
                c, b = 2 * n, 2 * (n % 3)
                link(V.reciprocal(stat[:, 3, c:c + 2], stat[:, 2, c:c + 2]))
                link(V.tensor_tensor(stat[:, 4, c:c + 1], stat[:, 3, c + 1:c + 2], misc[:, 4:5], ALU.mult))
                if n >= 2:
                    dve.wait_ge(m1_tr, n - 1)
                w = wsm1[:, n % 2]
                link(V.tensor_scalar(w, pexp1[:, b], stat[:, 3, c:c + 1], None, ALU.mult))
                V.scalar_tensor_tensor(w, pexp1[:, b + 1], stat[:, 4, c:c + 1], w, ALU.mult, ALU.add).then_inc(m1_w, 1)
            for n in range(17):
                if n < 16:
                    maxima(n)
                if n:
                    mix_weights(n - 1)
            dve.wait_ge(m1_srt, 1)
            V.reciprocal(stat[:, 1, 0:16], stat[:, 0, 0:16]).then_inc(m1_inv, 1)

            def sub_low(h):
                dve.wait_ge(m1_shi, h + 1)
                V.tensor_tensor(a_lo[:, h], q1[:, h], a_hi[:, h], ALU.subtract).then_inc(m1_slo, 1)
            for h in range(4):
                dve.wait_ge(m1_bc, h + 1)
                V.scalar_tensor_tensor(q1[:, h], q1[:, h], misc[:, 5:6], Dn[:, h], ALU.mult, ALU.mult).then_inc(m1_sub, 1)
                if h:
                    sub_low(h - 1)
            sub_low(3)
            end_norm("mix_end", 1, 24 + 16, NG + 24, 1.0)
            dve.wait_ge(x_done, XDONE["ffn2"])

            V.memset(misc[:, 58:59], 0.0).then_inc(arena_back, 1)
            modulated("ffn2", x, 48 + 8, NG + 32)
            units("ffn2")
            dve.wait_ge(mod_out, MB0["moe0"])
            N1 = COL["norm1"]
            modulated("ctx", ctxx, MOD_OUT["ctx"] + 8, N1, CTX)
            end_norm("ffn2_end", 2, 48 + 16, NG + 40, 0.5)
            dve.wait_ge(x_done, XDONE["even"])

            V.memset(misc[:, 58:59], 0.0).then_inc(arena_free, 1)
            link(V.memset(p2[:, :, 0:8], 0.0))
            V.memset(p2[:, :, 8 + S:PW], 0.0).then_inc(m2_pad, 1)
            dve.wait_ge(group_done, GROUPS_BEFORE[T0["evenin"]] + 2)
            modulated("even", x, MOD_OUT["mod0"] + 8, N1)
            link(V.memset(vz[:, :, 0:64], 0.0))
            link(V.memset(vz[:, :, 128:192], 0.0))
            dve.wait_ge(ld_rope2, 16)

            link(V.tensor_scalar(misc[:, 6:7], pv[:, COL["q_gain"]:COL["q_gain"] + 1], 0.125, None, ALU.mult))
            kg = COL["k_gain"]

            def head_norm(idx):
                z = (kall[:, 0:CTX], kall[:, CTX:SK])[idx] if idx < 2 else q2[:, idx - 2]
                n = CTX if idx == 0 else S
                gain = pv[:, kg:kg + 1] if idx < 2 else misc[:, 6:7]
                dve.wait_ge(m2_srt, idx + 1)
                link(V.reciprocal(rinv[:, 0:n], m2_roots[idx % 2][:, 0:n]))
                V.scalar_tensor_tensor(z, z, gain, rinv[:, 0:n], ALU.mult, ALU.mult).then_inc(m2_kn, 1)
                dve.wait_ge(m2_kn, idx + 1)

            def turn_half(idx):
                z = kall[:, CTX:SK] if idx == 1 else q2[:, idx - 2]
                rotate(z, Dn[:, 1 + idx % 2], nt[:, 2], S, m2_rot, idx, m2_rope)
                dve.wait_ge(m2_rope, idx)

            head_norm(0)
            head_norm(1)
            head_norm(2)
            turn_half(1)
            link(V.tensor_copy(kswap[0:64], kall[64:128]))
            V.tensor_copy(kswap[64:128], kall[0:64]).then_inc(m2_swap, 1)
            head_norm(3)
            head_norm(4)
            turn_half(2)
            head_norm(5)
            turn_half(3)
            turn_half(4)
            turn_half(5)

            def pool_low(n):
                g = POOL_ORDER[n]
                dve.wait_ge(m2_phi, n + 1)
                V.tensor_tensor(a_lo[:, 4 + g], ic[:, g], a_hi[:, 4 + g], ALU.subtract).then_inc(m2_pool, 1)

            def maxima2(n):
                dve.wait_ge(m2_qk, n + 1)
                b = 2 * (n % 2)
                V.tensor_reduce(stat[:, 1, n:n + 1], G[:, b:b + 2].rearrange("p a b -> p (a b)")[:, 0:SK], AX.X,
                                ALU.max, negate=True).then_inc(m2_nm, 1)

            def scale2(n):
                dve.wait_ge(m2_exp, n + 1)
                link(V.reciprocal(stat[:, 3, n:n + 1], stat[:, 2, n:n + 1]))
                V.tensor_scalar(pexp2[:, 2 - n % 3], pexp2[:, 2 - n % 3], stat[:, 3, n:n + 1], None, ALU.mult).then_inc(m2_w, 1)

            def heads_low(c):
                dve.wait_ge(m2_ohi, c + 1)
                V.tensor_tensor(a_lo[:, c], Dn[:, 2 + c % 2], a_hi[:, c], ALU.subtract).then_inc(m2_olo, 1)
            for n in range(38):
                if n < 32:
                    maxima2(n)
                if 1 <= n < 33:
                    scale2(n - 1)
                if n - 2 in POOL_STEPS:
                    pool_low(POOL_STEPS.index(n - 2))
                if n >= 13 and n % 8 == 5:
                    heads_low(n // 8 - 1)

            def project_residual(stage, gate_col):
                for k in range(KC):
                    dve.wait_ge(group_done, GROUPS_BEFORE[T0[stage]] + k + 1)
                    V.scalar_tensor_tensor(x[:, k], G[:, k % 4], mods[:, gate_col + k:gate_col + k + 1], x[:, k],
                                           ALU.mult, ALU.add).then_inc(x_done, 1)
            project_residual("evenout", MOD_OUT["mod0"] + 16)

            def first_of(oh, eq, tmp):
                link(V.tensor_tensor(oh, eq, rank.to_broadcast([P, TT, 4]), ALU.mult))
                link(V.tensor_reduce(tmp, oh, AX.X, ALU.max))
                link(V.tensor_tensor(oh, oh, tmp.to_broadcast([P, TT, 4]), ALU.is_equal))

            def router(l):
                def r3(at, n):
                    return rt[:, at:at + 4 * n].rearrange("p (t n) -> p t n", n=n)
                logit, gsh, gm = r3(0, 20), r3(96, 4), r3(112, 1)
                e2, gp, tmp = r3(116, 1), r3(120, 1), r3(124, 1)
                eq, gh, oh1, oh2, esel, m1, m2, msk = (r3(128, 4), r3(144, 4), r3(160, 4), r3(176, 4), r3(192, 4),
                                                       r3(208, 1), r3(212, 1), r3(216, 4))
                wide = rt[:, 232:296].rearrange("p (t g j) -> p t g j", g=4, j=4)

                def b(v, n=4):
                    return v.to_broadcast([P, TT, n])
                link(V.memset(comb_pad, 0.0))
                dve.wait_ge(rt_rows, l + 1)
                V.tensor_copy(hid[0:20, 0], Dn[0:20, 2]).then_inc(rt_copy, 1)
                dve.wait_ge(rt_logit, l + 1)
                link(V.tensor_tensor(logit, Dn[:, 2, 0:80].rearrange("p (t n) -> p t n", n=20),
                                     rb[:, l].unsqueeze(1).to_broadcast([P, TT, 20]), ALU.add))
                lg = logit[:, :, 0:4]
                link(V.tensor_reduce(gm, lg, AX.X, ALU.max))
                V.tensor_tensor(gsh, lg, b(gm), ALU.subtract).then_inc(rt_d1, 1)
                link(V.tensor_tensor(eq, lg, b(gm), ALU.is_equal))
                first_of(gh, eq, tmp)
                le = logit[:, :, 4:20].rearrange("p t (g j) -> p t g j", j=4)
                link(V.tensor_tensor(wide, le, gh.unsqueeze(3).to_broadcast([P, TT, 4, 4]), ALU.mult))
                link(V.tensor_reduce(esel, wide.rearrange("p t g j -> p t j g"), AX.X, ALU.add))
                link(V.tensor_reduce(m1, esel, AX.X, ALU.max))
                link(V.tensor_tensor(eq, esel, b(m1), ALU.is_equal))
                first_of(oh1, eq, tmp)
                link(V.scalar_tensor_tensor(msk, oh1, -1e30, esel, ALU.mult, ALU.add))
                link(V.tensor_reduce(m2, msk, AX.X, ALU.max))
                link(V.tensor_tensor(eq, msk, b(m2), ALU.is_equal))
                first_of(oh2, eq, tmp)
                V.tensor_tensor(e2, m2, m1, ALU.subtract).then_inc(rt_d2, 1)
                dve.wait_ge(rt_exp1, l + 1)
                link(V.tensor_reduce(gp, gsh, AX.X, ALU.add))
                dve.wait_ge(rt_exp2, l + 1)
                link(V.scalar_tensor_tensor(tmp, e2, 1.0, gp, ALU.add, ALU.mult))
                link(V.reciprocal(tmp, tmp))
                link(V.tensor_tensor(oh1, oh1, b(tmp), ALU.mult))
                link(V.tensor_tensor(tmp, tmp, e2, ALU.mult))
                link(V.tensor_tensor(oh2, oh2, b(tmp), ALU.mult))
                link(V.tensor_tensor(oh1, oh1, oh2, ALU.add))
                link(V.tensor_tensor(comb_pad[:, :, 0:16].rearrange("p t (g j) -> p t g j", j=4),
                                     gh.unsqueeze(3).to_broadcast([P, TT, 4, 4]),
                                     oh1.unsqueeze(2).to_broadcast([P, TT, 4, 4]), ALU.mult))
                V.transpose(comb_t.rearrange("p t j -> p (t j)"), comb_pad.rearrange("p t j -> p (t j)")).then_inc(rt_comb, 1)
                dve.wait_ge(rt_comb, l + 1)

            N2 = COL["norm2"]
            for l in range(2):
                stage = f"moe{l}"
                dve.wait_ge(x_done, XDONE[stage])
                if l == 0:
                    V.memset(misc[:, 58:59], 0.0).then_inc(arena_back, 1)
                dve.wait_ge(rt_w, 2 * l + 1)
                V.tensor_tensor(rw_lo[:], rw[:], rw_hi[:], ALU.subtract).then_inc(rt_w, 1)
                modulated(stage, x, MOD_OUT[f"mod{l}"] + 32, N2 + 8 * l)
                units(stage, lambda: router(l))
                for k in range(KC):
                    g = MOD_OUT[f"mod{l}"] + 40 + k
                    V.scalar_tensor_tensor(x[:, k], yacc[:, k], mods[:, g:g + 1], x[:, k],
                                           ALU.mult, ALU.add).then_inc(x_done, 1)
                if l == 1:
                    break
                dve.wait_ge(x_done, XDONE["odd"])
                dve.wait_ge(mod_out, MB0["moe0"] + UNITS["moe0"])
                V.memset(misc[:, 58:59], 0.0).then_inc(arena_free, 1)
                link(V.memset(z3[:, :, 0:1], 0.0))
                V.memset(z3[:, :, 1 + S:ZW], 0.0).then_inc(m3_pad, 1)
                modulated("odd", x, MOD_OUT["mod1"] + 8, N1 + 8)
                dve.wait_ge(act_z, Z0["oddin"] + 8)
                for t in range(TT):
                    link(V.tensor_tensor(nt[:, t], v3[:, t], v3[:, t], ALU.mult))
                    V.tensor_reduce(stat[:, 0, 4 * t:4 * t + 4], nt[:, t].rearrange("p (g n) -> p g n", n=P), AX.X,
                                    ALU.add).then_inc(m3_ss, 1)
                dve.wait_ge(m3_srt, 1)
                link(V.reciprocal(stat[:, 2, 0:16], stat[:, 1, 0:16]))
                for t in range(TT):
                    vt = v3[:, t].rearrange("p (g n) -> p g n", n=P)
                    V.tensor_tensor(vt, vt, stat[:, 2, 4 * t:4 * t + 4].unsqueeze(2).to_broadcast([P, 4, P]),
                                    ALU.mult).then_inc(m3_vn, 1)
                dve.wait_ge(ld_odd, 32)
                for g in range(4):
                    gain = COL["sg_gain"] + g
                    dve.wait_ge(m3_sg, g + 1)
                    link(V.scalar_tensor_tensor(nt[:, 0].rearrange("p (n c) -> p n c", c=P),
                                                Dn[:, g].rearrange("p (n c) -> p n c", c=P), pv[:, gain:gain + 1],
                                                sgb[:, g].unsqueeze(1).to_broadcast([P, TT, P]), ALU.mult, ALU.add))
                    V.tensor_tensor(u3[:, g], nt[:, 0], u3[:, g], ALU.mult).then_inc(m3_y, 1)
                    dve.wait_ge(m3_y, g + 1)
                for c in range(4):
                    w = COL["conv_w2"] + c
                    dve.wait_ge(act_z, Z0["oddin"] + 12 + c + 1)
                    link(V.tensor_tensor(z3[:, c, 1:1 + S], z3[:, c, 1:1 + S], cg3[:, c], ALU.mult))
                    link(V.tensor_scalar(nt[:, c], z3[:, c, 0:S], pv[:, w:w + 1], None, ALU.mult))
                    for tap in (1, 2):
                        link(V.scalar_tensor_tensor(nt[:, c], z3[:, c, tap:tap + S], pv[:, w + 4 * tap:w + 4 * tap + 1],
                                                    nt[:, c], ALU.mult, ALU.add))
                for c in range(4):
                    dve.wait_ge(act_z, Z0["oddin"] + 16 + c + 1)
                    V.tensor_tensor(bg3[:, c], nt[:, c], bg3[:, c], ALU.mult).then_inc(m3_y, 1)
                for k in range(KC):
                    src = u3[:, k] if k < 4 else bg3[:, k - 4]
                    dve.wait_ge(m3_hi, k + 1)
                    V.tensor_tensor(a_lo[:, k], src, a_hi[:, k], ALU.subtract).then_inc(m3_lo, 1)
                project_residual("oddout", MOD_OUT["mod1"] + 16)

        @block.tensor
        def _(pe):
            mm = nc.tensor.matmul

            def product(out, weights, acts, first=True, last=True):
                (wh, wl), (ah, al) = weights, acts
                mm(out, wh, ah, start=first, stop=False)
                mm(out, wl, ah, start=False, stop=False)
                return mm(out, wh, al, start=False, stop=last)

            def mod_sums(n, batch, q):
                pe.wait_ge(mod_red, q + n)
                if not isinstance(batch, int) or batch:
                    pe.wait_ge(mod_out, batch)
                for r in range(n):
                    ins = mm(Dn[:, M, r:r + 1], red[:, r], ones[:, 0:1], start=True, stop=True)
                ins.then_inc(mod_sum, 1)

            def sum_squares(name, n=S):
                q = NORM[name][0]
                for k in range(KC):
                    pe.wait_ge(act_sq, KC * q + k + 1)
                    mm(sum_bank(name)[:, 0:n], ones[:], nt[:, k % 2, 0:n], start=(k == 0), stop=(k == KC - 1)).then_inc(pe_ss, 1)

            def in_pair(slot, outs, ready, t=None, ks=range(KC), ends=(0, KC - 1)):
                if t is not None:
                    pe.wait_ge(weight_lo, t + 1)
                for k in ks:
                    if ready is not None:
                        pe.wait_ge(*ready(k))
                    for c in range(2):
                        cs = slice(c * P, c * P + P)
                        ins = product(outs[c], (w_in(w_hi, slot)[:, k, cs], w_in(w_lo, slot)[:, k, cs]),
                                      (a_hi[:, k], a_lo[:, k]), k == ends[0], k == ends[1])
                        if k == ends[1]:
                            ins.then_inc(group_done, 1)

            def norm_ready(name):
                return lambda k: (dve_alo, KC * NORM[name][1] + k + 1)

            def in_group(slot, c, out, ready=None, n=S, mid=None, each=None):
                for k in range(KC):
                    if mid and k == 3:
                        mid()
                    if ready is not None:
                        pe.wait_ge(dve_alo, ready + k + 1)
                    cs = slice(c * P, c * P + P)
                    ins = product(out, (w_in(w_hi, slot)[:, k, cs], w_in(w_lo, slot)[:, k, cs]),
                                  (a_hi[:, k, 0:n], a_lo[:, k, 0:n]), k == 0, k == KC - 1)
                    if each:
                        each(k)
                return ins

            def token_group(slot, out, t, cs):
                ts = slice(t * P, t * P + P)
                for k in range(KC):
                    ins = product(out, (a_hi[:, k, ts], a_lo[:, k, ts]),
                                  (w_in(w_hi, slot)[:, k, cs], w_in(w_lo, slot)[:, k, cs]), k == 0, k == KC - 1)
                return ins

            def unit(stage, i, l=None):
                t, u = T0[stage], i + UNIT0[stage]

                def logits(k):
                    ins = product(Dn[0:20, 2], (rw_hi[:, k], rw_lo[:, k]), (a_hi[:, k], a_lo[:, k]), k == 0, k == KC - 1)
                    if k == KC - 1:
                        ins.then_inc(rt_rows, 1)

                def logits_by_token():
                    pe.wait_ge(rt_copy, l + 1)
                    for tt in range(TT):
                        ins = nc.tensor.transpose(Dn[:, 2, 20 * tt:20 * tt + 20], hid[0:20, 0, tt * P:(tt + 1) * P],
                                                  ident[0:20, 0:20])
                    ins.then_inc(rt_logit, 1)
                pe.wait_ge(weight_lo, 3 * i + (t + 1))
                pe.wait_ge(act_silu, 2 * u + 2)
                pe.wait_ge(down_added, 8 * u + (PRIME_ADD - 8 + 5))
                if l is None:
                    in_pair(t % RING, (G[:, 0], G[:, 1]), norm_ready(stage))
                else:
                    in_group(t % RING, 0, G[:, 0], KC * NORM[stage][1], each=logits).then_inc(group_done, 1)
                    in_group(t % RING, 1, G[:, 1], mid=logits_by_token).then_inc(group_done, 1)
                pe.wait_ge(weight_lo, 3 * i + (t + 2))
                for c in range(2):
                    pe.wait_ge(dve_gu, 2 * u + (c + 1))
                    in_group((t + 1) % RING, c, G[:, 2 + c]).then_inc(group_done, 1)
                pe.wait_ge(weight_lo, 3 * i + (t + 3))
                s = (t + 2) % RING
                for ms in (range(5), range(5, KC)):
                    for k in range(2):
                        for m in ms:
                            if k == 0:
                                if m == 2 and l is not None:
                                    pe.wait_ge(comb_full, 16 * EXPERTS * l + 16)
                                if m < 3:
                                    pe.wait_ge(down_added, 8 * u + (PRIME_ADD - 8 + m + 6))
                                elif m < 5:
                                    pe.wait_ge(act_silu, 2 * u + (PRIME_SILU + 2))
                                else:
                                    pe.wait_ge(down_added, 8 * u + (PRIME_ADD + m - 4))
                            ws = slice(m * P, m * P + P)
                            wh, wl = w_down(w_hi, s)[:, k, ws], w_down(w_lo, s)[:, k, ws]
                            if k == 0 or ms[0]:
                                if k == 0 and m == 0:
                                    pe.wait_ge(dve_hlo, 2 * u + 2)
                                ins = product(down_bank(m), (wh, wl), (h_hi[:, k], h_lo[:, k]), k == 0, k == 1)
                                if k == 1:
                                    ins.then_inc(group_done, 1)
                            else:
                                if m == 0:
                                    pe.wait_ge(act_hhi, 2 * u + 2)
                                mm(down_bank(m), wh, h_hi[:, 1], start=False, stop=False)
                                mm(down_bank(m), wl, h_hi[:, 1], start=False, stop=False)
                        if k == 1 and not ms[0]:
                            pe.wait_ge(dve_hlo, 2 * u + 3)
                            for m in ms:
                                mm(down_bank(m), w_down(w_hi, s)[:, 1, m * P:m * P + P], h_lo[:, 1], start=False,
                                   stop=True).then_inc(group_done, 1)
                n = MOD_PER_UNIT[stage]
                if n:
                    mod_sums(n, i + MB0[stage], i * n + MQ0[stage])

            def units(stage, l=None):
                if l is not None:
                    unit(stage, 0, l)
                with pe.Fori(int(l is not None), UNITS[stage]) as i:
                    unit(stage, i)

            def projection(stage, g0, z, j, groups=None, ready=None, between=None):
                t = T0[stage] + j
                pe.wait_ge(weight_lo, t + 1)
                if ready is not None:
                    in_pair(t % RING, (G[:, 0], G[:, 1]), ready)
                    return
                for c in range(2):
                    g = g0 + c
                    if g >= 4:
                        pe.wait_ge(*z(g - 3))
                    if groups:
                        groups(t % RING, c, G[:, g % 4]).then_inc(group_done, 1)
                    else:
                        in_group(t % RING, c, G[:, g % 4]).then_inc(group_done, 1)
                    if between and c == 0:
                        between()

            pe.wait_ge(ld_const, 80)
            q = 0
            for b, (_, _, n) in enumerate(MOD_FIRST):
                if b:
                    pe.wait_ge(mod_out, b)
                else:
                    pe.wait_ge(cond_done, 1)
                for r in range(n):
                    if r in MOD_VECTOR[b]:
                        continue
                    pe.wait_ge(mod_full[r], 16 * (1 + sum(k > r for _, _, k in MOD_FIRST[:b])))
                    for k in range(KC):
                        ins = mm(Dn[:, M, r:r + 1], mod_raw[:, r, k], cond[:, k:k + 1], start=(k == 0), stop=(k == KC - 1))
                    ins.then_inc(mod_direct, 1)
                for r in MOD_VECTOR[b]:
                    q += 1
                    pe.wait_ge(mod_red, q)
                    ins = mm(Dn[:, M, r:r + 1], red[:, r], ones[:, 0:1], start=True, stop=True)
                ins.then_inc(mod_sum, 1)
                if b == 1:
                    sum_squares("ffn1")
            units("ffn1")
            sum_squares("ffn1_end")

            sum_squares("mix")

            def values1(slot, c, out):
                for t in (2 * c, 2 * c + 1):
                    ins = token_group(slot, out[:, 256 * (t % 2):256 * (t % 2) + 256], t, slice(0, 256))
                return ins

            def rg_gates(c):
                pe.wait_ge(m1_xc, c + 1)
                if c == 0:
                    pe.wait_ge(ld_mix, 16)
                for dg in range(4):
                    if c:
                        pe.wait_ge(m1_sig, 4 * (c - 1) + dg + 1)
                    mm(Dn[:, dg], bd[:, dg, c * P:c * P + P], xc1[c % 2], start=True, stop=True).then_inc(m1_gate, 1)
            for j in range(10):
                projection("mixin", 2 * j, lambda n: (act_z, Z0["mixin"] + n), j,
                           values1 if j >= 8 else None, norm_ready("mix") if j == 0 else None)
                if j % 2 and j < 9:
                    rg_gates(j // 2)
            pe.wait_ge(m1_sig, 16)

            def modctx(j):
                _, cc, _ = MODCTX[j]
                t = T0["modctx"] + j
                pe.wait_ge(weight_lo, t + 1)
                if j >= 2:
                    pe.wait_ge(m1_row, j - 1)
                for k in range(KC):
                    for n, w in enumerate((w_hi, w_lo)):
                        ins = mm(Dn[0:2, 2 + j % 2, 0:256], cond_split[:, cc + k], w_in(w, t % RING)[:, k],
                                 start=(k == 0 and n == 0), stop=(k == KC - 1 and n == 1))
                ins.then_inc(group_done, 2)

            def modctx_columns(j):
                pe.wait_ge(m1_row, j + 1)
                for c in range(2):
                    ins = nc.tensor.transpose(Dn[:, 1, 4 * j + 2 * c:4 * j + 2 * c + 2],
                                              mod_rows[0:2, 2 * j + c], ident[0:2, 0:2])
                ins.then_inc(m1_col, 1)
            for idx in range(10):
                if idx < 8:
                    if idx < 4:
                        pe.wait_ge(act_z, 16 + idx + 1)
                    else:
                        pe.wait_ge(m1_rope, idx - 3)
                    mm(G[:, idx % 4], rot1[:], (q1, k1)[idx // 4][:, idx % 4], start=True, stop=True).then_inc(m1_rot, 1)
                modctx(idx)
                if idx >= 2:
                    modctx_columns(idx - 2)
            modctx_columns(8)
            modctx_columns(9)
            pe.wait_ge(m1_rope, 8)
            pe.wait_ge(m1_ylo, 4)

            def scores(n):
                h, i = n // 4, n % 4
                if n >= 2:
                    pe.wait_ge(m1_exp, 2 * n - 2)
                for m in range(2):
                    ps = slice(64 * m, 64 * m + 64)
                    mm(G[:, 2 * (n % 2) + m], q1[ps, h, i * P:(i + 1) * P], k1[ps, h], start=True,
                       stop=True).then_inc(m1_qk, 1)

            def turn(n):
                pe.wait_ge(m1_w, n + 1)
                if n >= 2:
                    pe.wait_ge(m1_wt, n - 1)
                for k in range(4):
                    ins = nc.tensor.transpose(Dn[:, n % 2, k * P:(k + 1) * P], wsm1[:, n % 2, k * P:(k + 1) * P], ident[:])
                ins.then_inc(m1_tr, 1)

            def values_sum(n):
                h, i = n // 4, n % 4
                pe.wait_ge(m1_wt, n + 1)
                if i == 0 and h >= 2:
                    pe.wait_ge(m1_o, h - 1)
                for k in range(4):
                    ins = mm(Dn[:, 2 + h % 2, i * P:(i + 1) * P], v1[:, k, h * P:(h + 1) * P], wt1[:, n % 2, k],
                             start=(k == 0), stop=(k == 3))
                ins.then_inc(m1_pv, 1)
            for n in range(19):
                if n < 16:
                    scores(n)
                if 2 <= n < 18:
                    turn(n - 2)
                if n >= 3:
                    values_sum(n - 3)
            pe.wait_ge(m1_wt, 16)
            for h in range(4):
                pe.wait_ge(m1_ssq, h + 1)
                for i in range(TT):
                    ins = mm(Dn[:, 0, 4 * h + i:4 * h + i + 1], nt[:, h, i * P:(i + 1) * P], ones[:, 0:1], start=True, stop=True)
            ins.then_inc(m1_ssp, 1)
            in_pair(T0["mixout"] % RING, (G[:, 0], G[:, 1]), None, T0["mixout"], range(4, KC), (4, 3))
            pe.wait_ge(m1_inv, 1)
            for h in range(4):
                for i in range(TT):
                    ins = mm(Dn[:, h, i * P:(i + 1) * P], stat[:, 1, 4 * h + i:4 * h + i + 1].to_broadcast([P, P]), ident[:],
                             start=True, stop=True)
                ins.then_inc(m1_bc, 1)
            in_pair(T0["mixout"] % RING, (G[:, 0], G[:, 1]), lambda k: (m1_slo, k + 1), None, range(4), (4, 3))
            for j in range(1, 4):
                projection("mixout", 2 * j, lambda n: (act_z, Z0["mixout"] + n), j)
            sum_squares("mix_end")

            sum_squares("ffn2")
            units("ffn2")
            sum_squares("ctx", CTX)
            sum_squares("ffn2_end")

            t = T0["evenin"]
            pe.wait_ge(weight_lo, t + 1)
            s = t % RING
            r = KC * NORM["ctx"][1]
            in_group(s, 1, G[:, 1, 0:CTX], r, CTX).then_inc(group_done, 1)
            in_group(s, 0, G[:, 0, 0:CTX], None, CTX).then_inc(group_done, 1)

            def values_by_token(n, bank, tiles):
                pe.wait_ge(m2_vf, n + 1)
                for tt in range(tiles):
                    ins = nc.tensor.transpose(G[:, bank, tt * P:(tt + 1) * P], v2f[n][:, tt * P:(tt + 1) * P], ident[:])
                ins.then_inc(m2_vtr, 1)
            sum_squares("even")
            values_by_token(0, 1, CT)

            def norm_sums(idx):
                n = CTX if idx == 0 else S
                pe.wait_ge(m2_ssq, idx + 1)
                if idx >= 2:
                    pe.wait_ge(m2_srt, idx - 1)
                mm(Dn[:, 3 * (idx % 2), 0:n], ones64[:], nt[:, idx % 2, 0:n], start=True, stop=True).then_inc(m2_ssp, 1)

            def turned(idx):
                z = kall[:, CTX:SK] if idx == 1 else q2[:, idx - 2]
                pe.wait_ge(m2_kn, idx + 1)
                if idx > 2:
                    pe.wait_ge(m2_rope, idx - 2)
                mm(Dn[:, 1 + idx % 2], rot2[:], z, start=True, stop=True).then_inc(m2_rot, 1)

            norm_sums(0)
            in_group(s, 1, G[:, 3], KC * NORM["even"][1]).then_inc(group_done, 1)
            in_group(s, 0, G[:, 2]).then_inc(group_done, 1)
            values_by_token(1, 3, TT)
            z = lambda n: (act_z, Z0["evenin"] + n)

            def sums_and_turn(idx):
                norm_sums(idx)
                turned(idx - 2)
            projection("evenin", 4, z, 1, between=lambda: norm_sums(1))
            projection("evenin", 6, z, 2, between=lambda: norm_sums(2))
            sums_and_turn(3)
            projection("evenin", 8, z, 3, between=lambda: sums_and_turn(4))
            sums_and_turn(5)
            projection("evenin", 10, z, 4, between=lambda: turned(4))
            turned(5)
            pe.wait_ge(ld_even, 32)
            pe.wait_ge(act_z, Z0["evenin"] + 12)
            pe.wait_ge(m2_rope, 5)
            pe.wait_ge(m2_swap, 1)

            def pool_product(n):
                pe.wait_ge(m2_d, n + 1)
                if n:
                    pe.wait_ge(m2_ps, n)
                g = POOL_ORDER[n]
                mm(Dn[:, 3], poolw[:, g], ic[:, g], start=True, stop=True).then_inc(m2_pw, 1)

            def scores2(n):
                c, i, half = n // 8, n // 2 % 4, n % 2
                ps = slice(64 * half, 64 * half + 64)
                keys = kall if c // 2 == half else kswap
                if n >= 2:
                    pe.wait_ge(m2_exp, n - 1)
                b = 2 * (n % 2)
                q = q2[ps, c, i * P:(i + 1) * P]
                mm(G[:, b], q, keys[ps, 0:S], start=True, stop=True)
                mm(G[:, b + 1, 0:CTX], q, keys[ps, S:SK], start=True, stop=True).then_inc(m2_qk, 1)

            def turn2(n):
                pe.wait_ge(m2_w, n + 1)
                if n >= 1:
                    pe.wait_ge(m2_wt, n)
                for k in range(6):
                    ins = nc.tensor.transpose(Dn[:, k // 4, (k % 4) * P:(k % 4 + 1) * P],
                                              pexp2[:, 2 - n % 3, k * P:(k + 1) * P], ident[:])
                ins.then_inc(m2_tr, 1)

            def values_sum2(n):
                c, i, half = n // 8, n // 2 % 4, n % 2
                pe.wait_ge(m2_wt, n + 1)
                if n == 8:
                    pe.wait_ge(m2_ps, 4)
                if c >= 2 and n % 8 == 0:
                    pe.wait_ge(m2_olo, c - 1)
                for k in range(6):
                    v = vz[:, 2 * k + c // 2, 64 * (1 - half):64 * (1 - half) + P]
                    ins = mm(Dn[:, 2 + c % 2, i * P:(i + 1) * P], v, wt2[:, n % 2, k], start=(half == 0 and k == 0),
                             stop=(half == 1 and k == 5))
                ins.then_inc(m2_pv, 1)
            for n in range(35):
                if n < 32:
                    scores2(n)
                if 2 <= n < 34:
                    turn2(n - 2)
                if n >= 3:
                    values_sum2(n - 3)
                if n in POOL_STEPS:
                    pool_product(POOL_STEPS.index(n))
            in_pair(T0["evenout"] % RING, (G[:, 0], G[:, 1]), lambda k: (m2_pool, 4) if k >= 4 else (m2_olo, k + 1),
                    T0["evenout"], (4, 5, 6, 7, 0, 1, 2, 3), (4, 3))
            for j in range(1, 4):
                projection("evenout", 2 * j, lambda n: (x_done, XDONE["even"] + n), j)

            for l in range(2):
                stage = f"moe{l}"
                sum_squares(stage)
                pe.wait_ge(rt_w, 2 * l + 2)
                units(stage, l)
                if l == 1:
                    break
                sum_squares("odd")

                def values3(slot, c, out):
                    for t in (2 * c, 2 * c + 1):
                        ins = token_group(slot, out[:, 256 * (t % 2):256 * (t % 2) + 256], t, slice(0, 256))
                    return ins
                for j in range(10):
                    projection("oddin", 2 * j, lambda n: (act_z, Z0["oddin"] + n), j,
                               values3 if j in (2, 3) else None, norm_ready("odd") if j == 0 else None)
                    if j == 5:
                        pe.wait_ge(ld_odd, 32)
                        pe.wait_ge(m3_vn, 4)
                        for g in range(4):
                            for n in range(TT):
                                ins = mm(Dn[:, g, n * P:(n + 1) * P], v3[:, n, g * P:(g + 1) * P], sgw[:, g],
                                         start=True, stop=True)
                            ins.then_inc(m3_sg, 1)
                pe.wait_ge(act_z, Z0["oddin"] + 20)
                in_pair(T0["oddout"] % RING, (G[:, 0], G[:, 1]), lambda k: (m3_lo, k + 1), T0["oddout"])
                for j in range(1, 4):
                    projection("oddout", 2 * j, lambda n: (x_done, XDONE["odd"] + n), j)


def kernel(x, c, positions, w_ada, b_ada, norm_g, ffn1_w_in, ffn1_w_out, ffn2_w_in, ffn2_w_out,
           w_mix_in, w_mix_out, lambda_q, lambda_k, subln_g, conv_w, conv_b, lru_w_gate, lru_b_gate,
           lru_lambda, c_2, ctx_2, c_ctx_2, mod_w_2, mod_b_2, norm1_g_2, norm2_g_2, even_w_in_2,
           q_gain_2, k_gain_2, pool_w_2, pool_scale_2, even_w_out_2, odd_w_in_2, sg_gain_2, sg_w_2,
           sg_b_2, conv_w_2, odd_w_out_2, router_g_w_2, router_g_b_2, router_e_w_2, router_e_b_2,
           w_gate_2, w_up_2, w_down_2):
    import numpy as np
    import concourse.bacc as bacc
    from concourse.bass_utils import run_bass_kernel_spmd as run

    f = np.float32

    def cols(v):
        return np.asarray(v).reshape(-1, P).T

    def twice(v):
        return np.concatenate([np.asarray(v).reshape(1, 64)] * 2, axis=1)

    idx = np.arange(P)
    inv = (f(10000.0) ** (-np.arange(0, 64, 2, dtype=f) / f(64))).astype(f)
    inv_col = inv[idx % 32].reshape(1, P)
    rot1 = np.zeros((P, P), f)
    rot2 = np.zeros((P, P), f)
    for o in range(P):
        rot1[o + 32 if o % 64 < 32 else o - 32, o] = -1.0 if o % 64 < 32 else 1.0
        rot2[o + 16 if o % 32 < 16 else o - 16, o] = -1.0 if o % 32 < 16 else 1.0
    inv2 = (f(10000.0) ** (-np.arange(0, 32, 2, dtype=f) / f(32))).astype(f)
    tok = np.arange(S)
    row, col = (tok // 64).astype(f), (tok % 64).astype(f)
    ang = np.where((idx % 64 < 32)[:, None], row[None, :], col[None, :]).astype(f) * inv2[idx % 16][:, None]
    rope2 = np.stack([np.cos(ang), np.sin(ang)], axis=1).astype(f)
    inv_count = np.stack([1.0 / (np.clip(tok + w - w // 2, 0, S) - np.clip(tok - w // 2, 0, S)).astype(f)
                          for w in (2, 4, 8, 16)]).astype(f)
    block64 = np.kron(np.eye(2, dtype=f), np.ones((64, 64), f))

    params = np.concatenate([cols(v) for v in (
        c, c_2, c_ctx_2, b_ada, mod_b_2, norm_g, norm1_g_2, norm2_g_2, subln_g, conv_w, conv_b, lru_b_gate,
        lru_lambda, twice(q_gain_2), twice(k_gain_2), pool_scale_2, sg_gain_2, conv_w_2, inv_col)], axis=1)
    assert params.shape == (P, NCOL), params.shape
    wg = np.asarray(lru_w_gate)[0]
    bd = np.zeros((P, 4, 4, P), wg.dtype)
    for d in range(2):
        for g in range(2):
            for n in range(8):
                h = 64 * (n % 2)
                bd[h:h + 64, 2 * d + g, n // 2, h:h + 64] = wg[d, g, n]
    arrays = {
        "x_t": np.asarray(x)[0].T, "ctx_t": np.asarray(ctx_2)[0].T, "params": params,
        "positions": np.asarray(positions),
        "lambda_qk": np.concatenate([np.asarray(lambda_q).reshape(-1), np.asarray(lambda_k).reshape(-1)]),
        "router_b": np.concatenate([np.asarray(router_g_b_2), np.asarray(router_e_b_2)], axis=1).reshape(-1),
        "router_w": np.concatenate([np.asarray(router_g_w_2), np.asarray(router_e_w_2)], axis=2),
        "lru_bd": bd.reshape(P, 4, 4 * P), "pool_w": np.asarray(pool_w_2)[0],
        "sg_w_t": np.asarray(sg_w_2)[0].transpose(2, 0, 1), "sg_b": np.asarray(sg_b_2)[0],
        "w_ada": np.asarray(w_ada)[0], "mod_w": np.asarray(mod_w_2),
        "ffn1_w_in": np.asarray(ffn1_w_in)[0], "ffn1_w_out": np.asarray(ffn1_w_out)[0],
        "ffn2_w_in": np.asarray(ffn2_w_in)[0], "ffn2_w_out": np.asarray(ffn2_w_out)[0],
        "w_mix_in": np.asarray(w_mix_in)[0], "w_mix_out": np.asarray(w_mix_out)[0],
        "even_w_in": np.asarray(even_w_in_2)[0], "even_w_out": np.asarray(even_w_out_2)[0],
        "odd_w_in": np.asarray(odd_w_in_2)[0], "odd_w_out": np.asarray(odd_w_out_2)[0],
        "w_gate": np.asarray(w_gate_2), "w_up": np.asarray(w_up_2), "w_down": np.asarray(w_down_2),
        "ident": np.eye(P, dtype=f), "ones": np.ones((P, P), f), "ones64": block64, "rot1": rot1, "rot2": rot2,
        "rope2": rope2, "inv_count": inv_count,
    }
    arrays = {n: np.ascontiguousarray(a) for n, a in arrays.items()}
    nc = bacc.Bacc("TRN2", target_bir_lowering=False, num_devices=1)
    io = {n: nc.dram_tensor(f"in_{n}", a.shape, mybir.dt.from_np(a.dtype), kind="ExternalInput").ap()
          for n, a in arrays.items()}
    io["comb_dram"] = nc.dram_tensor("comb_dram", (2 * EXPERTS, S), F32, kind="Internal").ap()
    io["out"] = nc.dram_tensor("out", (D, S), F32, kind="ExternalOutput").ap()
    build(nc, io)
    r = run(nc, [{f"in_{n}": a for n, a in arrays.items()}], core_ids=[0])
    return np.ascontiguousarray(r.results[0]["out"].T).reshape(1, S, D)
```
